# Optimizing a Trainium2 kernel written in Bass

```python
import jax, jax.numpy as jnp
from jax import lax
import numpy as np

D_MODEL = 1024
BATCH = 1
SEQ = 1024
DEPTH = 1
DEC_BATCH = 8
DEC_SEQ = 1
PAST_LEN = 2048
PAGE_SIZE = 128

H_A = 8
HD_A = 64
D_A = H_A * HD_A
D_LORA_W = 64
D_LORA_A = 64
D_LORA_G = 128
GN_EPS = 64e-5
H_Q = 8
H_KV = 2
G_Q = H_Q // H_KV
HD_B = 64
D_B = H_Q * HD_B
WINDOW = 128
ATTN_BLOCK = 128
N_KEYS = 128
N_EXPERTS = N_KEYS * N_KEYS
PEER_HEADS = 8
PEER_DKEY = 256
PEER_HALF = PEER_DKEY // 2
PEER_TOPK = 16
PEER_BLOCK = 128
OFF_R = 0
OFF_K = OFF_R + D_A
OFF_V = OFF_K + D_A
OFF_WD = OFF_V + D_A
OFF_AD = OFF_WD + D_LORA_W
OFF_GD = OFF_AD + D_LORA_A
SHIFT_W = OFF_GD + D_LORA_G
OFF_Q = SHIFT_W
OFF_KB = OFF_Q + D_B
OFF_VB = OFF_KB + H_KV * HD_B
OFF_GA = OFF_VB + H_KV * HD_B
OFF_GB = OFF_GA + D_MODEL
D_IN = OFF_GB + D_MODEL
N_MOD = 6
LN_EPS = 1e-5
DEEPNORM_ALPHA = (2.0 * DEPTH) ** 0.25
DEEPNORM_BETA = (8.0 * DEPTH) ** -0.25
NEG_INF = -1e30

kernel_name = 'rwkv7_swa_sink_peer_deepnorm_step'

def _layernorm(x, g, b, eps=LN_EPS):
    xf = x.astype(jnp.float32)
    mu = jnp.mean(xf, -1, keepdims=True)
    var = jnp.mean(jnp.square(xf - mu), -1, keepdims=True)
    return ((xf - mu) * lax.rsqrt(var + eps) * g + b).astype(x.dtype)

def _alibi_slopes():
    return jnp.asarray(2.0 ** (-8.0 * np.arange(1, H_Q + 1) / H_Q), jnp.float32)

def _sink_attention(q, k, v, rel, valid, sinks):
    s = jnp.einsum('...qkgd,...skd->...kgqs', q, k).astype(jnp.float32) * (HD_B ** -0.5)
    slopes = _alibi_slopes().reshape(H_KV, G_Q, 1, 1)
    s = s - slopes * rel[..., None, None, :, :].astype(jnp.float32)
    s = jnp.where(valid[..., None, None, :, :], s, NEG_INF)
    sink = jnp.broadcast_to(sinks.astype(jnp.float32).reshape(H_KV, G_Q, 1, 1), s.shape[:-1] + (1,))
    p = jax.nn.softmax(jnp.concatenate([s, sink], axis=-1), axis=-1)[..., :-1]
    return jnp.einsum('...kgqs,...skd->...qkgd', p.astype(v.dtype), v)

def _banded_window_attention(q, k, v, sinks):
    n, t = q.shape[:2]
    nb = t // ATTN_BLOCK
    qb = q.reshape(n, nb, ATTN_BLOCK, H_KV, G_Q, HD_B)

    def band(z):
        zp = jnp.concatenate([jnp.zeros_like(z[:, :ATTN_BLOCK]), z], axis=1)
        zp = zp.reshape(n, nb + 1, ATTN_BLOCK, H_KV, HD_B)
        return jnp.concatenate([zp[:, :-1], zp[:, 1:]], axis=2)

    blk = jnp.arange(nb)[:, None, None]
    q_pos = blk * ATTN_BLOCK + jnp.arange(ATTN_BLOCK)[None, :, None]
    k_pos = (blk - 1) * ATTN_BLOCK + jnp.arange(2 * ATTN_BLOCK)[None, None, :]
    rel = q_pos - k_pos
    valid = (k_pos >= 0) & (rel >= 0) & (rel <= WINDOW)
    o = _sink_attention(qb, band(k), band(v), rel, valid, sinks)
    return o.reshape(n, t, H_KV, G_Q, HD_B)

def _buffer_window_attention(q, k, v, k_buf, v_buf, sinks):
    t, wb = q.shape[1], k_buf.shape[1]
    k_all = jnp.concatenate([k_buf, k.astype(k_buf.dtype)], axis=1)
    v_all = jnp.concatenate([v_buf, v.astype(v_buf.dtype)], axis=1)
    q_pos = PAST_LEN + jnp.arange(t)
    k_pos = PAST_LEN - wb + jnp.arange(wb + t)
    rel = q_pos[:, None] - k_pos[None, :]
    valid = (rel >= 0) & (rel <= WINDOW)
    o = _sink_attention(q, k_all, v_all, rel, valid, sinks)
    return o, k_all[:, -wb:], v_all[:, -wb:]

def _rwkv7_scan(r, w, k, v, kk, a, s0):
    def step(S, inp):
        r_t, w_t, k_t, v_t, kk_t, a_t = inp
        sa = jnp.einsum('nhij,nhj->nhi', S, -kk_t)
        S = (S * w_t[:, :, None, :] + sa[..., None] * (kk_t * a_t)[:, :, None, :]
             + v_t[..., None] * k_t[:, :, None, :])
        return S, jnp.einsum('nhij,nhj->nhi', S, r_t)

    xs = tuple(jnp.moveaxis(z, 1, 0) for z in (r, w, k, v, kk, a))
    S, ys = lax.scan(step, s0, xs)
    return jnp.moveaxis(ys, 0, 1), S

def _mixer(h, shift_prev, wkv0, k_buf, v_buf, lp):
    n, t, _ = h.shape
    f32 = jnp.float32
    p = h @ lp['w_in']
    ps = p[..., :SHIFT_W]
    prev = jnp.concatenate([shift_prev[:, None].astype(ps.dtype), ps[:, :-1]], axis=1)
    xs = ps + (prev - ps) * lp['mu_shift']
    heads = lambda z: z.reshape(n, t, H_A, HD_A)
    r = xs[..., OFF_R:OFF_K].astype(f32)
    k = xs[..., OFF_K:OFF_V].astype(f32)
    v = xs[..., OFF_V:OFF_WD].astype(f32)
    wd = xs[..., OFF_WD:OFF_AD]
    ad = xs[..., OFF_AD:OFF_GD]
    gd = xs[..., OFF_GD:SHIFT_W]
    w_log = -jax.nn.softplus(-(lp['rwkv_w0'] + jnp.tanh(wd) @ lp['rwkv_w2']).astype(f32)) - 0.5
    decay = jnp.exp(-jnp.exp(w_log))
    a = jax.nn.sigmoid((lp['rwkv_a0'] + ad @ lp['rwkv_a2']).astype(f32))
    g = jax.nn.sigmoid(gd) @ lp['rwkv_g2']
    kk = heads(k * lp['rwkv_k_k'])
    kk = kk / jnp.maximum(jnp.sqrt(jnp.sum(jnp.square(kk), -1, keepdims=True)), 1e-12)
    k = k * (1.0 + (a - 1.0) * lp['rwkv_k_a'])
    r, k, v, a, decay = heads(r), heads(k), heads(v), heads(a), heads(decay)
    y, wkv_new = _rwkv7_scan(r, decay, k, v, kk, a, wkv0.astype(f32))
    mu = jnp.mean(y, -1, keepdims=True)
    var = jnp.mean(jnp.square(y - mu), -1, keepdims=True)
    y = ((y - mu) * lax.rsqrt(var + GN_EPS)).reshape(n, t, D_A) * lp['rwkv_gn_g'] + lp['rwkv_gn_b']
    bonus = jnp.sum(r * k * lp['rwkv_r_k'], -1, keepdims=True) * v
    y_a = ((y + bonus.reshape(n, t, D_A)).astype(h.dtype) * g) @ lp['w_pa']
    q = p[..., OFF_Q:OFF_KB].reshape(n, t, H_KV, G_Q, HD_B)
    kb = p[..., OFF_KB:OFF_VB].reshape(n, t, H_KV, HD_B)
    vb = p[..., OFF_VB:OFF_GA].reshape(n, t, H_KV, HD_B)
    if k_buf is None:
        ob = _banded_window_attention(q, kb, vb, lp['attn_sinks'])
        k_new, v_new = kb[:, -WINDOW:], vb[:, -WINDOW:]
    else:
        ob, k_new, v_new = _buffer_window_attention(q, kb, vb, k_buf, v_buf, lp['attn_sinks'])
    y_b = ob.reshape(n, t, D_B) @ lp['w_pb']
    merged = jax.nn.sigmoid(p[..., OFF_GA:OFF_GB]) * y_a + jax.nn.sigmoid(p[..., OFF_GB:D_IN]) * y_b
    return merged @ lp['w_o'], ps[:, -1], wkv_new, k_new, v_new

def _peer(h, lp):
    n, t, d = h.shape
    xf = h.reshape(n * t, d)
    m = xf.shape[0]
    xp = jnp.pad(xf, ((0, (-m) % PEER_BLOCK), (0, 0)))
    blocks = xp.reshape(-1, PEER_BLOCK, d)

    def one_block(xb):
        q = (xb @ lp['peer_wq']).astype(jnp.float32).reshape(PEER_BLOCK, PEER_HEADS, 2, PEER_HALF)
        s1 = jnp.einsum('bhd,kd->bhk', q[:, :, 0], lp['peer_sub_keys'][0].astype(jnp.float32))
        s2 = jnp.einsum('bhd,kd->bhk', q[:, :, 1], lp['peer_sub_keys'][1].astype(jnp.float32))
        v1, i1 = lax.top_k(s1, PEER_TOPK)
        v2, i2 = lax.top_k(s2, PEER_TOPK)
        cand = (v1[..., :, None] + v2[..., None, :]).reshape(PEER_BLOCK, PEER_HEADS, PEER_TOPK * PEER_TOPK)
        sc, ci = lax.top_k(cand, PEER_TOPK)
        e1 = jnp.take_along_axis(i1, ci // PEER_TOPK, axis=-1)
        e2 = jnp.take_along_axis(i2, ci % PEER_TOPK, axis=-1)
        idx = (e1 * N_KEYS + e2).reshape(PEER_BLOCK, PEER_HEADS * PEER_TOPK)
        gate = jax.nn.softmax(sc, axis=-1).reshape(PEER_BLOCK, PEER_HEADS * PEER_TOPK)
        u = lp['peer_u'][idx]
        act = jax.nn.gelu(jnp.einsum('bkd,bd->bk', u, xb).astype(jnp.float32), approximate=False)
        return jnp.einsum('bk,bkd->bd', (gate * act).astype(xb.dtype), lp['peer_v'][idx])

    out = lax.map(one_block, blocks)
    return out.reshape(-1, d)[:m].reshape(n, t, d)

def _layer(x, c, shift_prev, wkv0, k_buf, v_buf, lp):
    mod = (jax.nn.silu(c) @ lp['w_ada'] + lp['b_ada'])[:, None, :]
    sh_m, sc_m, gt_m, sh_f, sc_f, gt_f = jnp.split(mod, N_MOD, axis=-1)
    mix, shift_new, wkv_new, k_new, v_new = _mixer(x * (1.0 + sc_m) + sh_m, shift_prev, wkv0, k_buf, v_buf, lp)
    x = _layernorm(DEEPNORM_ALPHA * x + gt_m * mix, lp['ln1_g'], lp['ln1_b'])
    ff = _peer(x * (1.0 + sc_f) + sh_f, lp)
    x = _layernorm(DEEPNORM_ALPHA * x + gt_f * ff, lp['ln2_g'], lp['ln2_b'])
    return x, (shift_new, wkv_new, k_new, v_new)

def setup_inputs(seed: int = 0) -> dict:
    key = jax.random.key(seed)
    ks = iter(jax.random.split(key, 40))
    nrm = lambda shape, scale: scale * jax.random.normal(next(ks), shape, jnp.float32)
    L, D = DEPTH, D_MODEL
    wb = min(WINDOW, PAST_LEN)
    return {
        'x_prompt': nrm((BATCH, SEQ, D), 1.0),
        'x_sample': nrm((DEC_BATCH, DEC_SEQ, D), 1.0),
        'state_wkv': nrm((L, DEC_BATCH, H_A, HD_A, HD_A), 0.1),
        'state_shift': nrm((L, DEC_BATCH, SHIFT_W), 1.0),
        'cache_k_win': nrm((L, DEC_BATCH, wb, H_KV, HD_B), 1.0),
        'cache_v_win': nrm((L, DEC_BATCH, wb, H_KV, HD_B), 1.0),
        'c_prompt': nrm((BATCH, D), 1.0),
        'c_sample': nrm((DEC_BATCH, D), 1.0),
        'ln_in_g': 1.0 + nrm((D,), 0.05),
        'ln_in_b': nrm((D,), 0.02),
        'w_ada': nrm((L, D, N_MOD * D), 0.5 * D ** -0.5),
        'b_ada': nrm((L, N_MOD * D), 0.02),
        'w_in': nrm((L, D, D_IN), D ** -0.5),
        'mu_shift': jax.random.uniform(next(ks), (L, SHIFT_W), jnp.float32),
        'rwkv_w0': jax.random.uniform(next(ks), (L, D_A), jnp.float32, -6.0, -1.0),
        'rwkv_w2': nrm((L, D_LORA_W, D_A), 0.5 * D_LORA_W ** -0.5),
        'rwkv_a0': nrm((L, D_A), 0.5),
        'rwkv_a2': nrm((L, D_LORA_A, D_A), D_LORA_A ** -0.5),
        'rwkv_g2': nrm((L, D_LORA_G, D_A), D_LORA_G ** -0.5),
        'rwkv_k_k': 0.85 + nrm((L, D_A), 0.1),
        'rwkv_k_a': 1.0 + nrm((L, D_A), 0.1),
        'rwkv_r_k': nrm((L, H_A, HD_A), 0.1),
        'rwkv_gn_g': 1.0 + nrm((L, D_A), 0.05),
        'rwkv_gn_b': nrm((L, D_A), 0.02),
        'attn_sinks': nrm((L, H_Q), 1.0),
        'w_pa': nrm((L, D_A, D), DEEPNORM_BETA * D_A ** -0.5),
        'w_pb': nrm((L, D_B, D), DEEPNORM_BETA * D_B ** -0.5),
        'w_o': nrm((L, D, D), DEEPNORM_BETA * D ** -0.5),
        'ln1_g': 1.0 + nrm((L, D), 0.05),
        'ln1_b': nrm((L, D), 0.02),
        'peer_wq': nrm((L, D, PEER_HEADS * PEER_DKEY), D ** -0.5),
        'peer_sub_keys': nrm((L, 2, N_KEYS, PEER_HALF), PEER_HALF ** -0.5),
        'peer_u': nrm((L, N_EXPERTS, D), D ** -0.5),
        'peer_v': nrm((L, N_EXPERTS, D), DEEPNORM_BETA),
        'ln2_g': 1.0 + nrm((L, D), 0.05),
        'ln2_b': nrm((L, D), 0.02),
    }

def reference(x_prompt, x_sample, state_wkv, state_shift, cache_k_win, cache_v_win, c_prompt, c_sample,
              ln_in_g, ln_in_b, w_ada, b_ada, w_in, mu_shift, rwkv_w0, rwkv_w2, rwkv_a0, rwkv_a2, rwkv_g2,
              rwkv_k_k, rwkv_k_a, rwkv_r_k, rwkv_gn_g, rwkv_gn_b, attn_sinks, w_pa, w_pb, w_o, ln1_g, ln1_b,
              peer_wq, peer_sub_keys, peer_u, peer_v, ln2_g, ln2_b):
    xp = _layernorm(x_prompt, ln_in_g, ln_in_b)
    xs = _layernorm(x_sample, ln_in_g, ln_in_b)
    n_p = xp.shape[0]
    st_p, st_s = [], []
    for l in range(DEPTH):
        lp = {
            'w_ada': w_ada[l], 'b_ada': b_ada[l], 'w_in': w_in[l], 'mu_shift': mu_shift[l],
            'rwkv_w0': rwkv_w0[l], 'rwkv_w2': rwkv_w2[l], 'rwkv_a0': rwkv_a0[l], 'rwkv_a2': rwkv_a2[l],
            'rwkv_g2': rwkv_g2[l], 'rwkv_k_k': rwkv_k_k[l], 'rwkv_k_a': rwkv_k_a[l], 'rwkv_r_k': rwkv_r_k[l],
            'rwkv_gn_g': rwkv_gn_g[l], 'rwkv_gn_b': rwkv_gn_b[l], 'attn_sinks': attn_sinks[l],
            'w_pa': w_pa[l], 'w_pb': w_pb[l], 'w_o': w_o[l], 'ln1_g': ln1_g[l], 'ln1_b': ln1_b[l],
            'peer_wq': peer_wq[l], 'peer_sub_keys': peer_sub_keys[l], 'peer_u': peer_u[l],
            'peer_v': peer_v[l], 'ln2_g': ln2_g[l], 'ln2_b': ln2_b[l],
        }
        xp, sp = _layer(xp, c_prompt, jnp.zeros((n_p, SHIFT_W), xp.dtype),
                        jnp.zeros((n_p, H_A, HD_A, HD_A), jnp.float32), None, None, lp)
        xs, ss = _layer(xs, c_sample, state_shift[l], state_wkv[l], cache_k_win[l], cache_v_win[l], lp)
        st_p.append(sp)
        st_s.append(ss)
    stk = lambda sts, i: jnp.stack([s[i] for s in sts])
    return (xp, xs, stk(st_p, 1), stk(st_s, 1), stk(st_p, 0), stk(st_s, 0),
            stk(st_p, 2), stk(st_s, 2), stk(st_p, 3), stk(st_s, 3))


_drawn_inputs = setup_inputs


def setup_inputs(seed=0):
    import zlib

    import numpy as np

    out = dict(_drawn_inputs(seed))
    spreads = {}
    factors = {'rwkv_r_k': 5.447,
     'rwkv_gn_g': 31.842,
     'rwkv_gn_b': 64.0,
     'attn_sinks': 36.732,
     'ln2_b': 2.939,
     'w_pb': 3.047}
    for name, (base, spread) in spreads.items():
        noise = np.random.default_rng([zlib.crc32(name.encode()), seed]).standard_normal(out[name].shape)
        drawn = base * np.exp(spread * noise) if base else spread * noise
        out[name] = __import__('jax').numpy.asarray(drawn.astype(out[name].dtype))
    for name, factor in factors.items():
        out[name] = (out[name] * factor).astype(out[name].dtype)
    return out
```

```python
from contextlib import ExitStack

import concourse.bass as bass
from concourse import mybir

F32 = mybir.dt.float32
U32 = mybir.dt.uint32
ALU = mybir.AluOpType
ACT = mybir.ActivationFunctionType
AX_X = mybir.AxisListType.X

P = 128
D = 1024
KD = D // P
TP = 1024
NS = 8
T = TP + NS
NT = 3
TN = T // NT
HD = 64
NP = 4
NMOD = 48
C = 64
NC = TP // C
DECAY = 0.6065306597126334
ALPHA = 2.0 ** 0.25
LN_EPS = 1e-5
GN_EPS = 64e-5
WIN = 128
NB = TP // WIN
NEG = -1e30
NH = 8
TOPK = 16
NKEY = 128
SCALE = HD ** -0.5

CONST = {}
VEC = {}


def _layout(table, names):
    at = 0
    for name, n in names:
        table[name] = (at, n)
        at += n
    return at


LEVELS = (2, 4, 8, 16, 32)
NCONST = _layout(CONST, [("ident", 128), ("ident64", 64), ("headsum", 128), ("mean", 128), ("headmean", 128),
                         ("upper", 64), ("upper_incl", 64), ("first_u", 64), ("first_l", 64)]
                 + [(f"level{s}", 64) for s in LEVELS]
                 + [("iota", 128), ("iota16", 16), ("ones", 1), ("ln_eps", 1), ("gn_eps", 1)])
NVEC = _layout(VEC, [("ln_in_g", 8), ("ln_in_b", 8), ("ln1_g", 8), ("ln1_b", 8), ("ln2_g", 8), ("ln2_b", 8),
                     ("b_ada", NMOD), ("mu", 14), ("w0", 4), ("a0", 4), ("k_k", 4), ("k_a", 4), ("r_k", 4),
                     ("gn_g", 4), ("gn_b", 4)])
SH_M, SC_M, GT_M, SH_F, SC_F, GT_F = (8 * i for i in range(6))


def carry(eng, sem):
    eng.sem_inc(sem, 1)


class Chain:

    def __init__(self, eng, sem):
        self.eng, self.sem, self.base, self.n = eng, sem, 0, 0

    def __call__(self, ins):
        self.n += 1
        ins.then_inc(self.sem, 1)
        self.eng.wait_ge(self.sem, self.base + self.n)

    def enter(self, i, per):
        self.start = self.base + self.n
        self.base, self.n, self.per = i * per + self.start, 0, per

    def leave(self, turns):
        assert self.n == self.per, f"links per turn: {self.n}, not {self.per}"
        self.base, self.n = self.start + turns * self.per, 0


def kernel_program(nc, io, dbg):
    with ExitStack() as top:
        def sb(stack, name, shape, dt=F32):
            return stack.enter_context(nc.sbuf_tensor(name, shape, dt))

        def pb(stack, name, shape, dt=F32):
            return stack.enter_context(nc.psum_tensor(name, shape, dt))

        def sm(stack, *names):
            sems = [nc.alloc_semaphore(n) for n in names]
            stack.callback(nc.all_engine_barrier)
            stack.callback(nc.clear_and_free_semaphores, sems)
            return sems

        consts = sb(top, "consts", [P, NCONST])
        vecs = sb(top, "vecs", [P, NVEC])
        mod = sb(top, "mod", [P, NMOD, 1 + NS])
        x = sb(top, "x", [P, KD, T])
        h = sb(top, "h", [P, KD, T])
        env = dict(nc=nc, io=io, sb=sb, pb=pb, sm=sm, consts=consts, vecs=vecs, mod=mod, x=x, h=h, dbg=dbg)

        modulation_and_input(**env)
        layernorm(**env, name="in", modulate=(SC_M, SH_M))
        if dbg.get("stop") == 1:
            dump(**env, what={"x": x, "h": h, "mod": mod}); return
        with ExitStack() as mix:
            env["ya"] = sb(mix, "ya", [P, NP, T])
            env["ob"] = sb(mix, "ob", [P, NP, T])
            with ExitStack() as rw:
                for n in ("kt", "kh", "bh", "vt"):
                    env[n] = sb(rw, n, [P, NP, T])
                env["sgd"] = sb(rw, "sgd", [P, T])
                env["pc"] = sb(rw, "pc", [P, NP, NC])
                env["ws"] = sb(rw, "ws", [P, NP, NS])
                rwkv_inputs(**env)
                if dbg.get("stop") == 2:
                    dump(**env, what={n: env[n] for n in ("ya", "kt", "kh", "bh", "vt", "ob", "ws", "pc", "sgd")}); return
                rwkv_scan(**env)
                if dbg.get("stop") == 3:
                    dump(**env, what={n: env[n] for n in ("ya",)}); return
                rwkv_samples(**env)
            attention(**env)
            if dbg.get("stop") == 4:
                dump(**env, what={n: env[n] for n in ("ya", "ob")}); return
            env["merged"] = sb(mix, "merged", [P, KD, T])
            merge(**env)
            if dbg.get("stop") == 5:
                dump(**env, what={n: env[n] for n in ("merged",)}); return
            mixer_output(**env)
        layernorm(**env, name="1", modulate=(SC_F, SH_F))
        if dbg.get("stop") == 6:
            dump(**env, what={n: env[n] for n in ("x", "h")}); return
        with ExitStack() as pr:
            slots = sb(pr, "slots", [P, 3, T])
            peer_select(**env, slots=slots)
            if dbg.get("stop") == 7:
                dump(**env, what={"slots": slots}); return
            peer_gates(**env, slots=slots)
        with ExitStack() as ex:
            acc = sb(ex, "acc", [P, KD, T])
            peer_experts(**env, acc=acc)
            peer_output(**env, acc=acc)
            if dbg.get("stop") == 8:
                dump(**env, what={"acc": acc}); return
        layernorm(**env, name="2")
        store_output(**env)


def col(consts, name):
    at, n = CONST[name]
    return consts[:, at:at + n]


def vec(vecs, name, k=None):
    at, n = VEC[name]
    return vecs[:, at:at + n] if k is None else vecs[:, at + k:at + k + 1]


def dump(nc, io, sm, dbg, what, **_):
    with ExitStack() as ph:
        dumped, = sm(ph, "dumped")
        with nc.Block() as block:
            @block.sync
            def _(sp):
                for n, (name, t) in enumerate(what.items()):
                    d = nc.dram_tensor("dbg_" + name, list(t.shape), F32, kind="ExternalOutput").ap()
                    sp.dma_start(d, t[:]).then_inc(dumped, 16)
                sp.wait_ge(dumped, 16 * len(what))


def modulation_and_input(nc, io, sb, pb, sm, consts, vecs, mod, x, **_):
    TURNS, SLOTS = 6, 2
    with ExitStack() as ph:
        c = sb(ph, "c", [P, KD, 1 + NS])
        c_sig = sb(ph, "c_sig", [P, KD, 1 + NS])
        slab = sb(ph, "slab", [P, SLOTS, KD, 512])
        row = sb(ph, "row", [1 + NS, SLOTS, 512])
        row_ps = [pb(ph, f"row_ps{s}", [1 + NS, 512]) for s in range(SLOTS)]
        turned_ps = [pb(ph, f"turned_ps{s}", [P, 4, 1 + NS]) for s in range(SLOTS)]
        (c_loaded, small_loaded, x_loaded, slab0_loaded, slab1_loaded, sig_ready, silu_ready, slab_free,
         row_summed, row_free, row_ready, turned, turned_free, chain, carried) = sm(
            ph, "c_loaded", "small_loaded", "x_loaded", "slab0_loaded", "slab1_loaded", "sig_ready", "silu_ready",
            "slab_free", "row_summed", "row_free", "row_ready", "turned", "turned_free", "mod_chain", "mod_carried")
        slab_loaded = (slab0_loaded, slab1_loaded)
        with nc.Block() as block:
            @block.sync
            def _(sp):
                sp.dma_start(c[:], io["c"]).then_inc(c_loaded, 16)
                sp.dma_start(vecs[:], io["vecs"]).then_inc(small_loaded, 16)
                sp.dma_start(consts[:], io["consts"]).then_inc(small_loaded, 16)
                with sp.Fori(0, TURNS) as i:
                    for s in range(SLOTS):
                        sp.wait_ge(slab_free, i * SLOTS + s + 1)
                        sp.dma_start(slab[:, s], io["w_ada"][bass.ds(i * SLOTS + s, 1)].rearrange(
                            "o p k n -> p (o k) n")).then_inc(slab_loaded[s], 16)
                sp.dma_start(x[:], io["x"]).then_inc(x_loaded, 16)
                sp.wait_ge(x_loaded, 16)

            @block.scalar
            def _(act):
                act.wait_ge(c_loaded, 16)
                nc.scalar.activation(c_sig[:], c[:], ACT.Sigmoid).then_inc(sig_ready, 1)
                with act.Fori(0, TURNS) as i:
                    for s in range(SLOTS):
                        act.wait_ge(row_summed, i * SLOTS + s + 1)
                        act.wait_ge(row_free, i * SLOTS + s + 1)
                        nc.scalar.activation(row[:, s], row_ps[s][:], ACT.Copy).then_inc(row_ready, 1)

            @block.vector
            def _(dve):
                link = Chain(dve, chain)
                dve.sem_inc(slab_free, SLOTS)
                dve.sem_inc(row_free, SLOTS)
                dve.wait_ge(sig_ready, 1)
                nc.vector.tensor_tensor(c[:], c[:], c_sig[:], ALU.mult).then_inc(silu_ready, 1)
                dve.wait_ge(small_loaded, 32)
                with dve.Fori(0, TURNS) as i:
                    for s in range(SLOTS):
                        dve.wait_ge(turned, i * SLOTS + s + 1)
                        at = VEC["b_ada"][0]
                        bias = vecs[:, bass.ds(i * (4 * SLOTS) + (4 * s + at), 4)].unsqueeze(2).to_broadcast([P, 4, 1 + NS])
                        nc.vector.tensor_tensor(mod[:, bass.ds(i * (4 * SLOTS) + 4 * s, 4), :], turned_ps[s][:], bias,
                                                ALU.add).then_inc(turned_free, 1)
                dve.wait_ge(turned_free, TURNS * SLOTS)
                for m in (SC_M, SC_F):
                    link(nc.vector.tensor_scalar_add(mod[:, m:m + 8, :], mod[:, m:m + 8, :], 1.0))

            @block.tensor
            def _(pe):
                pe.wait_ge(silu_ready, 1)
                pe.wait_ge(small_loaded, 32)
                with pe.Fori(0, TURNS) as i:
                    for s in range(SLOTS):
                        pe.wait_ge(slab_loaded[s], i * 16 + 16)
                        if s == 0:
                            pe.wait_ge(row_ready, i * SLOTS)
                        for k in range(KD):
                            mm = nc.tensor.matmul(row_ps[s][:], c[:, k], slab[:, s, k], start=k == 0, stop=k == KD - 1)
                        mm.then_inc(row_summed, 1)
                        pe.wait_ge(row_summed, i * SLOTS + s + 1)
                        pe.sem_inc(slab_free, 1)
                    for s in range(SLOTS):
                        pe.wait_ge(row_ready, i * SLOTS + s + 1)
                        pe.wait_ge(turned_free, i * SLOTS)
                        carry(pe, carried)
                        for j in range(4):
                            mm = nc.tensor.transpose(turned_ps[s][:, j], row[:, s, j * P:(j + 1) * P],
                                                     col(consts, "ident")[0:1 + NS, 0:1 + NS])
                        mm.then_inc(turned, 1)
                        pe.wait_ge(turned, i * SLOTS + s + 1)
                        pe.sem_inc(row_free, 1)


def layernorm(nc, io, sb, pb, sm, consts, vecs, mod, x, h, name, modulate=None, **_):
    g, b = f"ln_{name}_g" if name == "in" else f"ln{name}_g", f"ln_{name}_b" if name == "in" else f"ln{name}_b"
    with ExitStack() as ph:
        stat = sb(ph, f"stat_{name}", [P, NT, TN])
        square = sb(ph, f"square_{name}", [P, 2, NT, TN])
        mean_ps = pb(ph, f"mean_ps_{name}", [P, NT, 512])
        var_ps = pb(ph, f"var_ps_{name}", [P, NT, 512])
        mean_summed, mean_ready, centred, squared, var_summed, std_ready, chain = sm(
            ph, *(f"{n}_{name}" for n in ("mean_summed", "mean_ready", "centred", "squared", "var_summed",
                                          "std_ready", "ln_chain")))
        flat = stat[:].rearrange("p t n -> p (t n)")
        with nc.Block() as block:
            @block.tensor
            def _(pe):
                for t in range(NT):
                    for k in range(KD):
                        mm = nc.tensor.matmul(mean_ps[:, t, 0:TN], col(consts, "mean"), x[:, k, t * TN:(t + 1) * TN],
                                              start=k == 0, stop=k == KD - 1)
                mm.then_inc(mean_summed, 1)
                for k in range(KD):
                    pe.wait_ge(squared, k + 1)
                    for t in range(NT):
                        mm = nc.tensor.matmul(var_ps[:, t, 0:TN], col(consts, "mean"), square[:, k % 2, t],
                                              start=k == 0, stop=k == KD - 1)
                    mm.then_inc(var_summed, 1)

            @block.scalar
            def _(act):
                act.wait_ge(mean_summed, 1)
                nc.scalar.activation(stat[:], mean_ps[:, :, 0:TN], ACT.Copy).then_inc(mean_ready, 1)
                for k in range(KD):
                    act.wait_ge(centred, k + 1)
                    if k >= 2:
                        act.wait_ge(var_summed, k - 1)
                    nc.scalar.activation(square[:, k % 2].rearrange("p t n -> p (t n)"), x[:, k], ACT.Square)\
                        .then_inc(squared, 1)
                act.wait_ge(var_summed, KD)
                nc.scalar.activation(stat[:], var_ps[:, :, 0:TN], ACT.Sqrt, bias=col(consts, "ln_eps"))\
                    .then_inc(std_ready, 1)

            @block.vector
            def _(dve):
                link = Chain(dve, chain)
                dve.wait_ge(mean_ready, 1)
                for k in range(KD):
                    nc.vector.tensor_tensor(x[:, k], x[:, k], flat, ALU.subtract).then_inc(centred, 1)
                dve.wait_ge(std_ready, 1)
                link(nc.vector.reciprocal(flat, flat))
                for k in range(KD):
                    link(nc.vector.tensor_tensor(x[:, k], x[:, k], flat, ALU.mult))
                    link(nc.vector.tensor_scalar(x[:, k], x[:, k], vec(vecs, g, k), vec(vecs, b, k), ALU.mult, ALU.add))
                    if modulate:
                        sc, sh = (m + k for m in modulate)
                        nc.vector.tensor_scalar(h[:, k, 0:TP], x[:, k, 0:TP], mod[:, sc, 0:1], mod[:, sh, 0:1],
                                                ALU.mult, ALU.add).then_inc(chain, 1)
                        link.n += 1
                        link(nc.vector.tensor_tensor(h[:, k, TP:T], x[:, k, TP:T], mod[:, sc, 1:], ALU.mult))
                        link(nc.vector.tensor_tensor(h[:, k, TP:T], h[:, k, TP:T], mod[:, sh, 1:], ALU.add))


def rwkv_inputs(nc, io, sb, pb, sm, consts, vecs, mod, x, h, ya, ob, kt, kh, bh, vt, sgd, pc, ws, **_):
    with ExitStack() as ph:
        w = sb(ph, "w", [P, 3, KD, P])
        w_small = sb(ph, "w_small", [P, P])
        before = sb(ph, "before", [P, 14, NS])
        last = sb(ph, "last", [P, 14, 1 + NS])
        reset = sb(ph, "reset", [P, T])
        room = x[:].rearrange("p k n -> p (k n)")
        raw = [room[:, q * (1 + T):(q + 1) * (1 + T)] for q in range(3)]
        lora, tmp, sz = (room[:, 3 * (1 + T) + q * T:3 * (1 + T) + (q + 1) * T] for q in range(3))
        a = raw[0]
        norm, decay = raw[1], raw[2]
        one_minus_ka = sb(ph, "one_minus_ka", [P, NP])
        ps = [pb(ph, f"ps{s}", [P, NT, 512]) for s in range(2)]
        (loaded, w0_loaded, w1_loaded, w2_loaded, ws_loaded, w_free, summed, taken, mixed, tanh_ready, sq_ready,
         rk_ready, norm_taken, scan_ready, exp_ready, exp_used, bonus_taken, turn_done, small_free, chain, out_done, x_saved) = sm(
            ph, "loaded", "w0_loaded", "w1_loaded", "w2_loaded", "ws_loaded", "w_free", "summed", "taken", "mixed",
            "tanh_ready", "sq_ready", "rk_ready", "norm_taken", "scan_ready", "exp_ready", "exp_used", "bonus_taken",
            "turn_done", "small_free", "in_chain", "out_done", "x_saved")
        w_loaded = (w0_loaded, w1_loaded, w2_loaded)

        def tiles(buf):
            return buf[:].rearrange("p (t n) -> p t n", t=NT)

        with nc.Block() as block:
            @block.sync
            def _(sp):
                sp.dma_start(io["x_saved"], x[:]).then_inc(x_saved, 16)
                sp.dma_start(before[:], io["shift_before"]).then_inc(loaded, 16)
                sp.dma_start(reset[:], io["reset"]).then_inc(loaded, 16)
                for q in range(2):
                    sp.dma_start(w[:, q], io["w_in"][q]).then_inc(w_loaded[q], 16)
                with sp.Fori(0, NP) as p:
                    sp.wait_ge(w_free, 2 + p * 5)
                    for q in range(3):
                        sp.dma_start(w[:, q], io["w_in"][bass.ds(p * 3 + (2 + q), 1)].rearrange(
                            "o p k n -> p (o k) n")).then_inc(w_loaded[q], 16)
                    sp.dma_start(w_small[:], io["w_lora"][bass.ds(p, 1)].rearrange("o p n -> p (o n)"))\
                        .then_inc(ws_loaded, 16)
                sp.wait_ge(turn_done, NP)
                sp.dma_start(io["shift_out"], last[:]).then_inc(out_done, 16)
                sp.wait_ge(out_done, 16)

            @block.tensor
            def _(pe):
                def project(q, s):
                    for t in range(NT):
                        for k in range(KD):
                            mm = nc.tensor.matmul(ps[s][:, t, 0:TN], w[:, q, k], h[:, k, t * TN:(t + 1) * TN],
                                                  start=k == 0, stop=k == KD - 1)
                    return mm

                for q in range(2):
                    pe.wait_ge(w_loaded[q], 16)
                    project(q, q).then_inc(summed, 1)
                    pe.wait_ge(summed, q + 1)
                    pe.sem_inc(w_free, 1)
                pe.wait_ge(tanh_ready, 1)
                with pe.Fori(0, NP) as p:
                    for q in range(3):
                        pe.wait_ge(w_loaded[q], p * 16 + (32 if q < 2 else 16))
                        if q == 0:
                            pe.wait_ge(bonus_taken, p)
                        pe.wait_ge(taken, p * 6 + (2, 2, 3)[q])
                        project(q, q % 2).then_inc(summed, 1)
                        pe.wait_ge(summed, p * 7 + 3 + q)
                        pe.sem_inc(w_free, 1)
                    pe.wait_ge(ws_loaded, p * 16 + 16)
                    pe.wait_ge(taken, p * 6 + 4)
                    for t in range(NT):
                        mm = nc.tensor.matmul(ps[1][:, t, 0:TN], w_small[0:HD], lora[0:HD, t * TN:(t + 1) * TN],
                                              start=True, stop=True)
                    mm.then_inc(summed, 1)
                    pe.wait_ge(taken, p * 6 + 5)
                    for t in range(NT):
                        mm = nc.tensor.matmul(ps[0][:, t, 0:TN], w_small[HD:P], lora[HD:P, t * TN:(t + 1) * TN],
                                              start=True, stop=True)
                    mm.then_inc(summed, 1)
                    pe.wait_ge(summed, p * 7 + 7)
                    pe.sem_inc(w_free, 2)
                    pe.wait_ge(taken, p * 6 + 6)
                    pe.wait_ge(sq_ready, p + 1)
                    for t in range(NT):
                        mm = nc.tensor.matmul(ps[1][:, t, 0:TN], col(consts, "headsum"), tmp[:, t * TN:(t + 1) * TN],
                                              start=True, stop=True)
                    mm.then_inc(summed, 1)
                    pe.wait_ge(taken, p * 6 + 7)
                    pe.wait_ge(rk_ready, p + 1)
                    for t in range(NT):
                        mm = nc.tensor.matmul(ps[0][:, t, 0:TN], col(consts, "headsum"), tmp[:, t * TN:(t + 1) * TN],
                                              start=True, stop=True)
                    mm.then_inc(summed, 1)

            @block.scalar
            def _(act):
                act.wait_ge(x_saved, 16)
                for q in range(2):
                    act.wait_ge(summed, q + 1)
                    nc.scalar.activation(raw[q][:, 1:].rearrange("p (t n) -> p t n", t=NT), ps[q][:, :, 0:TN], ACT.Copy)\
                        .then_inc(taken, 1)
                act.wait_ge(mixed, 1)
                nc.scalar.activation(lora[0:HD], lora[0:HD], ACT.Tanh).then_inc(tanh_ready, 1)
                act.wait_ge(mixed, 2)
                nc.scalar.activation(sgd[:], sgd[:], ACT.Sigmoid).then_inc(tanh_ready, 1)
                with act.Fori(0, NP) as p:
                    act.wait_ge(turn_done, p)
                    for q in range(3):
                        act.wait_ge(summed, p * 7 + 3 + q)
                        nc.scalar.activation(raw[q][:, 1:].rearrange("p (t n) -> p t n", t=NT), ps[q % 2][:, :, 0:TN],
                                             ACT.Copy).then_inc(taken, 1)
                    act.wait_ge(summed, p * 7 + 6)
                    nc.scalar.activation(tiles(sz), ps[1][:, :, 0:TN], ACT.Sigmoid,
                                         bias=vecs[:, bass.ds(p + VEC["w0"][0], 1)]).then_inc(taken, 1)
                    act.wait_ge(summed, p * 7 + 7)
                    act.wait_ge(mixed, p * 3 + 3)
                    nc.scalar.activation(a[:, 1:].rearrange("p (t n) -> p t n", t=NT), ps[0][:, :, 0:TN], ACT.Sigmoid,
                                         bias=vecs[:, bass.ds(p + VEC["a0"][0], 1)]).then_inc(taken, 1)
                    act.wait_ge(summed, p * 7 + 8)
                    act.wait_ge(mixed, p * 3 + 4)
                    nc.scalar.activation(norm[:, 1:].rearrange("p (t n) -> p t n", t=NT), ps[1][:, :, 0:TN], ACT.Sqrt)\
                        .then_inc(taken, 1)
                    act.wait_ge(mixed, p * 3 + 5)
                    for n, sign in enumerate((-DECAY, DECAY, -DECAY)):
                        act.wait_ge(scan_ready, p * 2 + (1, 1, 2)[n])
                        if n:
                            act.wait_ge(exp_used, p * 2 + n)
                        nc.scalar.activation(decay[:, 1:], sz[:], ACT.Exp, scale=sign).then_inc(exp_ready, 1)

            @block.gpsimd
            def _(pool):
                pool.wait_ge(x_saved, 16)
                for q in range(3):
                    nc.gpsimd.memset(raw[q][:, 0:1], 0.0).then_inc(small_free, 1)

            @block.vector
            def _(dve):
                link = Chain(dve, chain)
                V = nc.vector

                def mix(q, dst, m):
                    mu = vecs[:, bass.ds(m + VEC["mu"][0], 1)] if not isinstance(m, int) else vec(vecs, "mu", m)
                    m_ = bass.ds(m, 1)
                    V.tensor_tensor(tmp[:, 0:TP], raw[q][:, 0:TP], raw[q][:, 1:1 + TP], ALU.subtract).then_inc(chain, 1)
                    link.n += 1
                    V.tensor_copy(last[:, m_, :], raw[q][:, TP:1 + T].unsqueeze(1)).then_inc(chain, 1)
                    link.n += 1
                    link(V.tensor_tensor(tmp[:, TP:T].unsqueeze(1), before[:, m_, :], raw[q][:, 1 + TP:1 + T].unsqueeze(1),
                                         ALU.subtract))
                    ins = V.scalar_tensor_tensor(dst, tmp[:], mu, raw[q][:, 1:], ALU.mult, ALU.add)
                    ins.then_inc(mixed, 1)

                dve.wait_ge(loaded, 32)
                dve.wait_ge(small_free, 3)
                link(V.tensor_scalar(one_minus_ka[:], vec(vecs, "k_a"), -1.0, 1.0, ALU.mult, ALU.add))
                for q in range(2):
                    dve.wait_ge(taken, q + 1)
                    mix(q, (lora, sgd)[q][:], 12 + q)
                    dve.wait_ge(mixed, q + 1)
                with dve.Fori(0, NP) as p:
                    link.enter(p, 25)

                    def at(t):
                        return t[:, bass.ds(p, 1), :].rearrange("p o n -> p (o n)")

                    def prompt(t):
                        return t[:, bass.ds(p, 1), 0:TP].rearrange("p o n -> p (o n)")

                    def feature(name):
                        return vecs[:, bass.ds(p + VEC[name][0], 1)]

                    for q, dst in enumerate((ya, kh, vt)):
                        dve.wait_ge(taken, p * 6 + 3 + q)
                        mix(q, at(dst), p + 4 * q)
                        dve.wait_ge(mixed, p * 3 + 3 + q)
                    link(V.tensor_scalar(at(kt), at(kh), feature("k_k"), None, ALU.mult))
                    V.tensor_tensor(tmp[:], at(kt), at(kt), ALU.mult).then_inc(sq_ready, 1)
                    dve.wait_ge(taken, p * 6 + 6)
                    link(V.tensor_tensor_scan(decay[:, 1:], reset[:], sz[:], 0.0, ALU.mult, ALU.add))
                    dve.wait_ge(taken, p * 6 + 7)
                    dve.wait_ge(sq_ready, p + 1)
                    link(V.tensor_scalar(at(bh), a[:, 1:], feature("k_a"), one_minus_ka[:, bass.ds(p, 1)], ALU.mult, ALU.add))
                    link(V.tensor_tensor(at(kh), at(kh), at(bh), ALU.mult))
                    dve.wait_ge(taken, p * 6 + 8)
                    ins = V.scalar_tensor_tensor(tmp[:], at(ya), feature("r_k"), at(kh), ALU.mult, ALU.mult)
                    ins.then_inc(rk_ready, 1)
                    link(V.tensor_scalar_max(norm[:, 1:], norm[:, 1:], 1e-12))
                    link(V.reciprocal(norm[:, 1:], norm[:, 1:]))
                    link(V.tensor_tensor(at(kt), at(kt), norm[:, 1:], ALU.mult))
                    link(V.tensor_tensor(at(bh), at(kt), a[:, 1:], ALU.mult))
                    link(V.tensor_tensor(norm[:, 1:], decay[:, 1:], sz[:], ALU.subtract))
                    ins = V.tensor_copy(sz[:], decay[:, 1:])
                    ins.then_inc(scan_ready, 1)
                    dve.wait_ge(summed, p * 7 + 9)
                    ins = V.tensor_tensor(at(ob).rearrange("p (t n) -> p t n", t=NT), ps[0][:, :, 0:TN],
                                          at(vt).rearrange("p (t n) -> p t n", t=NT), ALU.mult)
                    ins.then_inc(bonus_taken, 1)
                    dve.wait_ge(exp_ready, p * 3 + 1)
                    V.tensor_tensor(prompt(ya), prompt(ya), decay[:, 1:1 + TP], ALU.mult).then_inc(chain, 1)
                    link.n += 1
                    V.tensor_copy(ws[:, bass.ds(p, 1), :], decay[:, 1 + TP:1 + T].unsqueeze(1)).then_inc(chain, 1)
                    link.n += 1
                    link(V.tensor_copy(pc[:, bass.ds(p, 1), :], decay[:, 1:1 + TP].rearrange("p (c s) -> p c s", s=C)[:, :, C - 1].unsqueeze(1)))
                    dve.sem_inc(exp_used, 1)
                    dve.wait_ge(exp_ready, p * 3 + 2)
                    V.tensor_tensor(prompt(bh), prompt(bh), decay[:, 1:1 + TP], ALU.mult).then_inc(chain, 1)
                    link.n += 1
                    link(V.tensor_tensor(prompt(kh), prompt(kh), decay[:, 1:1 + TP], ALU.mult))
                    link(V.tensor_copy(sz[:], norm[:, 1:]))
                    dve.sem_inc(scan_ready, 1)
                    dve.sem_inc(exp_used, 1)
                    dve.wait_ge(exp_ready, p * 3 + 3)
                    link(V.tensor_tensor(prompt(kt), prompt(kt), decay[:, 1:1 + TP], ALU.mult))
                    dve.wait_ge(rk_ready, p + 1)
                    dve.wait_ge(bonus_taken, p + 1)
                    dve.sem_inc(turn_done, 1)
                    link.leave(NP)


def rwkv_scan(nc, io, sb, pb, sm, consts, x, ya, kt, kh, bh, vt, pc, **_):
    NL = len(LEVELS)
    with ExitStack() as ph:
        room = x[:].rearrange("p k n -> p (k n)")
        at = [0]

        def rows(*shape):
            n = 1
            for v in shape:
                n *= v
            ap = room[:, at[0]:at[0] + n]
            at[0] += n
            if len(shape) == 3:
                ap = ap.rearrange("p (a b c) -> p a b c", a=shape[0], b=shape[1])
            elif len(shape) == 2:
                ap = ap.rearrange("p (a b) -> p a b", a=shape[0])
            return ap

        kr = rows(NP, 2, C)
        bhc, khc, vtc = rows(NP, C), rows(NP, C), rows(NP, C)
        tb_up, tk_up, ab_up, ak_up = rows(NP, C), rows(NP, C), rows(NP, C), rows(NP, C)
        inv = rows(2, NP, C)
        level = rows(NL, NP, C)
        q_sb = rows(NP, C)
        tok = rows(3, NP, C)
        rhs, sa, state = rows(NP, C), rows(NP, C), rows(NP, C)
        b_ps = pb(ph, "b_ps", [P, NP, 2, C])
        k_ps = pb(ph, "k_ps", [P, NP, 2, C])
        t_ps = pb(ph, "t_ps", [P, 2, NP, C])
        tok_ps = pb(ph, "tok_ps", [P, 4, NP, C])
        q_ps = pb(ph, "q_ps", [P, NP, C])
        inv_ps = pb(ph, "inv_ps", [P, 2, NP, C])
        seq_ps = pb(ph, "seq_ps", [P, 2, NP, C])
        (staged, scores, masked, tok_turned, tok_ready, levels_ready, q_summed, q_ready, inv_summed, inv_grown,
         rhs_summed, rhs_ready, sa_summed, sa_ready, out_summed, y_ready, state_ready, chain, pool_chain, saved, carried) = sm(
            ph, "staged", "scores", "masked", "tok_turned", "tok_ready", "levels_ready", "q_summed", "q_ready",
            "inv_summed", "inv_grown", "rhs_summed", "rhs_ready", "sa_summed", "sa_ready", "out_summed", "y_ready",
            "state_ready", "scan_chain", "pool_chain", "state_saved", "scan_carried")
        halves = [slice(0, HD), slice(HD, P)]

        def mask(name, n=NP):
            return col(consts, name).unsqueeze(1).to_broadcast([P, n, C])

        def chunk(t, c):
            return t[:, :, bass.ds(c * C, C)]

        with nc.Block() as block:
            @block.gpsimd
            def _(pool):
                link = Chain(pool, pool_chain)
                with pool.Fori(0, NC) as c:
                    pool.wait_ge(out_summed, c)
                    G = nc.gpsimd
                    G.tensor_copy(kr[:, :, 0], chunk(kt, c)).then_inc(staged, 1)
                    G.tensor_copy(kr[:, :, 1], chunk(ya, c)).then_inc(staged, 1)
                    G.tensor_copy(bhc, chunk(bh, c)).then_inc(staged, 1)
                    G.tensor_copy(khc, chunk(kh, c)).then_inc(staged, 1)
                    G.tensor_copy(vtc, chunk(vt, c)).then_inc(staged, 1)
                    pool.wait_ge(masked, c * 6 + 6)
                    for n, s in enumerate(LEVELS):
                        G.tensor_tensor(level[:, n], tb_up, mask(f"level{s}"), ALU.mult).then_inc(levels_ready, 1)

            @block.tensor
            def _(pe):
                def heads(out, lhsT, rhs, start=True, stop=True):
                    for p in range(NP):
                        for half in halves:
                            mm = nc.tensor.matmul(out(p, half), lhsT(p, half), rhs(p, half), start=start, stop=stop)
                    return mm

                def of(t, *idx):
                    return lambda p, half: t[(half,) + idx + (p,)]

                with pe.Fori(0, NC) as c:
                    pe.wait_ge(staged, c * 5 + 5)
                    pe.wait_ge(state_ready, c + 1)
                    pe.wait_ge(masked, c * 6)
                    carry(pe, carried)
                    heads(lambda p, r: b_ps[r, p].rearrange("q a b -> q (a b)"), of(bhc), lambda p, r: kr[r, p].rearrange("q a b -> q (a b)"))
                    heads(lambda p, r: k_ps[r, p].rearrange("q a b -> q (a b)"), of(khc), lambda p, r: kr[r, p].rearrange("q a b -> q (a b)"))
                    heads(of(t_ps, 0), lambda p, r: kr[r, p, 0], of(bhc)).then_inc(scores, 1)
                    pe.wait_ge(tok_ready, c)
                    carry(pe, carried)
                    for n, src in enumerate((vtc, bhc, khc)):
                        mm = heads(of(tok_ps, n), of(src), lambda p, r: col(consts, "ident64")[r])
                    mm.then_inc(tok_turned, 1)
                    for n in range(NL):
                        pe.wait_ge(levels_ready, c * NL + n + 1)
                        if n == 0:
                            pe.wait_ge(masked, c * 6 + 6)
                            pe.wait_ge(q_ready, c * NL)
                            carry(pe, carried)
                        else:
                            pe.wait_ge(inv_grown, c * NL + n)
                            carry(pe, carried)
                        heads(of(q_ps), of(level, n), of(inv, 0)).then_inc(q_summed, 1)
                        pe.wait_ge(q_ready, c * NL + n + 1)
                        carry(pe, carried)
                        if n < NL - 1:
                            heads(of(inv_ps, 0), of(inv, 1), of(q_sb))
                        heads(of(inv_ps, 1), of(q_sb), of(inv, 1)).then_inc(inv_summed, 1)
                    pe.wait_ge(state_ready, c + 1)
                    pe.wait_ge(tok_ready, c + 1)
                    carry(pe, carried)
                    for p in range(NP):
                        for r in halves:
                            nc.tensor.matmul(seq_ps[r, 0, p], kr[r, p, 0], state[r, p], start=True, stop=False)
                            mm = nc.tensor.matmul(seq_ps[r, 0, p], tk_up[r, p], tok[r, 0, p], start=False, stop=True)
                    mm.then_inc(rhs_summed, 1)
                    pe.wait_ge(rhs_ready, c + 1)
                    pe.wait_ge(inv_grown, c * NL + NL)
                    carry(pe, carried)
                    heads(of(seq_ps, 1), of(inv, 1), of(rhs)).then_inc(sa_summed, 1)
                    pe.wait_ge(sa_ready, c + 1)
                    carry(pe, carried)
                    for p in range(NP):
                        for r in halves:
                            nc.tensor.matmul(seq_ps[r, 0, p], state[r, p], kr[r, p, 1], start=True, stop=False)
                            nc.tensor.matmul(seq_ps[r, 0, p], sa[r, p], ab_up[r, p], start=False, stop=False)
                            nc.tensor.matmul(seq_ps[r, 0, p], tok[r, 0, p], ak_up[r, p], start=False, stop=True)
                    for p in range(NP):
                        for r in halves:
                            nc.tensor.matmul(t_ps[r, 1, p], tok[r, 1, p], sa[r, p], start=True, stop=False)
                            mm = nc.tensor.matmul(t_ps[r, 1, p], tok[r, 2, p], tok[r, 0, p], start=False, stop=True)
                    mm.then_inc(out_summed, 1)

            @block.scalar
            def _(act):
                with act.Fori(0, NC) as c:
                    act.wait_ge(tok_turned, c + 1)
                    act.wait_ge(out_summed, c)
                    nc.scalar.activation(tok, tok_ps[:, 0:3], ACT.Copy).then_inc(tok_ready, 1)
                    for n in range(NL):
                        act.wait_ge(q_summed, c * NL + n + 1)
                        nc.scalar.activation(q_sb, q_ps[:], ACT.Copy).then_inc(q_ready, 1)
                    act.wait_ge(rhs_summed, c + 1)
                    nc.scalar.activation(rhs, seq_ps[:, 0], ACT.Copy, scale=-1.0).then_inc(rhs_ready, 1)
                    act.wait_ge(sa_summed, c + 1)
                    nc.scalar.activation(sa, seq_ps[:, 1], ACT.Copy).then_inc(sa_ready, 1)
                    act.wait_ge(out_summed, c + 1)
                    nc.scalar.activation(chunk(ya, c), seq_ps[:, 0], ACT.Copy).then_inc(y_ready, 1)

            @block.vector
            def _(dve):
                link = Chain(dve, chain)
                V = nc.vector
                V.memset(state, 0.0).then_inc(state_ready, 1)
                with dve.Fori(0, NC) as c:
                    link.enter(c, 3)
                    dve.wait_ge(scores, c + 1)
                    V.tensor_tensor(tb_up, b_ps[:, :, 0], mask("upper"), ALU.mult).then_inc(masked, 1)
                    V.tensor_tensor(ab_up, b_ps[:, :, 1], mask("upper_incl"), ALU.mult).then_inc(masked, 1)
                    V.tensor_tensor(tk_up, k_ps[:, :, 0], mask("upper"), ALU.mult).then_inc(masked, 1)
                    V.tensor_tensor(ak_up, k_ps[:, :, 1], mask("upper_incl"), ALU.mult).then_inc(masked, 1)
                    V.tensor_tensor(inv[:, 0], t_ps[:, 0], mask("first_l"), ALU.mult).then_inc(chain, 1)
                    link.n += 1
                    link(V.tensor_tensor(inv[:, 1], b_ps[:, :, 0], mask("first_u"), ALU.mult))
                    V.scalar_tensor_tensor(inv[:, 0], inv[:, 0], -1.0, mask("ident64"), ALU.mult, ALU.add).then_inc(masked, 1)
                    V.scalar_tensor_tensor(inv[:, 1], inv[:, 1], -1.0, mask("ident64"), ALU.mult, ALU.add).then_inc(masked, 1)
                    for n in range(NL):
                        dve.wait_ge(inv_summed, c * NL + n + 1)
                        if n == 0:
                            dve.wait_ge(masked, c * 6 + 6)
                        else:
                            dve.wait_ge(inv_grown, c * NL + n)
                        if n < NL - 1:
                            V.tensor_tensor(inv, inv, inv_ps[:], ALU.subtract).then_inc(inv_grown, 1)
                        else:
                            V.tensor_tensor(inv[:, 1], inv[:, 1], inv_ps[:, 1], ALU.subtract).then_inc(inv_grown, 1)
                    dve.wait_ge(out_summed, c + 1)
                    link(V.tensor_tensor(state, state, t_ps[:, 1], ALU.add))
                    through = pc[:, :, bass.ds(c, 1)].to_broadcast([P, NP, C])
                    V.tensor_tensor(state, state, through, ALU.mult).then_inc(state_ready, 1)
                    dve.wait_ge(state_ready, c + 2)
                    link.leave(NC)

            @block.sync
            def _(sp):
                sp.wait_ge(state_ready, NC + 1)
                sp.dma_start(io["wkv_prompt_out"], state).then_inc(saved, 16)
                sp.wait_ge(saved, 16)


def rwkv_samples(nc, io, sb, pb, sm, consts, vecs, x, ya, ob, kt, kh, bh, vt, sgd, ws, **_):
    with ExitStack() as ph:
        room = x[:].rearrange("p k n -> p (k n)")
        n_state = NP * NS * HD
        state, part, part2 = (room[:, q * n_state:(q + 1) * n_state].rearrange("p (a b c) -> p a b c", a=NP, b=NS)
                              for q in range(3))
        sum_ps = pb(ph, "sum_ps", [P, NP, NS, HD])
        spread_ps = pb(ph, "spread_ps", [P, NP, NS, HD])
        loaded, part_ready, summed, used, state_ready, chain, stored = sm(
            ph, "state_loaded", "part_ready", "part_summed", "sums_used", "new_state", "samples_chain", "new_state_stored")

        def spread(t):
            return t[:, :, TP:T].unsqueeze(3).to_broadcast([P, NP, NS, HD])

        unit = col(consts, "ident64").unsqueeze(1).unsqueeze(1).to_broadcast([P, NP, NS, HD])
        with nc.Block() as block:
            @block.sync
            def _(sp):
                sp.dma_start(state, io["state_wkv"]).then_inc(loaded, 16)
                sp.wait_ge(state_ready, 1)
                sp.dma_start(io["wkv_sample_out"], state).then_inc(stored, 16)
                sp.wait_ge(stored, 16)

            @block.tensor
            def _(pe):
                for n, (src, out) in enumerate(((part, sum_ps), (part2, spread_ps), (part, sum_ps))):
                    pe.wait_ge(part_ready, n + 1)
                    for p in range(NP):
                        mm = nc.tensor.matmul(out[:, p].rearrange("p a b -> p (a b)"), col(consts, "headsum"),
                                              src[:, p].rearrange("p a b -> p (a b)"), start=True, stop=True)
                    mm.then_inc(summed, 1)

            @block.vector
            def _(dve):
                link = Chain(dve, chain)
                V = nc.vector
                dve.wait_ge(loaded, 16)
                V.tensor_tensor(part, state, spread(kt), ALU.mult).then_inc(part_ready, 1)
                V.tensor_tensor(part2, unit, spread(vt), ALU.mult).then_inc(part_ready, 1)
                decay = ws[:].unsqueeze(3).to_broadcast([P, NP, NS, HD])
                link(V.tensor_tensor(state, state, decay, ALU.mult))
                dve.wait_ge(summed, 1)
                link(V.tensor_tensor(part, sum_ps[:], spread(bh), ALU.mult))
                link(V.tensor_tensor(state, state, part, ALU.subtract))
                dve.wait_ge(summed, 2)
                link(V.tensor_tensor(part2, spread_ps[:], spread(kh), ALU.mult))
                link(V.tensor_tensor(state, state, part2, ALU.add))
                dve.sem_inc(state_ready, 1)
                V.tensor_tensor(part, state, spread(ya), ALU.mult).then_inc(part_ready, 1)
                dve.wait_ge(summed, 3)
                link(V.tensor_tensor(part2, sum_ps[:], unit, ALU.mult))
                V.tensor_reduce(ya[:, :, TP:T], part2, AX_X, ALU.add).then_inc(used, 1)
    with ExitStack() as ph:
        square = [sb(ph, f"gn_sq{q}", [P, NT, TN]) for q in range(2)]
        g2 = sb(ph, "g2_gn", [P, NP, P])
        m_ps = pb(ph, "m_ps", [P, NT, 512])
        g_ps = pb(ph, "g_ps", [P, NT, 512])
        (g2_loaded, mean_summed, centred, squared, var_summed, std_ready, std_used, gate_summed, gated, chain) = sm(
            ph, "g2_loaded", "gn_mean_summed", "gn_centred", "gn_squared", "gn_var_summed", "gn_std_ready",
            "gn_std_used", "gate_summed", "gated", "gn_chain")

        def tiles(t):
            return t.rearrange("p (t n) -> p t n", t=NT)

        with nc.Block() as block:
            @block.sync
            def _(sp):
                sp.dma_start(g2[:], io["g2"]).then_inc(g2_loaded, 16)

            @block.tensor
            def _(pe):
                pe.wait_ge(g2_loaded, 16)
                for p in range(NP):
                    for t in range(NT):
                        mm = nc.tensor.matmul(m_ps[:, t, 0:TN], col(consts, "headmean"), ya[:, p, t * TN:(t + 1) * TN],
                                              start=True, stop=True)
                    mm.then_inc(mean_summed, 1)
                    if p:
                        pe.wait_ge(gated, p)
                    for t in range(NT):
                        mm = nc.tensor.matmul(g_ps[:, t, 0:TN], g2[:, p], sgd[:, t * TN:(t + 1) * TN],
                                              start=True, stop=True)
                    mm.then_inc(gate_summed, 1)
                    pe.wait_ge(squared, p + 1)
                    for t in range(NT):
                        mm = nc.tensor.matmul(m_ps[:, t, 0:TN], col(consts, "headmean"), square[0][:, t],
                                              start=True, stop=True)
                    mm.then_inc(var_summed, 1)
                    pe.wait_ge(std_ready, p + 1)

            @block.scalar
            def _(act):
                for p in range(NP):
                    act.wait_ge(centred, p + 1)
                    if p:
                        act.wait_ge(var_summed, p)
                    nc.scalar.activation(square[0][:], tiles(ya[:, p]), ACT.Square).then_inc(squared, 1)
                    act.wait_ge(var_summed, p + 1)
                    if p:
                        act.wait_ge(std_used, p)
                    nc.scalar.activation(square[1][:], m_ps[:, :, 0:TN], ACT.Sqrt, bias=col(consts, "gn_eps"))\
                        .then_inc(std_ready, 1)

            @block.vector
            def _(dve):
                link = Chain(dve, chain)
                V = nc.vector
                for p in range(NP):
                    y = ya[:, p]
                    dve.wait_ge(mean_summed, p + 1)
                    V.tensor_tensor(tiles(y), tiles(y), m_ps[:, :, 0:TN], ALU.subtract).then_inc(centred, 1)
                    dve.wait_ge(std_ready, p + 1)
                    link(V.reciprocal(square[1][:], square[1][:]))
                    V.tensor_tensor(tiles(y), tiles(y), square[1][:], ALU.mult).then_inc(std_used, 1)
                    dve.wait_ge(std_used, p + 1)
                    link(V.tensor_scalar(y, y, vec(vecs, "gn_g", p), vec(vecs, "gn_b", p), ALU.mult, ALU.add))
                    link(V.tensor_tensor(y, y, ob[:, p], ALU.add))
                    dve.wait_ge(gate_summed, p + 1)
                    V.tensor_tensor(tiles(y), tiles(y), g_ps[:, :, 0:TN], ALU.mult).then_inc(gated, 1)


def attention(nc, io, sb, pb, sm, consts, x, h, ob, dbg, **_):
    room = x[:].rearrange("p k n -> p (k n)")
    with ExitStack() as at:
        qkv = sb(at, "qkv", [P, 6, T])
        with ExitStack() as ph:
            w = sb(ph, "wqkv", [P, 2, KD, P])
            ps = [pb(ph, f"qkv_ps{s}", [P, NT, 512]) for s in range(2)]
            w0_loaded, w1_loaded, w_free, summed, taken = sm(ph, "wq0_loaded", "wq1_loaded", "wq_free", "qkv_summed",
                                                             "qkv_taken")
            project(nc, io["w_qkv"], 3, w, (w0_loaded, w1_loaded), w_free, summed, taken, ps, h,
                    lambda m: qkv[:, m, :].rearrange("p o (t n) -> p (o t) n", t=NT))
        if dbg.get("stop") == 41:
            return
        kt, vt = qkv[:, 4], qkv[:, 5]
        with ExitStack() as ph:
            k_pad = room[:, 0:WIN + TP]
            bias = sb(ph, "bias", [P, 2, NH * 2 * WIN])
            vtok = sb(ph, "vtok", [P, 1 + NB, P])
            qs = sb(ph, "qs", [P, NP, WIN])
            ks = sb(ph, "ks", [P, 2 * WIN])
            vs = sb(ph, "vs", [P, 2, P])
            s = sb(ph, "s", [P, NH, 2 * WIN])
            prob = sb(ph, "prob", [P, NH, 2 * WIN])
            prob_t = sb(ph, "prob_t", [P, NH, 2, P])
            stat = sb(ph, "att_stat", [P, 6, NH])
            sinks = sb(ph, "sinks", [P, NH])
            o = sb(ph, "o", [P, NP, 2, HD])
            s_ps = pb(ph, "s_ps", [P, NH, 2 * WIN])
            pt_ps = pb(ph, "pt_ps", [P, 4, 2, P])
            o_ps = pb(ph, "o_ps", [P, 2, NP, HD])
            ot_ps = pb(ph, "ot_ps", [P, NP, P])
            (loaded, padded, v_turned, v_taken, staged, scored, biased, chain, max_ready, exped, sink_ready, p_turned,
             p_taken, o_summed, o_ready, o_turned, o_taken, kv_stored) = sm(
                ph, "att_loaded", "padded", "v_turned", "v_taken", "att_staged", "scored", "biased", "att_chain",
                "max_ready", "exped", "sink_ready", "p_turned", "p_taken", "o_summed", "o_ready", "o_turned",
                "o_taken", "kv_stored")
            with nc.Block() as block:
                @block.sync
                def _(sp):
                    sp.dma_start(bias[:], io["att_bias"]).then_inc(loaded, 16)
                    sp.dma_start(sinks[:], io["sinks"]).then_inc(loaded, 16)
                    sp.dma_start(io["k_win_prompt_out"], qkv[:, 4, TP - WIN:TP]).then_inc(kv_stored, 16)
                    sp.dma_start(io["v_win_prompt_out"], qkv[:, 5, TP - WIN:TP]).then_inc(kv_stored, 16)
                    sp.wait_ge(kv_stored, 32)

                def both(eng, body, turns):
                    body(0, 0)
                    with eng.Fori(1, NB) as b:
                        body(b, 1)

                @block.gpsimd
                def _(pool):
                    G = nc.gpsimd
                    G.memset(k_pad[:, 0:WIN], 0.0).then_inc(padded, 1)
                    G.tensor_copy(k_pad[:, WIN:], kt[:, 0:TP]).then_inc(padded, 1)
                    G.memset(vtok[:, 0], 0.0).then_inc(padded, 1)
                    pool.wait_ge(padded, 3)
                    pool.wait_ge(v_taken, 2)

                    def body(b, _):
                        pool.wait_ge(o_summed, b)
                        G.tensor_copy(qs[:], qkv[:, 0:NP, bass.ds(b * WIN, WIN)]).then_inc(staged, 1)
                        G.tensor_copy(ks[:], k_pad[:, bass.ds(b * WIN, 2 * WIN)]).then_inc(staged, 1)
                        G.tensor_copy(vs[:], vtok[:, bass.ds(b, 2), :]).then_inc(staged, 1)
                    both(pool, body, None)

                @block.tensor
                def _(pe):
                    for r in range(2):
                        for b in range(4):
                            mm = nc.tensor.transpose(pt_ps[:, b, 0], vt[:, (4 * r + b) * P:(4 * r + b + 1) * P], col(consts, "ident"))
                        mm.then_inc(v_turned, 1)
                        pe.wait_ge(v_taken, r + 1)

                    def body(b, _):
                        pe.wait_ge(staged, b * 3 + 3)
                        pe.wait_ge(biased, b)
                        for kv, r in enumerate((slice(0, HD), slice(HD, P))):
                            for c in range(NP):
                                mm = nc.tensor.matmul(s_ps[:, 4 * kv + c], qs[r, c], ks[r], start=True, stop=True)
                        mm.then_inc(scored, 1)
                        pe.wait_ge(exped, b * 9 + 8)
                        for half in range(2):
                            if half or not isinstance(b, int):
                                pe.wait_ge(p_taken, b * 2 + half)
                            for c in range(4):
                                for q in range(2):
                                    mm = nc.tensor.transpose(pt_ps[:, c, q], prob[:, 4 * half + c, q * WIN:(q + 1) * WIN],
                                                             col(consts, "ident"))
                            mm.then_inc(p_turned, 1)
                        pe.wait_ge(p_taken, b * 2 + 2)
                        pe.wait_ge(o_ready, b)
                        for kv in range(2):
                            for c in range(NP):
                                for q in range(2):
                                    mm = nc.tensor.matmul(o_ps[:, kv, c], prob_t[:, 4 * kv + c, q],
                                                          vs[:, q, kv * HD:(kv + 1) * HD], start=q == 0, stop=q == 1)
                        mm.then_inc(o_summed, 1)
                        pe.wait_ge(o_ready, b + 1)
                        pe.wait_ge(o_taken, b)
                        for c in range(NP):
                            mm = nc.tensor.transpose(ot_ps[:, c], o[:, c].rearrange("p a b -> p (a b)"), col(consts, "ident"))
                        mm.then_inc(o_turned, 1)
                    both(pe, body, None)

                @block.scalar
                def _(act):
                    S = nc.scalar
                    for r in range(2):
                        act.wait_ge(v_turned, r + 1)
                        S.activation(vtok[:, 1 + 4 * r:5 + 4 * r], pt_ps[:, :, 0], ACT.Copy).then_inc(v_taken, 1)

                    def body(b, _):
                        act.wait_ge(max_ready, b + 1)
                        act.wait_ge(p_turned, b * 2)
                        for n in range(NH):
                            S.activation(prob[:, n], s[:, n], ACT.Exp, bias=stat[:, 1, n:n + 1],
                                         accum_out=stat[:, 2, n:n + 1]).then_inc(exped, 1)
                        S.activation(stat[:, 3], stat[:, 3], ACT.Exp).then_inc(exped, 1)
                        for half in range(2):
                            act.wait_ge(p_turned, b * 2 + half + 1)
                            S.activation(prob_t[:, 4 * half:4 * half + 4], pt_ps[:], ACT.Copy).then_inc(p_taken, 1)
                        act.wait_ge(o_turned, b + 1)
                        S.activation(ob[:, :, bass.ds(b * WIN, WIN)], ot_ps[:], ACT.Copy).then_inc(o_taken, 1)
                    both(act, body, None)

                @block.vector
                def _(dve):
                    link = Chain(dve, chain)
                    V = nc.vector
                    dve.wait_ge(loaded, 32)

                    def body(b, later):
                        dve.wait_ge(scored, b + 1)
                        dve.wait_ge(exped, b * 9)
                        V.scalar_tensor_tensor(s[:].rearrange("p a b -> p (a b)"), s_ps[:].rearrange("p a b -> p (a b)"),
                                               SCALE, bias[:, later], ALU.mult, ALU.add).then_inc(biased, 1)
                        dve.wait_ge(biased, b + 1)
                        link(V.tensor_reduce(stat[:, 0], s[:], AX_X, ALU.max))
                        link(V.tensor_tensor(stat[:, 0], stat[:, 0], sinks[:], ALU.max))
                        V.tensor_tensor(stat[:, 3], sinks[:], stat[:, 0], ALU.subtract).then_inc(chain, 1)
                        link.n += 1
                        link(V.tensor_scalar(stat[:, 1], stat[:, 0], -1.0, None, ALU.mult))
                        dve.sem_inc(max_ready, 1)
                        dve.wait_ge(exped, b * 9 + 9)
                        link(V.tensor_tensor(stat[:, 4], stat[:, 2], stat[:, 3], ALU.add))
                        link(V.reciprocal(stat[:, 5], stat[:, 4]))
                        dve.wait_ge(o_summed, b + 1)
                        dve.wait_ge(o_turned, b)
                        V.tensor_tensor(o[:].rearrange("p c k d -> p k c d"), o_ps[:],
                                        stat[:, 5].rearrange("p (k c) -> p k c", k=2).unsqueeze(3).to_broadcast([P, 2, NP, HD]),
                                        ALU.mult).then_inc(o_ready, 1)
                    body(0, 0)
                    link.n, link.base = 0, link.n
                    with dve.Fori(1, NB) as b:
                        link.enter(b - 1, 6)
                        body(b, 1)
                        link.leave(NB - 1)
        with ExitStack() as ph:
            kc = sb(ph, "kc", [P, NS, WIN])
            vc = sb(ph, "vc", [P, NS, P])
            kw = sb(ph, "kw", [P, NS, WIN])
            prod = sb(ph, "prod", [P, NS, 2, NP])
            s_t = sb(ph, "s_t", [P, NS, 2, NP])
            s = sb(ph, "ss", [64, WIN + 1])
            rel = sb(ph, "rel", [64, WIN + 2])
            stat = sb(ph, "ss_stat", [64, 6])
            pt = sb(ph, "pt", [P, NS, 2, NP])
            row = sb(ph, "self_row", [1, 64])
            ones = sb(ph, "ones_row", [1, P])
            vrow = sb(ph, "vrow", [NS, P])
            part = sb(ph, "self_part", [P, NS, 2, NP])
            st_ps = [pb(ph, f"st_ps{kv}", [P, NS, NP]) for kv in range(2)]
            s_ps = pb(ph, "ss_ps", [64, WIN + 1])
            pt_ps = pb(ph, "pts_ps", [P, 64])
            row_ps = pb(ph, "srow_ps", [1, 64])
            self_ps = pb(ph, "self_ps", [P, NS, 2, NP])
            o_ps = pb(ph, "os_ps", [P, NS, 2, NP])
            v_ps = pb(ph, "vr_ps", [NS, P])
            loaded, pe_step, act_step, dve_step, kv_stored, sink_done, kw_ready, st_copied = sm(ph, "cache_loaded", "samples_pe_step", "samples_act_step",
                                                                "samples_dve_step", "cache_stored", "sample_sinks", "kw_ready", "st_copied")
            flat = "p a b c -> p (a b c)"
            halves = (slice(0, HD), slice(HD, P))
            with nc.Block() as block:
                @block.sync
                def _(sp):
                    sp.dma_start(kc[:], io["k_cache"]).then_inc(loaded, 16)
                    sp.dma_start(vc[:], io["v_cache"]).then_inc(loaded, 16)
                    sp.dma_start(rel[:], io["sample_bias"]).then_inc(loaded, 16)
                    sp.wait_ge(loaded, 48)
                    sp.dma_start(io["v_win_sample_out"][0:WIN - 1], vc[1:WIN]).then_inc(kv_stored, 16)
                    sp.wait_ge(act_step, 3)
                    sp.dma_start(io["v_win_sample_out"][WIN - 1], vrow[:]).then_inc(kv_stored, 16)
                    sp.wait_ge(kw_ready, 2)
                    sp.dma_start(io["k_win_sample_out"], kw[:]).then_inc(kv_stored, 16)
                    sp.wait_ge(kv_stored, 48)

                @block.tensor
                def _(pe):
                    M = nc.tensor.matmul
                    pe.wait_ge(loaded, 48)
                    for kv, r in enumerate(halves):
                        for b in range(NS):
                            mm = M(st_ps[kv][:, b], kc[r, b], qkv[r, 0:NP, TP + b], start=True, stop=True)
                    mm.then_inc(pe_step, 1)
                    nc.tensor.transpose(v_ps[:], vt[:, TP:T], col(consts, "ident")).then_inc(pe_step, 1)
                    pe.wait_ge(dve_step, 4)
                    pe.wait_ge(act_step, 1)
                    nc.tensor.transpose(s_ps[:, 0:WIN], s_t[:].rearrange(flat), col(consts, "ident"))
                    M(s_ps[:, WIN:], prod[:].rearrange(flat), col(consts, "ones"), start=True, stop=True)\
                        .then_inc(pe_step, 1)
                    pe.wait_ge(dve_step, 12)
                    nc.tensor.transpose(pt_ps[:], s[:, 0:WIN], col(consts, "ident")[0:64, 0:64]).then_inc(pe_step, 1)
                    nc.tensor.transpose(row_ps[:], s[:, WIN:], col(consts, "ident")[0:64, 0:64]).then_inc(pe_step, 1)
                    pe.wait_ge(act_step, 6)
                    M(self_ps[:].rearrange(flat), ones[:], row[:], start=True, stop=True)
                    for b in range(NS):
                        mm = M(o_ps[:, b].rearrange("p a b -> p (a b)"), vc[:, b], pt[:, b].rearrange("p a b -> p (a b)"),
                               start=True, stop=True)
                    mm.then_inc(pe_step, 1)

                @block.scalar
                def _(act):
                    S = nc.scalar
                    act.wait_ge(pe_step, 1)
                    for kv in range(2):
                        act.wait_ge(pe_step, 1)
                        S.activation(s_t[:, :, kv], st_ps[kv][:], ACT.Copy).then_inc(st_copied, 1)
                    act.wait_ge(st_copied, 2)
                    act.sem_inc(act_step, 1)
                    act.wait_ge(pe_step, 2)
                    S.activation(vrow[:], v_ps[:], ACT.Copy).then_inc(act_step, 2)
                    act.wait_ge(dve_step, 9)
                    S.activation(stat[:, 3:4], stat[:, 3:4], ACT.Exp).then_inc(sink_done, 1)
                    S.activation(s[:], s[:], ACT.Exp, bias=stat[:, 1:2], accum_out=stat[:, 2:3]).then_inc(act_step, 1)
                    act.wait_ge(pe_step, 4)
                    S.activation(pt[:].rearrange(flat), pt_ps[:], ACT.Copy).then_inc(act_step, 1)
                    act.wait_ge(pe_step, 5)
                    S.activation(row[:], row_ps[:], ACT.Copy).then_inc(act_step, 1)

                @block.vector
                def _(dve):
                    V = nc.vector
                    step = Chain(dve, dve_step)
                    step(V.memset(prod[:], 0.0))
                    step(V.memset(ones[:], 1.0))
                    dve.wait_ge(loaded, 48)
                    V.tensor_copy(kw[:, :, 0:WIN - 1], kc[:, :, 1:WIN]).then_inc(kw_ready, 1)
                    V.tensor_copy(kw[:, :, WIN - 1], kt[:, TP:T]).then_inc(kw_ready, 1)
                    for kv, r in enumerate(halves):
                        step(V.tensor_tensor(prod[r, :, kv], qkv[r, 0:NP, TP:T].rearrange("p c b -> p b c"),
                                             kt[r, TP:T].unsqueeze(2).to_broadcast([HD, NS, NP]), ALU.mult))
                    dve.wait_ge(pe_step, 3)
                    step(V.scalar_tensor_tensor(s[:], s_ps[:], SCALE, rel[:, 0:WIN + 1], ALU.mult, ALU.add))
                    step(V.tensor_reduce(stat[:, 0:1], s[:], AX_X, ALU.max))
                    step(V.tensor_tensor(stat[:, 0:1], stat[:, 0:1], rel[:, WIN + 1:], ALU.max))
                    step(V.tensor_scalar(stat[:, 1:2], stat[:, 0:1], -1.0, None, ALU.mult))
                    step(V.tensor_tensor(stat[:, 3:4], rel[:, WIN + 1:], stat[:, 1:2], ALU.add))
                    dve.wait_ge(act_step, 4)
                    dve.wait_ge(sink_done, 1)
                    step(V.tensor_tensor(stat[:, 4:5], stat[:, 2:3], stat[:, 3:4], ALU.add))
                    step(V.reciprocal(stat[:, 5:6], stat[:, 4:5]))
                    step(V.tensor_scalar(s[:], s[:], stat[:, 5:6], None, ALU.mult))
                    dve.wait_ge(pe_step, 6)
                    step(V.tensor_tensor(part[:], self_ps[:], vt[:, TP:T].unsqueeze(2).unsqueeze(3).to_broadcast([P, NS, 2, NP]),
                                         ALU.mult))
                    for kv, r in enumerate(halves):
                        step(V.tensor_tensor(ob[r, :, TP:T].rearrange("p c b -> p b c"), part[r, :, kv], o_ps[r, :, kv], ALU.add))


def project(nc, w_dram, turns, w, w_loaded, w_free, summed, taken, ps, src, out, kd=KD):
    with nc.Block() as block:
        @block.sync
        def _(sp):
            with sp.Fori(0, turns) as i:
                for s in range(2):
                    sp.wait_ge(w_free, i * 2 + s + 1)
                    sp.dma_start(w[:, s], w_dram[bass.ds(i * 2 + s, 1)].rearrange("o p k n -> p (o k) n"))\
                        .then_inc(w_loaded[s], 16)

        @block.tensor
        def _(pe):
            pe.sem_inc(w_free, 2)
            with pe.Fori(0, turns) as i:
                for s in range(2):
                    pe.wait_ge(w_loaded[s], i * 16 + 16)
                    pe.wait_ge(taken, i * 2)
                    for t in range(NT):
                        for k in range(kd):
                            mm = nc.tensor.matmul(ps[s][:, t, 0:TN], w[:, s, k], src[:, k, t * TN:(t + 1) * TN],
                                                  start=k == 0, stop=k == kd - 1)
                    mm.then_inc(summed, 1)
                    pe.wait_ge(summed, i * 2 + s + 1)
                    pe.sem_inc(w_free, 1)

        @block.scalar
        def _(act):
            with act.Fori(0, turns) as i:
                for s in range(2):
                    act.wait_ge(summed, i * 2 + s + 1)
                    nc.scalar.activation(out(bass.ds(i * 2 + s, 1)), ps[s][:, :, 0:TN], ACT.Copy).then_inc(taken, 1)


def merge(nc, io, sb, pb, sm, h, ya, ob, merged, **_):
    K = (KD, NP, KD, NP)
    FROM = (0, 8, 12, 20)
    with ExitStack() as ph:
        w = sb(ph, "w_merge", [P, 2, 24, P])
        gate = sb(ph, "gate", [P, 2, 2, TN])
        ps = [[pb(ph, f"merge_ps{s}{q}", [P, 512]) for q in range(4)] for s in range(2)]
        w0_loaded, w1_loaded, w_free, summed, gates_ready, used, chain = sm(
            ph, "wm0_loaded", "wm1_loaded", "wm_free", "merge_summed", "gates_ready", "merge_used", "merge_chain")
        w_loaded = (w0_loaded, w1_loaded)
        with nc.Block() as block:
            @block.sync
            def _(sp):
                with sp.Fori(0, KD // 2) as i:
                    for s in range(2):
                        sp.wait_ge(w_free, i * 2 + s + 1)
                        sp.dma_start(w[:, s], io["w_merge"][bass.ds(i * 2 + s, 1)].rearrange("o p k n -> p (o k) n"))\
                            .then_inc(w_loaded[s], 16)

            @block.tensor
            def _(pe):
                pe.sem_inc(w_free, 2)
                with pe.Fori(0, KD // 2) as i:
                    for n in range(2 * NT):
                        s, t = n // NT, n % NT
                        if t == 0:
                            pe.wait_ge(w_loaded[s], i * 16 + 16)
                        if n < 2:
                            pe.wait_ge(used, i * 12)
                        else:
                            pe.wait_ge(used, i * 12 + 2 * (n - 1))
                        for q, src in enumerate((h, ya, h, ob)):
                            for k in range(K[q]):
                                mm = nc.tensor.matmul(ps[n % 2][q][:, 0:TN], w[:, s, FROM[q] + k],
                                                      src[:, k, t * TN:(t + 1) * TN], start=k == 0, stop=k == K[q] - 1)
                        mm.then_inc(summed, 1)
                        if t == NT - 1:
                            pe.wait_ge(summed, i * 6 + n + 1)
                            pe.sem_inc(w_free, 1)

            @block.scalar
            def _(act):
                with act.Fori(0, KD // 2) as i:
                    for n in range(2 * NT):
                        act.wait_ge(summed, i * 6 + n + 1)
                        act.wait_ge(used, i * 12 if n < 2 else i * 12 + 2 * (n - 1))
                        for q in range(2):
                            nc.scalar.activation(gate[:, n % 2, q], ps[n % 2][2 * q][:, 0:TN], ACT.Sigmoid)\
                                .then_inc(gates_ready, 1)

            @block.vector
            def _(dve):
                link = Chain(dve, chain)
                V = nc.vector
                with dve.Fori(0, KD // 2) as i:
                    link.enter(i, 12)
                    for n in range(2 * NT):
                        t = n % NT
                        dve.wait_ge(gates_ready, i * 12 + 2 * n + 2)
                        for q in range(2):
                            V.tensor_tensor(gate[:, n % 2, q], gate[:, n % 2, q], ps[n % 2][2 * q + 1][:, 0:TN], ALU.mult)\
                                .then_inc(chain, 1)
                            link.n += 1
                        dve.wait_ge(chain, link.base + link.n)
                        V.tensor_tensor(merged[:, bass.ds(i * 2 + n // NT, 1), t * TN:(t + 1) * TN],
                                        gate[:, n % 2, 0:1], gate[:, n % 2, 1:2], ALU.add).then_inc(used, 2)
                    link.leave(KD // 2)


def mixer_output(nc, io, sb, pb, sm, mod, x, merged, **_):
    with ExitStack() as ph:
        w = sb(ph, "w_o", [P, 2, KD, P])
        mix = sb(ph, "mix", [P, 2, T])
        ps = [pb(ph, f"o_ps{s}", [P, NT, 512]) for s in range(2)]
        w0_loaded, w1_loaded, w_free, summed, taken, x_loaded, chain = sm(
            ph, "wo0_loaded", "wo1_loaded", "wo_free", "wo_summed", "wo_taken", "x_back", "wo_chain")
        w_loaded = (w0_loaded, w1_loaded)
        with nc.Block() as block:
            @block.sync
            def _(sp):
                sp.dma_start(x[:], io["x_saved"]).then_inc(x_loaded, 16)
                with sp.Fori(0, KD // 2) as i:
                    for s in range(2):
                        sp.wait_ge(w_free, i * 2 + s + 1)
                        sp.dma_start(w[:, s], io["w_o"][bass.ds(i * 2 + s, 1)].rearrange("o p k n -> p (o k) n"))\
                            .then_inc(w_loaded[s], 16)

            @block.tensor
            def _(pe):
                pe.sem_inc(w_free, 2)
                with pe.Fori(0, KD // 2) as i:
                    for s in range(2):
                        pe.wait_ge(w_loaded[s], i * 16 + 16)
                        pe.wait_ge(taken, i * 2)
                        for t in range(NT):
                            for k in range(KD):
                                mm = nc.tensor.matmul(ps[s][:, t, 0:TN], w[:, s, k], merged[:, k, t * TN:(t + 1) * TN],
                                                      start=k == 0, stop=k == KD - 1)
                        mm.then_inc(summed, 1)
                        pe.wait_ge(summed, i * 2 + s + 1)
                        pe.sem_inc(w_free, 1)

            @block.vector
            def _(dve):
                link = Chain(dve, chain)
                V = nc.vector
                dve.wait_ge(x_loaded, 16)
                with dve.Fori(0, KD // 2) as i:
                    link.enter(i, 4)
                    for s in range(2):
                        dve.wait_ge(summed, i * 2 + s + 1)
                        m_ = bass.ds(i * 2 + s, 1)
                        gate = mod[:, bass.ds(i * 2 + (s + GT_M), 1), :].rearrange("p o n -> p (o n)")
                        link(V.tensor_scalar(mix[:, s].rearrange("p (t n) -> p t n", t=NT), ps[s][:, :, 0:TN], gate[:, 0:1],
                                             None, ALU.mult))
                        V.tensor_tensor(mix[:, s, TP:T], ps[s][:, NT - 1, TN - NS:TN], gate[:, 1:], ALU.mult)\
                            .then_inc(taken, 1)
                        dve.wait_ge(taken, i * 2 + s + 1)
                        xm = x[:, m_, :].rearrange("p o n -> p (o n)")
                        link(V.scalar_tensor_tensor(xm, xm, ALPHA, mix[:, s], ALU.mult, ALU.add))
                    link.leave(KD // 2)


TILES = -(-T // P)


def peer_select(nc, io, sb, pb, sm, consts, h, slots, **_):
    with ExitStack() as both:
        query = sb(both, "query", [P, 2 * NH, T])
        with ExitStack() as ph:
            w = sb(ph, "wq", [P, 2, KD, P])
            ps = [pb(ph, f"wq_ps{s}", [P, NT, 512]) for s in range(2)]
            w0_loaded, w1_loaded, w_free, summed, taken = sm(ph, "wpq0_loaded", "wpq1_loaded", "wpq_free", "query_summed",
                                                             "query_taken")
            project(nc, io["peer_wq"], NH, w, (w0_loaded, w1_loaded), w_free, summed, taken, ps, h,
                    lambda m: query[:, m, :].rearrange("p o (t n) -> p (o t) n", t=NT))
        with ExitStack() as ph:
            NJ = 2 * NH
            keys = sb(ph, "keys", [P, 2, NKEY])
            qt = sb(ph, "qt", [P, NJ, P])
            s = sb(ph, "scores", [P, NJ, NKEY])
            s2 = sb(ph, "scores2", [P, NJ, NKEY])
            best = sb(ph, "best", [P, NJ, TOPK])
            best_at = sb(ph, "best_at", [P, NJ, TOPK], U32)
            best_key = sb(ph, "best_key", [P, NJ, TOPK])
            cand, cand2 = (t[:].rearrange("p (h q) n -> p h (q n)", q=2) for t in (s, s2))
            top = sb(ph, "top", [P, NH, TOPK])
            top_at = sb(ph, "top_at", [P, NH, TOPK], U32)
            half_at = sb(ph, "half_at", [P, 2, NH, TOPK], U32)
            half_pos = sb(ph, "half_pos", [P, 2, NH, TOPK])
            pick = [s, s2]
            slot = sb(ph, "slot", [P, 3, NH, TOPK])
            total = sb(ph, "total", [P, 2, NH])
            s_ps = pb(ph, "score_ps", [P, NJ, NKEY])
            t_ps = pb(ph, "slot_ps", [P, 3, P])
            (keys_loaded, staged, scored, copied, cands_ready, chain, gate_ready, slots_ready, turned, slots_taken,
             exp_in, carried) = sm(ph, "keys_loaded", "query_staged", "scored_keys", "scores_copied", "cands_ready", "select_chain",
                          "gate_exp", "slots_ready", "slots_turned", "slots_taken", "exp_in", "select_carried")
            LINKS = 15

            def shape(t):
                return t[:].rearrange("p (h q) n -> p h (q n)", q=2).rearrange("p h (k a) -> p h k a", k=TOPK)

            def steps(eng, body):
                with eng.Fori(0, TILES - 1) as i:
                    body(i, i * P, P)
                body(TILES - 1, (TILES - 1) * P, T - (TILES - 1) * P)

            with nc.Block() as block:
                @block.sync
                def _(sp):
                    sp.dma_start(keys[:], io["keys"]).then_inc(keys_loaded, 16)

                @block.gpsimd
                def _(pool):
                    def body(i, at, n):
                        pool.wait_ge(scored, i)
                        nc.gpsimd.tensor_copy(qt[:, :, 0:n], query[:, :, bass.ds(at, n)]).then_inc(staged, 1)
                    steps(pool, body)

                @block.tensor
                def _(pe):
                    pe.wait_ge(keys_loaded, 16)

                    def body(i, at, n):
                        pe.wait_ge(staged, i + 1)
                        pe.wait_ge(copied, i)
                        for j in range(NJ):
                            mm = nc.tensor.matmul(s_ps[0:n, j], qt[:, j, 0:n], keys[:, j % 2], start=True, stop=True)
                        mm.then_inc(scored, 1)
                        pe.wait_ge(slots_ready, i + 1)
                        pe.wait_ge(slots_taken, i)
                        for q in range(3):
                            mm = nc.tensor.transpose(t_ps[:, q, 0:n], slot[0:n, q].rearrange("p h k -> p (h k)"),
                                                     col(consts, "ident")[0:n, 0:n])
                        mm.then_inc(turned, 1)
                    steps(pe, body)

                @block.scalar
                def _(act):
                    def body(i, at, n):
                        act.wait_ge(scored, i + 1)
                        act.wait_ge(slots_ready, i)
                        nc.scalar.activation(s[0:n], s_ps[0:n], ACT.Copy).then_inc(copied, 1)
                        act.wait_ge(exp_in, i + 1)
                        nc.scalar.activation(slot[0:n, 2], slot[0:n, 2], ACT.Exp).then_inc(gate_ready, 1)
                        act.wait_ge(turned, i + 1)
                        nc.scalar.activation(slots[:, :, bass.ds(at, n)], t_ps[:, :, 0:n], ACT.Copy).then_inc(slots_taken, 1)
                    steps(act, body)

                @block.vector
                def _(dve):
                    link = Chain(dve, chain)
                    V = nc.vector

                    def top16(n, values, rest, out, out_at, count):
                        carry(dve, carried)
                        for j in range(count):
                            ins = V.max(out=out[0:n, j, 0:8], in_=values[0:n, j])
                        link(ins)
                        carry(dve, carried)
                        for j in range(count):
                            ins = V.max_index(out=out_at[0:n, j, 0:8], in_max=out[0:n, j, 0:8], in_values=values[0:n, j])
                            ins = V.match_replace(out=rest[0:n, j], in_to_replace=out[0:n, j, 0:8],
                                                  in_values=values[0:n, j], imm_value=-3e38)
                        link(ins)
                        carry(dve, carried)
                        for j in range(count):
                            ins = V.max(out=out[0:n, j, 8:16], in_=rest[0:n, j])
                        link(ins)
                        carry(dve, carried)
                        for j in range(count):
                            ins = V.max_index(out=out_at[0:n, j, 8:16], in_max=out[0:n, j, 8:16], in_values=rest[0:n, j])
                        link(ins)
                        carry(dve, carried)

                    def body(i, at, n):
                        dve.wait_ge(copied, i + 1)
                        dve.wait_ge(turned, i)
                        top16(n, s, s2, best, best_at, NJ)
                        link(V.tensor_copy(best_key[0:n], best_at[0:n]))
                        b4 = best[0:n].rearrange("p (h q) k -> p h q k", q=2)
                        k4 = best_key[0:n].rearrange("p (h q) k -> p h q k", q=2)
                        wide = [n, NH, TOPK, TOPK]
                        link(V.tensor_tensor(shape(s)[0:n], b4[:, :, 0].unsqueeze(3).to_broadcast(wide),
                                             b4[:, :, 1].unsqueeze(2).to_broadcast(wide), ALU.add))
                        top16(n, cand, cand2, top, top_at, NH)
                        V.tensor_scalar(half_at[0:n, 0], top_at[0:n], 4, None, ALU.logical_shift_right)
                        link(V.tensor_scalar(half_at[0:n, 1], top_at[0:n], 15, None, ALU.bitwise_and))
                        V.tensor_copy(half_pos[0:n], half_at[0:n])
                        link(V.tensor_tensor(slot[0:n, 2], top[0:n], top[0:n, :, 0:1].to_broadcast([n, NH, TOPK]), ALU.subtract))
                        dve.sem_inc(exp_in, 1)
                        iota = col(consts, "iota16")[0:n].unsqueeze(1).unsqueeze(1).to_broadcast(wide)
                        for q in range(2):
                            ins = V.tensor_tensor(shape(pick[q])[0:n], half_pos[0:n, q].unsqueeze(3).to_broadcast(wide), iota,
                                                  ALU.is_equal)
                        link(ins)
                        for q in range(2):
                            ins = V.tensor_tensor(shape(pick[q])[0:n], shape(pick[q])[0:n],
                                                  k4[:, :, q].unsqueeze(2).to_broadcast(wide), ALU.mult)
                        link(ins)
                        dve.wait_ge(gate_ready, i + 1)
                        for q in range(2):
                            V.tensor_reduce(slot[0:n, q], shape(pick[q])[0:n], AX_X, ALU.add)
                        link(V.tensor_reduce(total[0:n, 0], slot[0:n, 2], AX_X, ALU.add))
                        link(V.reciprocal(total[0:n, 1], total[0:n, 0]))
                        V.tensor_tensor(slot[0:n, 2], slot[0:n, 2], total[0:n, 1].unsqueeze(2).to_broadcast([n, NH, TOPK]),
                                        ALU.mult).then_inc(slots_ready, 1)

                    with dve.Fori(0, TILES - 1) as i:
                        link.enter(i, 16)
                        body(i, i * P, P)
                        link.leave(TILES - 1)
                    body(TILES - 1, (TILES - 1) * P, T - (TILES - 1) * P)


TB = 24
NTB = T // TB


def peer_gates(nc, io, sb, pb, sm, consts, slots, **_):
    GR = 4
    NG = TB // GR
    with ExitStack() as ph:
        second = sb(ph, "second", [P, 2, GR, NKEY])
        first = sb(ph, "first", [P, 2, GR, NKEY])
        gates = sb(ph, "gates", [P, 2, NKEY, TB])
        ps = [pb(ph, f"gates_ps{s}", [P, GR, NKEY]) for s in range(2)]
        first_ready, second_ready, summed, taken, stored0, stored1, block_free, block_done = sm(
            ph, "first_ready", "second_ready", "gates_summed", "gates_taken", "gates_stored0", "gates_stored1",
            "gates_free", "gates_done")
        stored = (stored0, stored1)

        def blocks(eng, body):
            with eng.Fori(0, NTB // 2) as i:
                for half in range(2):
                    body(i * 2 + half, half)
            body(NTB - 1, 0)

        with nc.Block() as block:
            @block.vector
            def _(dve):
                V = nc.vector
                iota = col(consts, "iota")

                def body(b, half):
                    for g in range(NG):
                        dve.wait_ge(summed, b * NG + g + 1)
                        for t in range(GR):
                            at = bass.ds(b * TB + (g * GR + t), 1)
                            ins = V.tensor_scalar(first[:, g % 2, t], iota, slots[:, 0, at], slots[:, 2, at],
                                                  ALU.is_equal, ALU.mult)
                        ins.then_inc(first_ready, 1)
                        V.tensor_tensor(second[:, g % 2], iota.unsqueeze(1).to_broadcast([P, GR, NKEY]),
                                        slots[:, 1, bass.ds(b * TB + g * GR, GR)].unsqueeze(2).to_broadcast([P, GR, NKEY]),
                                        ALU.is_equal).then_inc(second_ready, 1)
                blocks(dve, body)

            @block.tensor
            def _(pe):
                pe.sem_inc(summed, 2)

                def body(b, half):
                    for g in range(NG):
                        pe.wait_ge(first_ready, b * NG + g + 1)
                        pe.wait_ge(second_ready, b * NG + g + 1)
                        pe.wait_ge(taken, b * NG + g + 1)
                        for t in range(GR):
                            mm = nc.tensor.matmul(ps[g % 2][:, t], second[:, g % 2, t], first[:, g % 2, t],
                                                  start=True, stop=True)
                        mm.then_inc(summed, 1)
                blocks(pe, body)

            @block.scalar
            def _(act):
                act.sem_inc(taken, 2)

                def body(b, half):
                    act.wait_ge(block_free, b + 1)
                    for g in range(NG):
                        act.wait_ge(summed, b * NG + g + 3)
                        nc.scalar.activation(gates[:, half, :, g * GR:(g + 1) * GR],
                                             ps[g % 2][:].rearrange("p t k -> p k t"), ACT.Copy).then_inc(taken, 1)
                    act.wait_ge(taken, b * NG + (NG + 2))
                    act.sem_inc(block_done, 1)
                blocks(act, body)

            @block.sync
            def _(sp):
                sp.sem_inc(block_free, 2)

                def body(b, half):
                    sp.wait_ge(block_done, b + 1)
                    out = io["gates"][:, bass.ds(b, 1)].rearrange("p o k t -> p (o k t)")
                    sp.dma_start(out, gates[:, half].rearrange("p k t -> p (k t)")).then_inc(stored[half], 16)
                with sp.Fori(0, NTB // 2) as i:
                    for half in range(2):
                        body(i * 2 + half, half)
                    for half in range(2):
                        sp.wait_ge(stored[half], i * 16 + 16)
                        sp.sem_inc(block_free, 1)
                body(NTB - 1, 0)
                sp.wait_ge(stored0, (NTB // 2 + 1) * 16)
                sp.wait_ge(stored1, (NTB // 2) * 16)


def peer_experts(nc, io, sb, pb, sm, h, acc, **_):
    GR = 4
    TURNS = NKEY // GR
    with ExitStack() as ph:
        u = sb(ph, "u", [P, GR, KD, P])
        v = sb(ph, "v", [P, GR, D])
        g = sb(ph, "g", [P, 2, NTB, GR, TB])
        hidden = sb(ph, "hidden", [P, 2, NT, TN])
        weight = sb(ph, "weight", [P, GR, T])
        h_ps = [pb(ph, f"h_ps{s}", [P, NT, 512]) for s in range(2)]
        out_ps = [pb(ph, f"out_ps{s}", [P, 512]) for s in range(2)]
        u_loaded = sm(ph, *(f"u{j}_loaded" for j in range(GR)))
        v_loaded = sm(ph, *(f"v{j}_loaded" for j in range(GR)))
        g_loaded = sm(ph, "g0_loaded", "g1_loaded")
        u_free, v_free, g_free, h_summed, h_ready, weighted, out_summed, out_added, cleared = sm(
            ph, "u_free", "v_free", "g_free", "h_summed", "h_ready", "weighted", "experts_summed", "experts_added", "acc_cleared")
        NO = KD * NT
        with nc.Block() as block:
            def turns(eng, body):
                with eng.Fori(0, TURNS // 2) as i:
                    for half in range(2):
                        body(i * 2 + half, i, half)

            @block.sync
            def _(sp):
                def body(n, i, half):
                    for j in range(GR):
                        sp.wait_ge(u_free, n * GR + j + 1)
                        sp.dma_start(u[:, j], io["u"][bass.ds(n * GR + j, 1)].rearrange("o p k n -> p (o k) n"))\
                            .then_inc(u_loaded[j], 16)
                turns(sp, body)

            @block.gpsimd
            def _(pool):
                def body(n, i, half):
                    pool.wait_ge(g_free, n + 1)
                    pool.dma_start(g[:, half], io["gates"][:, :, bass.ds(n * GR, GR), :]).then_inc(g_loaded[half], 16)
                    pool.wait_ge(v_free, n + 1)
                    for j in range(GR):
                        pool.dma_start(v[:, j], io["v"][bass.ds(n * GR + j, 1)].rearrange("o p n -> p (o n)"))\
                            .then_inc(v_loaded[j], 16)
                turns(pool, body)

            @block.tensor
            def _(pe):
                pe.sem_inc(u_free, GR)
                pe.sem_inc(v_free, 1)

                def body(n, i, half):
                    for j in range(GR):
                        pe.wait_ge(u_loaded[j], n * 16 + 16)
                        pe.wait_ge(h_ready, n * GR + j + 1)
                        for t in range(NT):
                            for k in range(KD):
                                mm = nc.tensor.matmul(h_ps[j % 2][:, t, 0:TN], u[:, j, k], h[:, k, t * TN:(t + 1) * TN],
                                                      start=k == 0, stop=k == KD - 1)
                        mm.then_inc(h_summed, 1)
                        pe.wait_ge(h_summed, n * GR + j + 1)
                        pe.sem_inc(u_free, 1)
                    for j in range(GR):
                        pe.wait_ge(v_loaded[j], n * 16 + 16)
                    pe.wait_ge(weighted, n * GR + GR)
                    for m in range(KD):
                        for t in range(NT):
                            o = m * NT + t
                            pe.wait_ge(out_added, n * NO + o + 1)
                            for j in range(GR):
                                mm = nc.tensor.matmul(out_ps[o % 2][:, 0:TN], v[:, j, m * P:(m + 1) * P],
                                                      weight[:, j, t * TN:(t + 1) * TN], start=j == 0, stop=j == GR - 1)
                            mm.then_inc(out_summed, 1)
                    pe.wait_ge(out_summed, n * NO + NO)
                    pe.sem_inc(v_free, 1)
                turns(pe, body)

            @block.scalar
            def _(act):
                act.sem_inc(h_ready, 2)

                def body(n, i, half):
                    for j in range(GR):
                        act.wait_ge(h_summed, n * GR + j + 1)
                        act.wait_ge(weighted, n * GR + j) if j == 0 else act.wait_ge(weighted, n * GR + j - 1)
                        nc.scalar.activation(hidden[:, j % 2], h_ps[j % 2][:, :, 0:TN], ACT.Gelu).then_inc(h_ready, 1)
                turns(act, body)

            @block.vector
            def _(dve):
                V = nc.vector
                dve.sem_inc(out_added, 2)
                dve.sem_inc(g_free, 2)
                V.memset(acc[:], 0.0).then_inc(cleared, 1)
                dve.wait_ge(cleared, 1)

                def body(n, i, half):
                    dve.wait_ge(g_loaded[half], i * 16 + 16)
                    dve.wait_ge(out_summed, n * NO)
                    for j in range(GR):
                        dve.wait_ge(h_ready, n * GR + j + 3)
                        V.tensor_tensor(weight[:, j].rearrange("p (b t) -> p b t", t=TB),
                                        hidden[:, j % 2].rearrange("p t n -> p (t n)").rearrange("p (b t) -> p b t", t=TB),
                                        g[:, half, :, j], ALU.mult).then_inc(weighted, 1)
                    dve.wait_ge(weighted, n * GR + GR)
                    dve.sem_inc(g_free, 1)
                    dve.wait_ge(out_added, n * NO + 2)
                    for m in range(KD):
                        for t in range(NT):
                            o = m * NT + t
                            dve.wait_ge(out_summed, n * NO + o + 1)
                            a = acc[:, m, t * TN:(t + 1) * TN]
                            V.tensor_tensor(a, a, out_ps[o % 2][:, 0:TN], ALU.add).then_inc(out_added, 1)
                turns(dve, body)


def peer_output(nc, sm, mod, x, acc, **_):
    with ExitStack() as ph:
        chain, = sm(ph, "peer_out_chain")
        with nc.Block() as block:
            @block.vector
            def _(dve):
                V = nc.vector
                for k in range(KD):
                    V.tensor_scalar(acc[:, k, 0:TP], acc[:, k, 0:TP], mod[:, GT_F + k, 0:1], None, ALU.mult).then_inc(chain, 1)
                    V.tensor_tensor(acc[:, k, TP:T], acc[:, k, TP:T], mod[:, GT_F + k, 1:], ALU.mult).then_inc(chain, 1)
                for k in range(KD):
                    dve.wait_ge(chain, 2 * k + 2)
                    V.scalar_tensor_tensor(x[:, k], x[:, k], ALPHA, acc[:, k], ALU.mult, ALU.add).then_inc(chain, 1)


def store_output(nc, io, sm, x, **_):
    with ExitStack() as ph:
        stored, = sm(ph, "y_stored")
        with nc.Block() as block:
            @block.sync
            def _(sp):
                sp.dma_start(io["y_out"], x[:]).then_inc(stored, 16)
                sp.wait_ge(stored, 16)


def _consts():
    import numpy as np
    t = np.zeros((P, NCONST), np.float32)

    def put(name, a):
        at, n = CONST[name]
        t[:, at:at + n] = a
    i64 = np.eye(HD)
    blocks = np.kron(np.eye(2), np.ones((HD, HD)))
    put("ident", np.eye(P))
    put("ident64", np.tile(i64, (2, 1)))
    put("headsum", blocks)
    put("mean", np.full((P, P), 1.0 / D))
    put("headmean", blocks / HD)
    r, c = np.arange(C)[:, None], np.arange(C)[None, :]
    put("upper", np.tile(c > r, (2, 1)))
    put("upper_incl", np.tile(c >= r, (2, 1)))
    put("first_u", np.tile((c == r + 1) & (r % 2 == 0), (2, 1)))
    put("first_l", np.tile((r == c + 1) & (c % 2 == 0), (2, 1)))
    for s in LEVELS:
        put(f"level{s}", np.tile((r // (2 * s) == c // (2 * s)) & (r % (2 * s) < s) & (c % (2 * s) >= s), (2, 1)))
    put("iota", np.tile(np.arange(P), (P, 1)))
    put("iota16", np.tile(np.arange(16), (P, 1)))
    put("ones", 1.0)
    put("ln_eps", LN_EPS)
    put("gn_eps", GN_EPS)
    return t


def _host_inputs(v):
    import numpy as np
    v = {k: np.asarray(a) for k, a in v.items()}

    def fm(a):
        return np.ascontiguousarray(a.T.reshape(-1, P, a.shape[0]).transpose(1, 0, 2))

    def colblocks(a, width=P):
        k, n = a.shape
        return np.ascontiguousarray(a.reshape(k // P, P, n // width, width).transpose(2, 1, 0, 3))

    def percol(a):
        return a.reshape(-1, P).T
    out = {}
    out["consts"] = _consts()
    out["x"] = fm(np.concatenate([v["x_prompt"][0], v["x_sample"][:, 0]]))
    out["c"] = fm(np.concatenate([v["c_prompt"], v["c_sample"]]))
    out["w_ada"] = colblocks(v["w_ada"][0], 512)
    vecs = np.zeros((P, NVEC), np.float32)
    for name, src in (("ln_in_g", "ln_in_g"), ("ln_in_b", "ln_in_b"), ("ln1_g", "ln1_g"), ("ln1_b", "ln1_b"),
                      ("ln2_g", "ln2_g"), ("ln2_b", "ln2_b"), ("b_ada", "b_ada"), ("mu", "mu_shift"),
                      ("w0", "rwkv_w0"), ("a0", "rwkv_a0"), ("k_k", "rwkv_k_k"), ("k_a", "rwkv_k_a"),
                      ("r_k", "rwkv_r_k"), ("gn_g", "rwkv_gn_g"), ("gn_b", "rwkv_gn_b")):
        at, n = VEC[name]
        vecs[:, at:at + n] = percol(v[src].reshape(-1))
    out["vecs"] = vecs
    blocks = colblocks(v["w_in"][0])
    order = [12, 13] + [b for p in range(NP) for b in (p, 4 + p, 8 + p)]
    out["w_in"] = np.ascontiguousarray(blocks[order])
    out["w_lora"] = np.ascontiguousarray(np.concatenate([v["rwkv_w2"][0], v["rwkv_a2"][0]]).reshape(P, NP, P).transpose(1, 0, 2))
    out["shift_before"] = fm(v["state_shift"][0])
    reset = np.ones((P, T), np.float32)
    reset[:, 0:TP:C] = 0.0
    reset[:, TP:] = 0.0
    out["reset"] = reset
    w = v["w_in"][0]
    q_at, k_at, v_at, ga_at, gb_at = 1792, 2304, 2432, 2560, 3584
    heads = [q_at + 64 * hd for c in range(NP) for hd in (c, 4 + c)]
    cols = np.concatenate([np.arange(a, a + 64) for a in heads] + [np.arange(k_at, v_at + 128)])
    out["w_qkv"] = colblocks(w[:, cols])
    out["state_wkv"] = np.ascontiguousarray(
        v["state_wkv"][0].reshape(NS, NP, 2, HD, HD).transpose(2, 4, 1, 0, 3).reshape(P, NP, NS, HD))
    out["g2"] = np.ascontiguousarray(v["rwkv_g2"][0].reshape(P, NP, P))
    pa, pb_ = (colblocks(a) for a in (v["w_pa"][0], v["w_pb"][0].reshape(2, NP, HD, D).transpose(1, 0, 2, 3).reshape(-1, D)))
    out["w_merge"] = np.ascontiguousarray(np.concatenate(
        [colblocks(w[:, ga_at:gb_at]), pa, colblocks(w[:, gb_at:]), pb_], axis=2))
    out["w_o"] = colblocks(v["w_o"][0])
    out["peer_wq"] = colblocks(v["peer_wq"][0])
    out["keys"] = np.ascontiguousarray(v["peer_sub_keys"][0].transpose(2, 0, 1))
    out["u"] = np.ascontiguousarray(v["peer_u"][0].reshape(NKEY, NKEY, KD, P).transpose(0, 3, 2, 1))
    out["v"] = v["peer_v"][0].reshape(NKEY, NKEY, D)
    slopes = 2.0 ** -np.arange(1.0, 9.0)
    rel = WIN + np.arange(WIN)[:, None] - np.arange(2 * WIN)[None, :]
    b = -slopes[None, :, None] * rel[:, None, :]
    b = np.where(((rel >= 0) & (rel <= WIN))[:, None, :], b, NEG)
    first = np.where(np.arange(2 * WIN) < WIN, NEG, b)
    out["att_bias"] = np.stack([first, b], 1).reshape(P, 2, -1).astype(np.float32)
    out["sinks"] = np.ascontiguousarray(np.broadcast_to(v["attn_sinks"][0], (P, NH)))
    out["k_cache"] = np.ascontiguousarray(v["cache_k_win"][0].reshape(NS, WIN, P).transpose(2, 0, 1))
    out["v_cache"] = np.ascontiguousarray(v["cache_v_win"][0].reshape(NS, WIN, P).transpose(1, 0, 2))
    sb_ = np.zeros((64, WIN + 2), np.float32)
    sb_[:, 0:WIN + 1] = np.tile(-slopes[:, None] * (WIN - np.arange(WIN + 1)), (NS, 1))
    sb_[:, WIN + 1] = np.tile(v["attn_sinks"][0], NS)
    out["sample_bias"] = sb_
    return out


_OUTS = {"shift_out": (P, 14, 1 + NS), "wkv_prompt_out": (P, NP, HD),
         "wkv_sample_out": (P, NP, NS, HD), "k_win_prompt_out": (P, WIN), "v_win_prompt_out": (P, WIN),
         "y_out": (P, KD, T), "k_win_sample_out": (P, NS, WIN), "v_win_sample_out": (WIN, NS, P)}
_DEBUG = {}


def kernel(**inputs):
    import numpy as np
    import concourse.bacc as bacc
    from concourse.bass_utils import run_bass_kernel_spmd

    nc = bacc.Bacc("TRN2", target_bir_lowering=False, num_devices=1)
    arrays = _host_inputs(inputs)
    io = {n: nc.dram_tensor("in_" + n, a.shape, mybir.dt.from_np(a.dtype), kind="ExternalInput").ap()
          for n, a in arrays.items()}
    io["x_saved"] = nc.dram_tensor("x_saved", [P, KD, T], F32, kind="Internal").ap()
    io["gates"] = nc.dram_tensor("gates_saved", [P, NTB, NKEY, TB], F32, kind="Internal").ap()
    for n, shape in _OUTS.items():
        io[n] = nc.dram_tensor("out_" + n, shape, F32, kind="ExternalOutput").ap()
    kernel_program(nc, io, _DEBUG)
    r = run_bass_kernel_spmd(nc, [{"in_" + n: a for n, a in arrays.items()}], core_ids=[0]).results[0]
    if _DEBUG:
        return r

    def rows(a):
        return a.transpose(2, 1, 0).reshape(a.shape[2], -1)

    out = {n: np.asarray(r["out_" + n]) for n in _OUTS}
    y = rows(out["y_out"])
    shift = rows(out["shift_out"])
    wkv_p = out["wkv_prompt_out"].reshape(2, HD, NP, HD).transpose(2, 0, 3, 1).reshape(1, 1, 8, HD, HD)
    wkv_s = out["wkv_sample_out"].reshape(2, HD, NP, NS, HD).transpose(3, 2, 0, 4, 1).reshape(1, NS, 8, HD, HD)
    k_p, v_p = (out[f"{n}_win_prompt_out"].T.reshape(1, 1, WIN, 2, HD) for n in "kv")
    k_s = out["k_win_sample_out"].transpose(1, 2, 0).reshape(1, NS, WIN, 2, HD)
    v_s = out["v_win_sample_out"].transpose(1, 0, 2).reshape(1, NS, WIN, 2, HD)
    return (y[:TP][None], y[TP:][:, None], wkv_p, wkv_s, shift[0][None, None], shift[1:][None], k_p, k_s, v_p, v_s)
```

```python
from contextlib import ExitStack

import concourse.bass as bass
from concourse import mybir

F32 = mybir.dt.float32
F32R = mybir.dt.float32r
BF16 = mybir.dt.bfloat16
U32 = mybir.dt.uint32
ALU = mybir.AluOpType
ACT = mybir.ActivationFunctionType
AX_X = mybir.AxisListType.X

P = 128
D = 1024
KD = D // P
TP = 1024
NS = 8
T = TP + NS
NT = 3
TN = T // NT
HD = 64
NP = 4
NMOD = 48
C = 64
NC = TP // C
DECAY = 0.6065306597126334
ALPHA = 2.0 ** 0.25
LN_EPS = 1e-5
GN_EPS = 64e-5
WIN = 128
NB = TP // WIN
NEG = -1e30
NH = 8
TOPK = 16
NKEY = 128
SCALE = HD ** -0.5

CONST = {}
VEC = {}


def _layout(table, names):
    at = 0
    for name, n in names:
        table[name] = (at, n)
        at += n
    return at


LEVELS = (2, 4, 8, 16, 32)
NCONST = _layout(CONST, [("ident", 128), ("ident64", 64), ("headsum", 128), ("mean", 128), ("headmean", 128),
                         ("upper", 64), ("upper_incl", 64), ("first_u", 64), ("first_l", 64)]
                 + [(f"level{s}", 64) for s in LEVELS]
                 + [("iota", 128), ("iota16", 16), ("ones", 1), ("ln_eps", 1), ("gn_eps", 1)])
NVEC = _layout(VEC, [("ln_in_g", 8), ("ln_in_b", 8), ("ln1_g", 8), ("ln1_b", 8), ("ln2_g", 8), ("ln2_b", 8),
                     ("b_ada", NMOD), ("mu", 14), ("w0", 4), ("a0", 4), ("k_k", 4), ("k_a", 4), ("r_k", 4),
                     ("gn_g", 4), ("gn_b", 4)])
SH_M, SC_M, GT_M, SH_F, SC_F, GT_F = (8 * i for i in range(6))


def carry(eng, sem):
    eng.sem_inc(sem, 1)


class Chain:

    def __init__(self, eng, sem):
        self.eng, self.sem, self.base, self.n = eng, sem, 0, 0

    def __call__(self, ins):
        self.n += 1
        ins.then_inc(self.sem, 1)
        self.eng.wait_ge(self.sem, self.base + self.n + 1)

    def enter(self, i, per):
        self.start = self.base + self.n
        self.base, self.n, self.per = i * per + self.start, 0, per

    def leave(self, turns):
        assert self.n == self.per, f"links per turn: {self.n}, not {self.per}"
        self.base, self.n = self.start + turns * self.per, 0


def kernel_program(nc, io):
    with ExitStack() as top:
        def sb(stack, name, shape, dt=F32):
            return stack.enter_context(nc.sbuf_tensor(name, shape, dt))

        def pb(stack, name, shape, dt=F32):
            return stack.enter_context(nc.psum_tensor(name, shape, dt))

        def sm(stack, *names):
            sems = [nc.alloc_semaphore(n) for n in names]
            for s in sems:
                nc.gpsimd.sem_inc(s, 1)
            nc.all_engine_barrier()
            stack.callback(nc.clear_and_free_semaphores, sems)
            return sems

        consts = sb(top, "consts", [P, NCONST])
        vecs = sb(top, "vecs", [P, NVEC])
        mod = sb(top, "mod", [P, NMOD, 1 + NS])
        x = sb(top, "x", [P, KD, T])
        env = dict(nc=nc, io=io, sb=sb, pb=pb, sm=sm, consts=consts, vecs=vecs, mod=mod, x=x)

        modulation_and_input(**env)
        with ExitStack() as mix:
            env["h"] = sb(mix, "h", [P, KD, T])
            layernorm(**env, name="in", modulate=(SC_M, SH_M))
            env["ya"] = sb(mix, "ya", [P, NP, T])
            env["ob"] = sb(mix, "ob", [P, NP, T])
            with ExitStack() as rw:
                for n in ("kt", "kh", "bh", "vt"):
                    env[n] = sb(rw, n, [P, NP, T])
                env["sgd"] = sb(rw, "sgd", [P, T])
                env["pc"] = sb(rw, "pc", [P, NP, NC])
                env["ws"] = sb(rw, "ws", [P, NP, NS])
                rwkv_inputs(**env)
                rwkv_scan(**env)
                rwkv_samples(**env)
            attention(**env)
            env["merged"] = sb(mix, "merged", [P, KD, T])
            merge(**env)
            mixer_output(**env)
        with ExitStack() as pr:
            env["hh"] = sb(pr, "hh", [P, KD, T], F32R)
            env["hl"] = sb(pr, "hl", [P, KD, T], F32R)
            with ExitStack() as q:
                env["h"] = sb(q, "h_peer", [P, KD, T])
                layernorm(**env, name="1", modulate=(SC_F, SH_F))
                split_input(**env)
                peer_queries(**env)
            env["slots"] = sb(pr, "slots", [P, 3, T])
            peer_select(**env)
            peer_gates(**env)
        with ExitStack() as ex:
            acc = sb(ex, "acc", [P, KD, T])
            peer_experts(**env, acc=acc)
            peer_output(**env, acc=acc)
        env["h"] = None
        layernorm(**env, name="2")
        store_output(**env)


def col(consts, name):
    at, n = CONST[name]
    return consts[:, at:at + n]


def vec(vecs, name, k=None):
    at, n = VEC[name]
    return vecs[:, at:at + n] if k is None else vecs[:, at + k:at + k + 1]


def modulation_and_input(nc, io, sb, pb, sm, consts, vecs, mod, x, **_):
    TURNS, SLOTS = 6, 2
    with ExitStack() as ph:
        c = sb(ph, "c", [P, KD, 1 + NS])
        c_sig = sb(ph, "c_sig", [P, KD, 1 + NS])
        slab = sb(ph, "slab", [P, SLOTS, KD, 512])
        row = sb(ph, "row", [1 + NS, SLOTS, 512])
        row_ps = [pb(ph, f"row_ps{s}", [1 + NS, 512]) for s in range(SLOTS)]
        turned_ps = [pb(ph, f"turned_ps{s}", [P, 4, 1 + NS]) for s in range(SLOTS)]
        (c_loaded, small_loaded, x_loaded, slab0_loaded, slab1_loaded, sig_ready, silu_ready, slab_free,
         row_summed, row_free, row_ready, turned, turned_free, chain, carried) = sm(
            ph, "c_loaded", "small_loaded", "x_loaded", "slab0_loaded", "slab1_loaded", "sig_ready", "silu_ready",
            "slab_free", "row_summed", "row_free", "row_ready", "turned", "turned_free", "mod_chain", "mod_carried")
        slab_loaded = (slab0_loaded, slab1_loaded)
        with nc.Block() as block:
            @block.sync
            def _(sp):
                sp.dma_start(c[:], io["c"]).then_inc(c_loaded, 16)
                sp.dma_start(vecs[:], io["vecs"]).then_inc(small_loaded, 16)
                sp.dma_start(consts[:], io["consts"]).then_inc(small_loaded, 16)
                with sp.Fori(0, TURNS) as i:
                    for s in range(SLOTS):
                        sp.wait_ge(slab_free, i * SLOTS + s + 2)
                        sp.dma_start(slab[:, s], io["w_ada"][bass.ds(i * SLOTS + s, 1)].rearrange(
                            "o p k n -> p (o k) n")).then_inc(slab_loaded[s], 16)
                sp.dma_start(x[:], io["x"]).then_inc(x_loaded, 16)
                sp.wait_ge(x_loaded, 17)

            @block.scalar
            def _(act):
                act.wait_ge(c_loaded, 17)
                nc.scalar.activation(c_sig[:], c[:], ACT.Sigmoid).then_inc(sig_ready, 1)
                with act.Fori(0, TURNS) as i:
                    for s in range(SLOTS):
                        act.wait_ge(row_summed, i * SLOTS + s + 2)
                        act.wait_ge(row_free, i * SLOTS + s + 2)
                        nc.scalar.activation(row[:, s], row_ps[s][:], ACT.Copy).then_inc(row_ready, 1)

            @block.vector
            def _(dve):
                link = Chain(dve, chain)
                dve.sem_inc(slab_free, SLOTS)
                dve.sem_inc(row_free, SLOTS)
                dve.wait_ge(sig_ready, 2)
                nc.vector.tensor_tensor(c[:], c[:], c_sig[:], ALU.mult).then_inc(silu_ready, 1)
                dve.wait_ge(small_loaded, 33)
                with dve.Fori(0, TURNS) as i:
                    for s in range(SLOTS):
                        dve.wait_ge(turned, i * SLOTS + s + 2)
                        at = VEC["b_ada"][0]
                        bias = vecs[:, bass.ds(i * (4 * SLOTS) + (4 * s + at), 4)].unsqueeze(2).to_broadcast([P, 4, 1 + NS])
                        nc.vector.tensor_tensor(mod[:, bass.ds(i * (4 * SLOTS) + 4 * s, 4), :], turned_ps[s][:], bias,
                                                ALU.add).then_inc(turned_free, 1)
                dve.wait_ge(turned_free, TURNS * SLOTS + 1)
                for m in (SC_M, SC_F):
                    link(nc.vector.tensor_scalar_add(mod[:, m:m + 8, :], mod[:, m:m + 8, :], 1.0))

            @block.tensor
            def _(pe):
                pe.wait_ge(silu_ready, 2)
                pe.wait_ge(small_loaded, 33)
                with pe.Fori(0, TURNS) as i:
                    for s in range(SLOTS):
                        pe.wait_ge(slab_loaded[s], i * 16 + 17)
                        if s == 0:
                            pe.wait_ge(row_ready, i * SLOTS + 1)
                        for k in range(KD):
                            mm = nc.tensor.matmul(row_ps[s][:], c[:, k], slab[:, s, k], start=k == 0, stop=k == KD - 1)
                        mm.then_inc(row_summed, 1)
                        pe.wait_ge(row_summed, i * SLOTS + s + 2)
                        pe.sem_inc(slab_free, 1)
                    for s in range(SLOTS):
                        pe.wait_ge(row_ready, i * SLOTS + s + 2)
                        pe.wait_ge(turned_free, i * SLOTS + 1)
                        carry(pe, carried)
                        for j in range(4):
                            mm = nc.tensor.transpose(turned_ps[s][:, j], row[:, s, j * P:(j + 1) * P],
                                                     col(consts, "ident")[0:1 + NS, 0:1 + NS])
                        mm.then_inc(turned, 1)
                        pe.wait_ge(turned, i * SLOTS + s + 2)
                        pe.sem_inc(row_free, 1)


def layernorm(nc, io, sb, pb, sm, consts, vecs, mod, x, h, name, modulate=None, **_):
    g, b = f"ln_{name}_g" if name == "in" else f"ln{name}_g", f"ln_{name}_b" if name == "in" else f"ln{name}_b"
    with ExitStack() as ph:
        stat = sb(ph, f"stat_{name}", [P, NT, TN])
        square = sb(ph, f"square_{name}", [P, 2, NT, TN])
        mean_ps = pb(ph, f"mean_ps_{name}", [P, NT, 512])
        var_ps = pb(ph, f"var_ps_{name}", [P, NT, 512])
        mean_summed, mean_ready, centred, squared, var_summed, std_ready, chain = sm(
            ph, *(f"{n}_{name}" for n in ("mean_summed", "mean_ready", "centred", "squared", "var_summed",
                                          "std_ready", "ln_chain")))
        flat = stat[:].rearrange("p t n -> p (t n)")
        with nc.Block() as block:
            @block.tensor
            def _(pe):
                for t in range(NT):
                    for k in range(KD):
                        mm = nc.tensor.matmul(mean_ps[:, t, 0:TN], col(consts, "mean"), x[:, k, t * TN:(t + 1) * TN],
                                              start=k == 0, stop=k == KD - 1)
                mm.then_inc(mean_summed, 1)
                for k in range(KD):
                    pe.wait_ge(squared, k + 2)
                    for t in range(NT):
                        mm = nc.tensor.matmul(var_ps[:, t, 0:TN], col(consts, "mean"), square[:, k % 2, t],
                                              start=k == 0, stop=k == KD - 1)
                    mm.then_inc(var_summed, 1)

            @block.scalar
            def _(act):
                act.wait_ge(mean_summed, 2)
                nc.scalar.activation(stat[:], mean_ps[:, :, 0:TN], ACT.Copy).then_inc(mean_ready, 1)
                for k in range(KD):
                    act.wait_ge(centred, k + 2)
                    if k >= 2:
                        act.wait_ge(var_summed, k)
                    nc.scalar.activation(square[:, k % 2].rearrange("p t n -> p (t n)"), x[:, k], ACT.Square)\
                        .then_inc(squared, 1)
                act.wait_ge(var_summed, KD + 1)
                nc.scalar.activation(stat[:], var_ps[:, :, 0:TN], ACT.Sqrt, bias=col(consts, "ln_eps"))\
                    .then_inc(std_ready, 1)

            @block.vector
            def _(dve):
                link = Chain(dve, chain)
                dve.wait_ge(mean_ready, 2)
                for k in range(KD):
                    nc.vector.tensor_tensor(x[:, k], x[:, k], flat, ALU.subtract).then_inc(centred, 1)
                dve.wait_ge(std_ready, 2)
                link(nc.vector.reciprocal(flat, flat))
                for k in range(KD):
                    link(nc.vector.tensor_tensor(x[:, k], x[:, k], flat, ALU.mult))
                    link(nc.vector.tensor_scalar(x[:, k], x[:, k], vec(vecs, g, k), vec(vecs, b, k), ALU.mult, ALU.add))
                    if modulate:
                        sc, sh = (m + k for m in modulate)
                        nc.vector.tensor_scalar(h[:, k, 0:TP], x[:, k, 0:TP], mod[:, sc, 0:1], mod[:, sh, 0:1],
                                                ALU.mult, ALU.add).then_inc(chain, 1)
                        link.n += 1
                        link(nc.vector.tensor_tensor(h[:, k, TP:T], x[:, k, TP:T], mod[:, sc, 1:], ALU.mult))
                        link(nc.vector.tensor_tensor(h[:, k, TP:T], h[:, k, TP:T], mod[:, sh, 1:], ALU.add))


def rwkv_inputs(nc, io, sb, pb, sm, consts, vecs, mod, x, h, ya, ob, kt, kh, bh, vt, sgd, pc, ws, **_):
    with ExitStack() as ph:
        w = sb(ph, "w", [P, 3, KD, P])
        w_small = sb(ph, "w_small", [P, P])
        before = sb(ph, "before", [P, 14, NS])
        last = sb(ph, "last", [P, 14, 1 + NS])
        reset = sb(ph, "reset", [P, T])
        room = x[:].rearrange("p k n -> p (k n)")
        raw = [room[:, q * (1 + T):(q + 1) * (1 + T)] for q in range(3)]
        lora, tmp, sz = (room[:, 3 * (1 + T) + q * T:3 * (1 + T) + (q + 1) * T] for q in range(3))
        a = raw[0]
        norm, decay = raw[1], raw[2]
        one_minus_ka = sb(ph, "one_minus_ka", [P, NP])
        ps = [pb(ph, f"ps{s}", [P, NT, 512]) for s in range(2)]
        (loaded, w0_loaded, w1_loaded, w2_loaded, ws_loaded, w_free, summed, taken, mixed, tanh_ready, sq_ready,
         rk_ready, norm_taken, scan_ready, exp_ready, exp_used, bonus_taken, turn_done, small_free, chain, out_done, x_saved) = sm(
            ph, "loaded", "w0_loaded", "w1_loaded", "w2_loaded", "ws_loaded", "w_free", "summed", "taken", "mixed",
            "tanh_ready", "sq_ready", "rk_ready", "norm_taken", "scan_ready", "exp_ready", "exp_used", "bonus_taken",
            "turn_done", "small_free", "in_chain", "out_done", "x_saved")
        w_loaded = (w0_loaded, w1_loaded, w2_loaded)

        def tiles(buf):
            return buf[:].rearrange("p (t n) -> p t n", t=NT)

        with nc.Block() as block:
            @block.sync
            def _(sp):
                sp.dma_start(io["x_saved"], x[:]).then_inc(x_saved, 16)
                sp.dma_start(before[:], io["shift_before"]).then_inc(loaded, 16)
                sp.dma_start(reset[:], io["reset"]).then_inc(loaded, 16)
                for q in range(2):
                    sp.dma_start(w[:, q], io["w_in"][q]).then_inc(w_loaded[q], 16)
                with sp.Fori(0, NP) as p:
                    sp.wait_ge(w_free, 2 + p * 5 + 1)
                    for q in range(3):
                        sp.dma_start(w[:, q], io["w_in"][bass.ds(p * 3 + (2 + q), 1)].rearrange(
                            "o p k n -> p (o k) n")).then_inc(w_loaded[q], 16)
                    sp.dma_start(w_small[:], io["w_lora"][bass.ds(p, 1)].rearrange("o p n -> p (o n)"))\
                        .then_inc(ws_loaded, 16)
                sp.wait_ge(turn_done, NP + 1)
                sp.dma_start(io["shift_out"], last[:]).then_inc(out_done, 16)
                sp.wait_ge(out_done, 17)

            @block.tensor
            def _(pe):
                def project(q, s):
                    for t in range(NT):
                        for k in range(KD):
                            mm = nc.tensor.matmul(ps[s][:, t, 0:TN], w[:, q, k], h[:, k, t * TN:(t + 1) * TN],
                                                  start=k == 0, stop=k == KD - 1)
                    return mm

                for q in range(2):
                    pe.wait_ge(w_loaded[q], 17)
                    project(q, q).then_inc(summed, 1)
                    pe.wait_ge(summed, q + 2)
                    pe.sem_inc(w_free, 1)
                pe.wait_ge(tanh_ready, 2)
                with pe.Fori(0, NP) as p:
                    for q in range(3):
                        pe.wait_ge(w_loaded[q], 1 + (p * 16 + (32 if q < 2 else 16)))
                        if q == 0:
                            pe.wait_ge(bonus_taken, p + 1)
                        pe.wait_ge(taken, p * 6 + (2, 2, 3)[q] + 1)
                        project(q, q % 2).then_inc(summed, 1)
                        pe.wait_ge(summed, p * 7 + 3 + q + 1)
                        pe.sem_inc(w_free, 1)
                    pe.wait_ge(ws_loaded, p * 16 + 17)
                    pe.wait_ge(taken, p * 6 + 5)
                    for t in range(NT):
                        mm = nc.tensor.matmul(ps[1][:, t, 0:TN], w_small[0:HD], lora[0:HD, t * TN:(t + 1) * TN],
                                              start=True, stop=True)
                    mm.then_inc(summed, 1)
                    pe.wait_ge(taken, p * 6 + 6)
                    for t in range(NT):
                        mm = nc.tensor.matmul(ps[0][:, t, 0:TN], w_small[HD:P], lora[HD:P, t * TN:(t + 1) * TN],
                                              start=True, stop=True)
                    mm.then_inc(summed, 1)
                    pe.wait_ge(summed, p * 7 + 8)
                    pe.sem_inc(w_free, 2)
                    pe.wait_ge(taken, p * 6 + 7)
                    pe.wait_ge(sq_ready, p + 2)
                    for t in range(NT):
                        mm = nc.tensor.matmul(ps[1][:, t, 0:TN], col(consts, "headsum"), tmp[:, t * TN:(t + 1) * TN],
                                              start=True, stop=True)
                    mm.then_inc(summed, 1)
                    pe.wait_ge(taken, p * 6 + 8)
                    pe.wait_ge(rk_ready, p + 2)
                    for t in range(NT):
                        mm = nc.tensor.matmul(ps[0][:, t, 0:TN], col(consts, "headsum"), tmp[:, t * TN:(t + 1) * TN],
                                              start=True, stop=True)
                    mm.then_inc(summed, 1)

            @block.scalar
            def _(act):
                act.wait_ge(x_saved, 17)
                for q in range(2):
                    act.wait_ge(summed, q + 2)
                    nc.scalar.activation(raw[q][:, 1:].rearrange("p (t n) -> p t n", t=NT), ps[q][:, :, 0:TN], ACT.Copy)\
                        .then_inc(taken, 1)
                act.wait_ge(mixed, 2)
                nc.scalar.activation(lora[0:HD], lora[0:HD], ACT.Tanh).then_inc(tanh_ready, 1)
                act.wait_ge(mixed, 3)
                nc.scalar.activation(sgd[:], sgd[:], ACT.Sigmoid).then_inc(tanh_ready, 1)
                with act.Fori(0, NP) as p:
                    act.wait_ge(turn_done, p + 1)
                    for q in range(3):
                        act.wait_ge(summed, p * 7 + 3 + q + 1)
                        nc.scalar.activation(raw[q][:, 1:].rearrange("p (t n) -> p t n", t=NT), ps[q % 2][:, :, 0:TN],
                                             ACT.Copy).then_inc(taken, 1)
                    act.wait_ge(summed, p * 7 + 7)
                    nc.scalar.activation(tiles(sz), ps[1][:, :, 0:TN], ACT.Sigmoid,
                                         bias=vecs[:, bass.ds(p + VEC["w0"][0], 1)]).then_inc(taken, 1)
                    act.wait_ge(summed, p * 7 + 8)
                    act.wait_ge(mixed, p * 3 + 4)
                    nc.scalar.activation(a[:, 1:].rearrange("p (t n) -> p t n", t=NT), ps[0][:, :, 0:TN], ACT.Sigmoid,
                                         bias=vecs[:, bass.ds(p + VEC["a0"][0], 1)]).then_inc(taken, 1)
                    act.wait_ge(summed, p * 7 + 9)
                    act.wait_ge(mixed, p * 3 + 5)
                    nc.scalar.activation(norm[:, 1:].rearrange("p (t n) -> p t n", t=NT), ps[1][:, :, 0:TN], ACT.Sqrt)\
                        .then_inc(taken, 1)
                    act.wait_ge(mixed, p * 3 + 6)
                    for n, sign in enumerate((-DECAY, DECAY, -DECAY)):
                        act.wait_ge(scan_ready, p * 2 + (1, 1, 2)[n] + 1)
                        if n:
                            act.wait_ge(exp_used, p * 2 + n + 1)
                        nc.scalar.activation(decay[:, 1:], sz[:], ACT.Exp, scale=sign).then_inc(exp_ready, 1)

            @block.gpsimd
            def _(pool):
                pool.wait_ge(x_saved, 17)
                for q in range(3):
                    nc.gpsimd.memset(raw[q][:, 0:1], 0.0).then_inc(small_free, 1)

            @block.vector
            def _(dve):
                link = Chain(dve, chain)
                V = nc.vector

                def mix(q, dst, m):
                    mu = vecs[:, bass.ds(m + VEC["mu"][0], 1)] if not isinstance(m, int) else vec(vecs, "mu", m)
                    m_ = bass.ds(m, 1)
                    V.tensor_tensor(tmp[:, 0:TP], raw[q][:, 0:TP], raw[q][:, 1:1 + TP], ALU.subtract).then_inc(chain, 1)
                    link.n += 1
                    V.tensor_copy(last[:, m_, :], raw[q][:, TP:1 + T].unsqueeze(1)).then_inc(chain, 1)
                    link.n += 1
                    link(V.tensor_tensor(tmp[:, TP:T].unsqueeze(1), before[:, m_, :], raw[q][:, 1 + TP:1 + T].unsqueeze(1),
                                         ALU.subtract))
                    ins = V.scalar_tensor_tensor(dst, tmp[:], mu, raw[q][:, 1:], ALU.mult, ALU.add)
                    ins.then_inc(mixed, 1)

                dve.wait_ge(loaded, 33)
                dve.wait_ge(small_free, 4)
                link(V.tensor_scalar(one_minus_ka[:], vec(vecs, "k_a"), -1.0, 1.0, ALU.mult, ALU.add))
                for q in range(2):
                    dve.wait_ge(taken, q + 2)
                    mix(q, (lora, sgd)[q][:], 12 + q)
                    dve.wait_ge(mixed, q + 2)
                with dve.Fori(0, NP) as p:
                    link.enter(p, 25)

                    def at(t):
                        return t[:, bass.ds(p, 1), :].rearrange("p o n -> p (o n)")

                    def prompt(t):
                        return t[:, bass.ds(p, 1), 0:TP].rearrange("p o n -> p (o n)")

                    def feature(name):
                        return vecs[:, bass.ds(p + VEC[name][0], 1)]

                    for q, dst in enumerate((ya, kh, vt)):
                        dve.wait_ge(taken, p * 6 + 3 + q + 1)
                        mix(q, at(dst), p + 4 * q)
                        dve.wait_ge(mixed, p * 3 + 3 + q + 1)
                    link(V.tensor_scalar(at(kt), at(kh), feature("k_k"), None, ALU.mult))
                    V.tensor_tensor(tmp[:], at(kt), at(kt), ALU.mult).then_inc(sq_ready, 1)
                    dve.wait_ge(taken, p * 6 + 7)
                    link(V.tensor_tensor_scan(decay[:, 1:], reset[:], sz[:], 0.0, ALU.mult, ALU.add))
                    dve.wait_ge(taken, p * 6 + 8)
                    dve.wait_ge(sq_ready, p + 2)
                    link(V.tensor_scalar(at(bh), a[:, 1:], feature("k_a"), one_minus_ka[:, bass.ds(p, 1)], ALU.mult, ALU.add))
                    link(V.tensor_tensor(at(kh), at(kh), at(bh), ALU.mult))
                    dve.wait_ge(taken, p * 6 + 9)
                    ins = V.scalar_tensor_tensor(tmp[:], at(ya), feature("r_k"), at(kh), ALU.mult, ALU.mult)
                    ins.then_inc(rk_ready, 1)
                    link(V.tensor_scalar_max(norm[:, 1:], norm[:, 1:], 1e-12))
                    link(V.reciprocal(norm[:, 1:], norm[:, 1:]))
                    link(V.tensor_tensor(at(kt), at(kt), norm[:, 1:], ALU.mult))
                    link(V.tensor_tensor(at(bh), at(kt), a[:, 1:], ALU.mult))
                    link(V.tensor_tensor(norm[:, 1:], decay[:, 1:], sz[:], ALU.subtract))
                    ins = V.tensor_copy(sz[:], decay[:, 1:])
                    ins.then_inc(scan_ready, 1)
                    dve.wait_ge(summed, p * 7 + 10)
                    ins = V.tensor_tensor(at(ob).rearrange("p (t n) -> p t n", t=NT), ps[0][:, :, 0:TN],
                                          at(vt).rearrange("p (t n) -> p t n", t=NT), ALU.mult)
                    ins.then_inc(bonus_taken, 1)
                    dve.wait_ge(exp_ready, p * 3 + 2)
                    V.tensor_tensor(prompt(ya), prompt(ya), decay[:, 1:1 + TP], ALU.mult).then_inc(chain, 1)
                    link.n += 1
                    V.tensor_copy(ws[:, bass.ds(p, 1), :], decay[:, 1 + TP:1 + T].unsqueeze(1)).then_inc(chain, 1)
                    link.n += 1
                    link(V.tensor_copy(pc[:, bass.ds(p, 1), :], decay[:, 1:1 + TP].rearrange("p (c s) -> p c s", s=C)[:, :, C - 1].unsqueeze(1)))
                    dve.sem_inc(exp_used, 1)
                    dve.wait_ge(exp_ready, p * 3 + 3)
                    V.tensor_tensor(prompt(bh), prompt(bh), decay[:, 1:1 + TP], ALU.mult).then_inc(chain, 1)
                    link.n += 1
                    link(V.tensor_tensor(prompt(kh), prompt(kh), decay[:, 1:1 + TP], ALU.mult))
                    link(V.tensor_copy(sz[:], norm[:, 1:]))
                    dve.sem_inc(scan_ready, 1)
                    dve.sem_inc(exp_used, 1)
                    dve.wait_ge(exp_ready, p * 3 + 4)
                    link(V.tensor_tensor(prompt(kt), prompt(kt), decay[:, 1:1 + TP], ALU.mult))
                    dve.wait_ge(rk_ready, p + 2)
                    dve.wait_ge(bonus_taken, p + 2)
                    dve.sem_inc(turn_done, 1)
                    link.leave(NP)


SIDE = 6 + 2 * KD


class Side:

    def __init__(self, nc, io, sb, pb, sm, ph, h, first, tag):
        self.nc, self.io, self.h, self.first = nc, io, h, first
        self.w = sb(ph, f"w_side_{tag}", [P, KD, P])
        self.out = sb(ph, f"side_{tag}", [P, NT, TN])
        self.ps = pb(ph, f"side_ps_{tag}", [P, 512])
        self.loaded, self.summed, self.taken, self.stored = sm(
            ph, *(f"side_{n}_{tag}" for n in ("loaded", "summed", "taken", "stored")))

    def load(self, sp, n):
        sp.wait_ge(self.summed, n * NT + 1)
        sp.dma_start(self.w[:], self.io["w_side"][bass.ds(n + self.first, 1)].rearrange("o p k n -> p (o k) n"))\
            .then_inc(self.loaded, 16)

    def store(self, sp, n):
        sp.wait_ge(self.taken, n * NT + (NT + 1))
        sp.dma_start(self.io["side_saved"][:, bass.ds(n + self.first, 1), :].rearrange("p o n -> p (o n)"),
                     self.out[:].rearrange("p t n -> p (t n)")).then_inc(self.stored, 16)

    def transfer(self, sp, count):
        sp.sem_inc(self.stored, 16)
        self.load(sp, 0)
        with sp.Fori(0, count - 1) as n:
            self.load(sp, n + 1)
            self.store(sp, n)
        self.store(sp, count - 1)
        sp.wait_ge(self.stored, count * 16 + 17)

    def multiply(self, pe, n, products):
        for at in products:
            t, k = at // KD, at % KD
            if at == 0:
                pe.wait_ge(self.loaded, n * 16 + 17)
            if k == 0:
                pe.wait_ge(self.taken, n * NT + (t + 1))
            mm = self.nc.tensor.matmul(self.ps[:, 0:TN], self.w[:, k], self.h[:, k, t * TN:(t + 1) * TN],
                                       start=k == 0, stop=k == KD - 1)
            if k == KD - 1:
                mm.then_inc(self.summed, 1)

    def take(self, act, n, t):
        act.wait_ge(self.summed, n * NT + (t + 2))
        if t == 0:
            act.wait_ge(self.stored, n * 16 + 17)
        self.nc.scalar.activation(self.out[:, t], self.ps[:, 0:TN], ACT.Copy).then_inc(self.taken, 1)


def rwkv_scan(nc, io, sb, pb, sm, consts, x, h, ya, kt, kh, bh, vt, pc, **_):
    NL = len(LEVELS)
    with ExitStack() as ph:
        room = x[:].rearrange("p k n -> p (k n)")
        at = [0]

        def rows(*shape):
            n = 1
            for v in shape:
                n *= v
            ap = room[:, at[0]:at[0] + n]
            at[0] += n
            if len(shape) == 3:
                ap = ap.rearrange("p (a b c) -> p a b c", a=shape[0], b=shape[1])
            elif len(shape) == 2:
                ap = ap.rearrange("p (a b) -> p a b", a=shape[0])
            return ap

        kr = rows(NP, 2, C)
        bhc, khc, vtc = rows(NP, C), rows(NP, C), rows(NP, C)
        tb_up, tk_up, ab_up, ak_up = rows(NP, C), rows(NP, C), rows(NP, C), rows(NP, C)
        inv = rows(2, NP, C)
        level = rows(NL, NP, C)
        q_sb = rows(NP, C)
        tok = rows(3, NP, C)
        rhs, sa, state = rows(NP, C), rows(NP, C), rows(NP, C)
        b_ps = pb(ph, "b_ps", [P, NP, 2, C])
        k_ps = pb(ph, "k_ps", [P, NP, 2, C])
        t_ps = pb(ph, "t_ps", [P, 2, NP, C])
        tok_ps = pb(ph, "tok_ps", [P, 4, NP, C])
        q_ps = tok_ps[:, 3]
        inv_ps = pb(ph, "inv_ps", [P, 2, NP, C])
        seq_ps = pb(ph, "seq_ps", [P, 2, NP, C])
        (staged, scores, masked, tok_turned, tok_ready, levels_ready, q_summed, q_ready, inv_summed, inv_grown,
         rhs_summed, rhs_ready, sa_summed, sa_ready, out_summed, y_ready, state_ready, chain, pool_chain, saved, carried) = sm(
            ph, "staged", "scores", "masked", "tok_turned", "tok_ready", "levels_ready", "q_summed", "q_ready",
            "inv_summed", "inv_grown", "rhs_summed", "rhs_ready", "sa_summed", "sa_ready", "out_summed", "y_ready",
            "state_ready", "scan_chain", "pool_chain", "state_saved", "scan_carried")
        side = Side(nc, io, sb, pb, sm, ph, h, 0, "scan")
        halves = [slice(0, HD), slice(HD, P)]

        def mask(name, n=NP):
            return col(consts, name).unsqueeze(1).to_broadcast([P, n, C])

        def chunk(t, c):
            return t[:, :, bass.ds(c * C, C)]

        with nc.Block() as block:
            @block.gpsimd
            def _(pool):
                link = Chain(pool, pool_chain)
                with pool.Fori(0, NC) as c:
                    pool.wait_ge(out_summed, c + 1)
                    G = nc.gpsimd
                    G.tensor_copy(kr[:, :, 0], chunk(kt, c)).then_inc(staged, 1)
                    G.tensor_copy(kr[:, :, 1], chunk(ya, c)).then_inc(staged, 1)
                    G.tensor_copy(bhc, chunk(bh, c)).then_inc(staged, 1)
                    G.tensor_copy(khc, chunk(kh, c)).then_inc(staged, 1)
                    G.tensor_copy(vtc, chunk(vt, c)).then_inc(staged, 1)
                    pool.wait_ge(masked, c * 6 + 7)
                    for n, s in enumerate(LEVELS):
                        G.tensor_tensor(level[:, n], tb_up, mask(f"level{s}"), ALU.mult).then_inc(levels_ready, 1)

            @block.tensor
            def _(pe):
                def heads(out, lhsT, rhs, start=True, stop=True):
                    for p in range(NP):
                        for half in halves:
                            mm = nc.tensor.matmul(out(p, half), lhsT(p, half), rhs(p, half), start=start, stop=stop)
                    return mm

                def of(t, *idx):
                    return lambda p, half: t[(half,) + idx + (p,)]

                with pe.Fori(0, NC) as c:
                    side.multiply(pe, c, range(0, 4))
                    pe.wait_ge(staged, c * 5 + 6)
                    pe.wait_ge(state_ready, c + 2)
                    pe.wait_ge(masked, c * 6 + 1)
                    carry(pe, carried)
                    heads(lambda p, r: b_ps[r, p].rearrange("q a b -> q (a b)"), of(bhc), lambda p, r: kr[r, p].rearrange("q a b -> q (a b)"))
                    heads(lambda p, r: k_ps[r, p].rearrange("q a b -> q (a b)"), of(khc), lambda p, r: kr[r, p].rearrange("q a b -> q (a b)"))
                    heads(of(t_ps, 0), lambda p, r: kr[r, p, 0], of(bhc)).then_inc(scores, 1)
                    pe.wait_ge(tok_ready, c + 1)
                    carry(pe, carried)
                    for n, src in enumerate((vtc, bhc, khc)):
                        mm = heads(of(tok_ps, n), of(src), lambda p, r: col(consts, "ident64")[r])
                    mm.then_inc(tok_turned, 1)
                    side.multiply(pe, c, range(4, 8))
                    for n in range(NL):
                        pe.wait_ge(levels_ready, c * NL + n + 2)
                        if n == 0:
                            pe.wait_ge(masked, c * 6 + 7)
                            pe.wait_ge(q_ready, c * NL + 1)
                            pe.wait_ge(tok_ready, c + 2)
                            carry(pe, carried)
                        else:
                            pe.wait_ge(inv_grown, c * NL + n + 1)
                            carry(pe, carried)
                        heads(of(q_ps), of(level, n), of(inv, 0)).then_inc(q_summed, 1)
                        side.multiply(pe, c, range(8 + 2 * n, 9 + 2 * n) if n < NL - 1 else range(16, 18))
                        pe.wait_ge(q_ready, c * NL + n + 2)
                        carry(pe, carried)
                        if n < NL - 1:
                            heads(of(inv_ps, 0), of(inv, 1), of(q_sb))
                        heads(of(inv_ps, 1), of(q_sb), of(inv, 1)).then_inc(inv_summed, 1)
                        side.multiply(pe, c, range(9 + 2 * n, 10 + 2 * n) if n < NL - 1 else range(18, 20))
                    pe.wait_ge(state_ready, c + 2)
                    pe.wait_ge(tok_ready, c + 2)
                    carry(pe, carried)
                    for p in range(NP):
                        for r in halves:
                            nc.tensor.matmul(seq_ps[r, 0, p], kr[r, p, 0], state[r, p], start=True, stop=False)
                            mm = nc.tensor.matmul(seq_ps[r, 0, p], tk_up[r, p], tok[r, 0, p], start=False, stop=True)
                    mm.then_inc(rhs_summed, 1)
                    side.multiply(pe, c, range(20, 22))
                    pe.wait_ge(rhs_ready, c + 2)
                    pe.wait_ge(inv_grown, c * NL + NL + 1)
                    carry(pe, carried)
                    heads(of(seq_ps, 1), of(inv, 1), of(rhs)).then_inc(sa_summed, 1)
                    side.multiply(pe, c, range(22, 24))
                    pe.wait_ge(sa_ready, c + 2)
                    carry(pe, carried)
                    for p in range(NP):
                        for r in halves:
                            nc.tensor.matmul(seq_ps[r, 0, p], state[r, p], kr[r, p, 1], start=True, stop=False)
                            nc.tensor.matmul(seq_ps[r, 0, p], sa[r, p], ab_up[r, p], start=False, stop=False)
                            nc.tensor.matmul(seq_ps[r, 0, p], tok[r, 0, p], ak_up[r, p], start=False, stop=True)
                    for p in range(NP):
                        for r in halves:
                            nc.tensor.matmul(t_ps[r, 1, p], tok[r, 1, p], sa[r, p], start=True, stop=False)
                            mm = nc.tensor.matmul(t_ps[r, 1, p], tok[r, 2, p], tok[r, 0, p], start=False, stop=True)
                    mm.then_inc(out_summed, 1)

            @block.scalar
            def _(act):
                with act.Fori(0, NC) as c:
                    act.wait_ge(tok_turned, c + 2)
                    act.wait_ge(out_summed, c + 1)
                    nc.scalar.activation(tok, tok_ps[:, 0:3], ACT.Copy).then_inc(tok_ready, 1)
                    side.take(act, c, 0)
                    for n in range(NL):
                        act.wait_ge(q_summed, c * NL + n + 2)
                        nc.scalar.activation(q_sb, q_ps, ACT.Copy).then_inc(q_ready, 1)
                        if n == NL - 2:
                            side.take(act, c, 1)
                    act.wait_ge(rhs_summed, c + 2)
                    nc.scalar.activation(rhs, seq_ps[:, 0], ACT.Copy, scale=-1.0).then_inc(rhs_ready, 1)
                    act.wait_ge(sa_summed, c + 2)
                    nc.scalar.activation(sa, seq_ps[:, 1], ACT.Copy).then_inc(sa_ready, 1)
                    side.take(act, c, 2)
                    act.wait_ge(out_summed, c + 2)
                    nc.scalar.activation(chunk(ya, c), seq_ps[:, 0], ACT.Copy).then_inc(y_ready, 1)

            @block.vector
            def _(dve):
                link = Chain(dve, chain)
                V = nc.vector
                V.memset(state, 0.0).then_inc(state_ready, 1)
                with dve.Fori(0, NC) as c:
                    link.enter(c, 3)
                    dve.wait_ge(scores, c + 2)
                    V.tensor_tensor(tb_up, b_ps[:, :, 0], mask("upper"), ALU.mult).then_inc(masked, 1)
                    V.tensor_tensor(ab_up, b_ps[:, :, 1], mask("upper_incl"), ALU.mult).then_inc(masked, 1)
                    V.tensor_tensor(tk_up, k_ps[:, :, 0], mask("upper"), ALU.mult).then_inc(masked, 1)
                    V.tensor_tensor(ak_up, k_ps[:, :, 1], mask("upper_incl"), ALU.mult).then_inc(masked, 1)
                    V.tensor_tensor(inv[:, 0], t_ps[:, 0], mask("first_l"), ALU.mult).then_inc(chain, 1)
                    link.n += 1
                    link(V.tensor_tensor(inv[:, 1], b_ps[:, :, 0], mask("first_u"), ALU.mult))
                    V.scalar_tensor_tensor(inv[:, 0], inv[:, 0], -1.0, mask("ident64"), ALU.mult, ALU.add).then_inc(masked, 1)
                    V.scalar_tensor_tensor(inv[:, 1], inv[:, 1], -1.0, mask("ident64"), ALU.mult, ALU.add).then_inc(masked, 1)
                    for n in range(NL):
                        dve.wait_ge(inv_summed, c * NL + n + 2)
                        if n == 0:
                            dve.wait_ge(masked, c * 6 + 7)
                        else:
                            dve.wait_ge(inv_grown, c * NL + n + 1)
                        if n < NL - 1:
                            V.tensor_tensor(inv, inv, inv_ps[:], ALU.subtract).then_inc(inv_grown, 1)
                        else:
                            V.tensor_tensor(inv[:, 1], inv[:, 1], inv_ps[:, 1], ALU.subtract).then_inc(inv_grown, 1)
                    dve.wait_ge(out_summed, c + 2)
                    link(V.tensor_tensor(state, state, t_ps[:, 1], ALU.add))
                    through = pc[:, :, bass.ds(c, 1)].to_broadcast([P, NP, C])
                    V.tensor_tensor(state, state, through, ALU.mult).then_inc(state_ready, 1)
                    dve.wait_ge(state_ready, c + 3)
                    link.leave(NC)

            @block.sync
            def _(sp):
                side.transfer(sp, NC)
                sp.wait_ge(state_ready, NC + 2)
                sp.dma_start(io["wkv_prompt_out"], state).then_inc(saved, 16)
                sp.wait_ge(saved, 17)


def rwkv_samples(nc, io, sb, pb, sm, consts, vecs, x, ya, ob, kt, kh, bh, vt, sgd, ws, **_):
    with ExitStack() as ph:
        room = x[:].rearrange("p k n -> p (k n)")
        n_state = NP * NS * HD
        state, part, part2 = (room[:, q * n_state:(q + 1) * n_state].rearrange("p (a b c) -> p a b c", a=NP, b=NS)
                              for q in range(3))
        sum_ps = pb(ph, "sum_ps", [P, NP, NS, HD])
        spread_ps = pb(ph, "spread_ps", [P, NP, NS, HD])
        loaded, part_ready, summed, used, state_ready, chain, stored = sm(
            ph, "state_loaded", "part_ready", "part_summed", "sums_used", "new_state", "samples_chain", "new_state_stored")

        def spread(t):
            return t[:, :, TP:T].unsqueeze(3).to_broadcast([P, NP, NS, HD])

        unit = col(consts, "ident64").unsqueeze(1).unsqueeze(1).to_broadcast([P, NP, NS, HD])
        with nc.Block() as block:
            @block.sync
            def _(sp):
                sp.dma_start(state, io["state_wkv"]).then_inc(loaded, 16)
                sp.wait_ge(state_ready, 2)
                sp.dma_start(io["wkv_sample_out"], state).then_inc(stored, 16)
                sp.wait_ge(stored, 17)

            @block.tensor
            def _(pe):
                for n, (src, out) in enumerate(((part, sum_ps), (part2, spread_ps), (part, sum_ps))):
                    pe.wait_ge(part_ready, n + 2)
                    for p in range(NP):
                        mm = nc.tensor.matmul(out[:, p].rearrange("p a b -> p (a b)"), col(consts, "headsum"),
                                              src[:, p].rearrange("p a b -> p (a b)"), start=True, stop=True)
                    mm.then_inc(summed, 1)

            @block.vector
            def _(dve):
                link = Chain(dve, chain)
                V = nc.vector
                dve.wait_ge(loaded, 17)
                V.tensor_tensor(part, state, spread(kt), ALU.mult).then_inc(part_ready, 1)
                V.tensor_tensor(part2, unit, spread(vt), ALU.mult).then_inc(part_ready, 1)
                decay = ws[:].unsqueeze(3).to_broadcast([P, NP, NS, HD])
                link(V.tensor_tensor(state, state, decay, ALU.mult))
                dve.wait_ge(summed, 2)
                link(V.tensor_tensor(part, sum_ps[:], spread(bh), ALU.mult))
                link(V.tensor_tensor(state, state, part, ALU.subtract))
                dve.wait_ge(summed, 3)
                link(V.tensor_tensor(part2, spread_ps[:], spread(kh), ALU.mult))
                link(V.tensor_tensor(state, state, part2, ALU.add))
                dve.sem_inc(state_ready, 1)
                V.tensor_tensor(part, state, spread(ya), ALU.mult).then_inc(part_ready, 1)
                dve.wait_ge(summed, 4)
                link(V.tensor_tensor(part2, sum_ps[:], unit, ALU.mult))
                V.tensor_reduce(ya[:, :, TP:T], part2, AX_X, ALU.add).then_inc(used, 1)
    with ExitStack() as ph:
        square = [sb(ph, f"gn_sq{q}", [P, NT, TN]) for q in range(2)]
        g2 = sb(ph, "g2_gn", [P, NP, P])
        m_ps = pb(ph, "m_ps", [P, NT, 512])
        g_ps = pb(ph, "g_ps", [P, NT, 512])
        (g2_loaded, mean_summed, centred, squared, var_summed, std_ready, std_used, gate_summed, gated, chain) = sm(
            ph, "g2_loaded", "gn_mean_summed", "gn_centred", "gn_squared", "gn_var_summed", "gn_std_ready",
            "gn_std_used", "gate_summed", "gated", "gn_chain")

        def tiles(t):
            return t.rearrange("p (t n) -> p t n", t=NT)

        with nc.Block() as block:
            @block.sync
            def _(sp):
                sp.dma_start(g2[:], io["g2"]).then_inc(g2_loaded, 16)

            @block.tensor
            def _(pe):
                pe.wait_ge(g2_loaded, 17)
                for p in range(NP):
                    for t in range(NT):
                        mm = nc.tensor.matmul(m_ps[:, t, 0:TN], col(consts, "headmean"), ya[:, p, t * TN:(t + 1) * TN],
                                              start=True, stop=True)
                    mm.then_inc(mean_summed, 1)
                    if p:
                        pe.wait_ge(gated, p + 1)
                    for t in range(NT):
                        mm = nc.tensor.matmul(g_ps[:, t, 0:TN], g2[:, p], sgd[:, t * TN:(t + 1) * TN],
                                              start=True, stop=True)
                    mm.then_inc(gate_summed, 1)
                    pe.wait_ge(squared, p + 2)
                    for t in range(NT):
                        mm = nc.tensor.matmul(m_ps[:, t, 0:TN], col(consts, "headmean"), square[0][:, t],
                                              start=True, stop=True)
                    mm.then_inc(var_summed, 1)
                    pe.wait_ge(std_ready, p + 2)

            @block.scalar
            def _(act):
                for p in range(NP):
                    act.wait_ge(centred, p + 2)
                    if p:
                        act.wait_ge(var_summed, p + 1)
                    nc.scalar.activation(square[0][:], tiles(ya[:, p]), ACT.Square).then_inc(squared, 1)
                    act.wait_ge(var_summed, p + 2)
                    if p:
                        act.wait_ge(std_used, p + 1)
                    nc.scalar.activation(square[1][:], m_ps[:, :, 0:TN], ACT.Sqrt, bias=col(consts, "gn_eps"))\
                        .then_inc(std_ready, 1)

            @block.vector
            def _(dve):
                link = Chain(dve, chain)
                V = nc.vector
                for p in range(NP):
                    y = ya[:, p]
                    dve.wait_ge(mean_summed, p + 2)
                    V.tensor_tensor(tiles(y), tiles(y), m_ps[:, :, 0:TN], ALU.subtract).then_inc(centred, 1)
                    dve.wait_ge(std_ready, p + 2)
                    link(V.reciprocal(square[1][:], square[1][:]))
                    V.tensor_tensor(tiles(y), tiles(y), square[1][:], ALU.mult).then_inc(std_used, 1)
                    dve.wait_ge(std_used, p + 2)
                    link(V.tensor_scalar(y, y, vec(vecs, "gn_g", p), vec(vecs, "gn_b", p), ALU.mult, ALU.add))
                    link(V.tensor_tensor(y, y, ob[:, p], ALU.add))
                    dve.wait_ge(gate_summed, p + 2)
                    V.tensor_tensor(tiles(y), tiles(y), g_ps[:, :, 0:TN], ALU.mult).then_inc(gated, 1)


def attention(nc, io, sb, pb, sm, consts, x, h, ob, **_):
    room = x[:].rearrange("p k n -> p (k n)")
    with ExitStack() as at:
        qkv = sb(at, "qkv", [P, 6, T])
        kt, vt = qkv[:, 4], qkv[:, 5]
        with ExitStack() as ph:
            k_pad = room[:, 0:WIN + TP]
            bias = sb(ph, "bias", [P, 2, NH * 2 * WIN])
            vtok = sb(ph, "vtok", [P, 1 + NB, P])
            qs = sb(ph, "qs", [P, NP, WIN])
            ks = sb(ph, "ks", [P, 2 * WIN])
            vs = sb(ph, "vs", [P, 2, P])
            s = sb(ph, "s", [P, NH, 2 * WIN])
            prob = sb(ph, "prob", [P, NH, 2 * WIN])
            prob_t = sb(ph, "prob_t", [P, NH, 2, P])
            stat = sb(ph, "att_stat", [P, 6, NH])
            sinks = sb(ph, "sinks", [P, NH])
            o = sb(ph, "o", [P, NP, 2, HD])
            s_ps = pb(ph, "s_ps", [P, NH, 2 * WIN])
            pt_ps = pb(ph, "pt_ps", [P, 4, 2, P])
            o_ps = pb(ph, "o_ps", [P, 2, NP, HD])
            ot_ps = o_ps[:].rearrange("p k c d -> p (k c d)").rearrange("p (c n) -> p c n", c=NP)
            (loaded, padded, v_turned, v_taken, staged, scored, biased, chain, max_ready, exped, sink_ready, p_turned,
             p_taken, o_summed, o_ready, o_turned, o_taken, kv_stored) = sm(
                ph, "att_loaded", "padded", "v_turned", "v_taken", "att_staged", "scored", "biased", "att_chain",
                "max_ready", "exped", "sink_ready", "p_turned", "p_taken", "o_summed", "o_ready", "o_turned",
                "o_taken", "kv_stored")
            qkv_loaded, = sm(ph, "qkv_loaded")
            side = Side(nc, io, sb, pb, sm, ph, h, NC, "att")
            LEFT = SIDE - NC
            with nc.Block() as block:
                @block.sync
                def _(sp):
                    sp.dma_start(qkv[:, NP:], io["side_saved"][:, NP:6]).then_inc(qkv_loaded, 16)
                    sp.dma_start(qkv[:, 0:NP], io["side_saved"][:, 0:NP]).then_inc(qkv_loaded, 16)
                    sp.dma_start(bias[:], io["att_bias"]).then_inc(loaded, 16)
                    sp.dma_start(sinks[:], io["sinks"]).then_inc(loaded, 16)
                    sp.wait_ge(qkv_loaded, 33)
                    sp.dma_start(io["k_win_prompt_out"], qkv[:, 4, TP - WIN:TP]).then_inc(kv_stored, 16)
                    sp.dma_start(io["v_win_prompt_out"], qkv[:, 5, TP - WIN:TP]).then_inc(kv_stored, 16)
                    side.transfer(sp, LEFT)
                    sp.wait_ge(kv_stored, 33)

                def both(eng, body):
                    body(0, False)
                    with eng.Fori(1, 1 + LEFT) as b:
                        body(b, True)
                    with eng.Fori(1 + LEFT, NB) as b:
                        body(b, False)

                @block.gpsimd
                def _(pool):
                    G = nc.gpsimd
                    pool.wait_ge(qkv_loaded, 33)
                    G.memset(k_pad[:, 0:WIN], 0.0).then_inc(padded, 1)
                    G.tensor_copy(k_pad[:, WIN:], kt[:, 0:TP]).then_inc(padded, 1)
                    G.memset(vtok[:, 0], 0.0).then_inc(padded, 1)
                    pool.wait_ge(padded, 4)
                    pool.wait_ge(v_taken, 3)

                    def body(b, _):
                        pool.wait_ge(o_summed, b + 1)
                        G.tensor_copy(qs[:], qkv[:, 0:NP, bass.ds(b * WIN, WIN)]).then_inc(staged, 1)
                        G.tensor_copy(ks[:], k_pad[:, bass.ds(b * WIN, 2 * WIN)]).then_inc(staged, 1)
                        G.tensor_copy(vs[:], vtok[:, bass.ds(b, 2), :]).then_inc(staged, 1)
                    both(pool, body)

                @block.tensor
                def _(pe):
                    pe.wait_ge(qkv_loaded, 33)
                    for r in range(2):
                        for b in range(4):
                            mm = nc.tensor.transpose(pt_ps[:, b, 0], vt[:, (4 * r + b) * P:(4 * r + b + 1) * P], col(consts, "ident"))
                        mm.then_inc(v_turned, 1)
                        pe.wait_ge(v_taken, r + 2)

                    def body(b, beside):
                        def fill(*products):
                            if beside:
                                side.multiply(pe, b - 1, range(*products))

                        fill(0, 6)
                        pe.wait_ge(staged, b * 3 + 4)
                        pe.wait_ge(biased, b + 1)
                        for kv, r in enumerate((slice(0, HD), slice(HD, P))):
                            for c in range(NP):
                                mm = nc.tensor.matmul(s_ps[:, 4 * kv + c], qs[r, c], ks[r], start=True, stop=True)
                        mm.then_inc(scored, 1)
                        fill(6, 16)
                        pe.wait_ge(exped, b * 9 + 9)
                        for half in range(2):
                            if half or not isinstance(b, int):
                                pe.wait_ge(p_taken, b * 2 + half + 1)
                            for c in range(4):
                                for q in range(2):
                                    mm = nc.tensor.transpose(pt_ps[:, c, q], prob[:, 4 * half + c, q * WIN:(q + 1) * WIN],
                                                             col(consts, "ident"))
                            mm.then_inc(p_turned, 1)
                            fill(16 + 2 * half, 18 + 2 * half)
                        pe.wait_ge(p_taken, b * 2 + 3)
                        pe.wait_ge(o_taken, b + 1)
                        for kv in range(2):
                            for c in range(NP):
                                for q in range(2):
                                    mm = nc.tensor.matmul(o_ps[:, kv, c], prob_t[:, 4 * kv + c, q],
                                                          vs[:, q, kv * HD:(kv + 1) * HD], start=q == 0, stop=q == 1)
                        mm.then_inc(o_summed, 1)
                        fill(20, 22)
                        pe.wait_ge(o_ready, b + 2)
                        for c in range(NP):
                            mm = nc.tensor.transpose(ot_ps[:, c], o[:, c].rearrange("p a b -> p (a b)"), col(consts, "ident"))
                        mm.then_inc(o_turned, 1)
                        fill(22, 24)
                    both(pe, body)

                @block.scalar
                def _(act):
                    S = nc.scalar
                    for r in range(2):
                        act.wait_ge(v_turned, r + 2)
                        S.activation(vtok[:, 1 + 4 * r:5 + 4 * r], pt_ps[:, :, 0], ACT.Copy).then_inc(v_taken, 1)

                    def body(b, beside):
                        for t in range(2 if beside else 0):
                            side.take(act, b - 1, t)
                        act.wait_ge(max_ready, b + 2)
                        act.wait_ge(p_turned, b * 2 + 1)
                        for n in range(NH):
                            S.activation(prob[:, n], s[:, n], ACT.Exp, bias=stat[:, 1, n:n + 1],
                                         accum_out=stat[:, 2, n:n + 1]).then_inc(exped, 1)
                        S.activation(stat[:, 3], stat[:, 3], ACT.Exp).then_inc(exped, 1)
                        for half in range(2):
                            act.wait_ge(p_turned, b * 2 + half + 2)
                            S.activation(prob_t[:, 4 * half:4 * half + 4], pt_ps[:], ACT.Copy).then_inc(p_taken, 1)
                        act.wait_ge(o_turned, b + 2)
                        S.activation(ob[:, :, bass.ds(b * WIN, WIN)], ot_ps, ACT.Copy).then_inc(o_taken, 1)
                        if beside:
                            side.take(act, b - 1, 2)
                    both(act, body)

                @block.vector
                def _(dve):
                    link = Chain(dve, chain)
                    V = nc.vector
                    dve.wait_ge(loaded, 33)

                    def body(b, later):
                        dve.wait_ge(scored, b + 2)
                        dve.wait_ge(exped, b * 9 + 1)
                        V.scalar_tensor_tensor(s[:].rearrange("p a b -> p (a b)"), s_ps[:].rearrange("p a b -> p (a b)"),
                                               SCALE, bias[:, later], ALU.mult, ALU.add).then_inc(biased, 1)
                        dve.wait_ge(biased, b + 2)
                        link(V.tensor_reduce(stat[:, 0], s[:], AX_X, ALU.max))
                        link(V.tensor_tensor(stat[:, 0], stat[:, 0], sinks[:], ALU.max))
                        V.tensor_tensor(stat[:, 3], sinks[:], stat[:, 0], ALU.subtract).then_inc(chain, 1)
                        link.n += 1
                        link(V.tensor_scalar(stat[:, 1], stat[:, 0], -1.0, None, ALU.mult))
                        dve.sem_inc(max_ready, 1)
                        dve.wait_ge(exped, b * 9 + 10)
                        link(V.tensor_tensor(stat[:, 4], stat[:, 2], stat[:, 3], ALU.add))
                        link(V.reciprocal(stat[:, 5], stat[:, 4]))
                        dve.wait_ge(o_summed, b + 2)
                        dve.wait_ge(o_turned, b + 1)
                        V.tensor_tensor(o[:].rearrange("p c k d -> p k c d"), o_ps[:],
                                        stat[:, 5].rearrange("p (k c) -> p k c", k=2).unsqueeze(3).to_broadcast([P, 2, NP, HD]),
                                        ALU.mult).then_inc(o_ready, 1)
                    body(0, 0)
                    link.n, link.base = 0, link.n
                    with dve.Fori(1, NB) as b:
                        link.enter(b - 1, 6)
                        body(b, 1)
                        link.leave(NB - 1)
        with ExitStack() as ph:
            kc = sb(ph, "kc", [P, NS, WIN])
            vc = sb(ph, "vc", [P, NS, P])
            kw = sb(ph, "kw", [P, NS, WIN])
            prod = sb(ph, "prod", [P, NS, 2, NP])
            s_t = sb(ph, "s_t", [P, NS, 2, NP])
            s = sb(ph, "ss", [64, WIN + 1])
            rel = sb(ph, "rel", [64, WIN + 2])
            stat = sb(ph, "ss_stat", [64, 6])
            pt = sb(ph, "pt", [P, NS, 2, NP])
            row = sb(ph, "self_row", [1, 64])
            ones = sb(ph, "ones_row", [1, P])
            vrow = sb(ph, "vrow", [NS, P])
            part = sb(ph, "self_part", [P, NS, 2, NP])
            st_ps = [pb(ph, f"st_ps{kv}", [P, NS, NP]) for kv in range(2)]
            s_ps = pb(ph, "ss_ps", [64, WIN + 1])
            pt_ps = pb(ph, "pts_ps", [P, 64])
            row_ps = pb(ph, "srow_ps", [1, 64])
            self_ps = pb(ph, "self_ps", [P, NS, 2, NP])
            o_ps = pb(ph, "os_ps", [P, NS, 2, NP])
            v_ps = pb(ph, "vr_ps", [NS, P])
            loaded, pe_step, act_step, dve_step, kv_stored, sink_done, kw_ready, st_copied = sm(ph, "cache_loaded", "samples_pe_step", "samples_act_step",
                                                                "samples_dve_step", "cache_stored", "sample_sinks", "kw_ready", "st_copied")
            flat = "p a b c -> p (a b c)"
            halves = (slice(0, HD), slice(HD, P))
            with nc.Block() as block:
                @block.sync
                def _(sp):
                    sp.dma_start(kc[:], io["k_cache"]).then_inc(loaded, 16)
                    sp.dma_start(vc[:], io["v_cache"]).then_inc(loaded, 16)
                    sp.dma_start(rel[:], io["sample_bias"]).then_inc(loaded, 16)
                    sp.wait_ge(loaded, 49)
                    sp.dma_start(io["v_win_sample_out"][0:WIN - 1], vc[1:WIN]).then_inc(kv_stored, 16)
                    sp.wait_ge(act_step, 4)
                    sp.dma_start(io["v_win_sample_out"][WIN - 1], vrow[:]).then_inc(kv_stored, 16)
                    sp.wait_ge(kw_ready, 3)
                    sp.dma_start(io["k_win_sample_out"], kw[:]).then_inc(kv_stored, 16)
                    sp.wait_ge(kv_stored, 49)

                @block.tensor
                def _(pe):
                    M = nc.tensor.matmul
                    pe.wait_ge(loaded, 49)
                    for kv, r in enumerate(halves):
                        for b in range(NS):
                            mm = M(st_ps[kv][:, b], kc[r, b], qkv[r, 0:NP, TP + b], start=True, stop=True)
                    mm.then_inc(pe_step, 1)
                    nc.tensor.transpose(v_ps[:], vt[:, TP:T], col(consts, "ident")).then_inc(pe_step, 1)
                    pe.wait_ge(dve_step, 5)
                    pe.wait_ge(act_step, 2)
                    nc.tensor.transpose(s_ps[:, 0:WIN], s_t[:].rearrange(flat), col(consts, "ident"))
                    M(s_ps[:, WIN:], prod[:].rearrange(flat), col(consts, "ones"), start=True, stop=True)\
                        .then_inc(pe_step, 1)
                    pe.wait_ge(dve_step, 13)
                    nc.tensor.transpose(pt_ps[:], s[:, 0:WIN], col(consts, "ident")[0:64, 0:64]).then_inc(pe_step, 1)
                    nc.tensor.transpose(row_ps[:], s[:, WIN:], col(consts, "ident")[0:64, 0:64]).then_inc(pe_step, 1)
                    pe.wait_ge(act_step, 7)
                    M(self_ps[:].rearrange(flat), ones[:], row[:], start=True, stop=True)
                    for b in range(NS):
                        mm = M(o_ps[:, b].rearrange("p a b -> p (a b)"), vc[:, b], pt[:, b].rearrange("p a b -> p (a b)"),
                               start=True, stop=True)
                    mm.then_inc(pe_step, 1)

                @block.scalar
                def _(act):
                    S = nc.scalar
                    act.wait_ge(pe_step, 2)
                    for kv in range(2):
                        act.wait_ge(pe_step, 2)
                        S.activation(s_t[:, :, kv], st_ps[kv][:], ACT.Copy).then_inc(st_copied, 1)
                    act.wait_ge(st_copied, 3)
                    act.sem_inc(act_step, 1)
                    act.wait_ge(pe_step, 3)
                    S.activation(vrow[:], v_ps[:], ACT.Copy).then_inc(act_step, 2)
                    act.wait_ge(dve_step, 10)
                    S.activation(stat[:, 3:4], stat[:, 3:4], ACT.Exp).then_inc(sink_done, 1)
                    S.activation(s[:], s[:], ACT.Exp, bias=stat[:, 1:2], accum_out=stat[:, 2:3]).then_inc(act_step, 1)
                    act.wait_ge(pe_step, 5)
                    S.activation(pt[:].rearrange(flat), pt_ps[:], ACT.Copy).then_inc(act_step, 1)
                    act.wait_ge(pe_step, 6)
                    S.activation(row[:], row_ps[:], ACT.Copy).then_inc(act_step, 1)

                @block.vector
                def _(dve):
                    V = nc.vector
                    step = Chain(dve, dve_step)
                    step(V.memset(prod[:], 0.0))
                    step(V.memset(ones[:], 1.0))
                    dve.wait_ge(loaded, 49)
                    V.tensor_copy(kw[:, :, 0:WIN - 1], kc[:, :, 1:WIN]).then_inc(kw_ready, 1)
                    V.tensor_copy(kw[:, :, WIN - 1], kt[:, TP:T]).then_inc(kw_ready, 1)
                    for kv, r in enumerate(halves):
                        step(V.tensor_tensor(prod[r, :, kv], qkv[r, 0:NP, TP:T].rearrange("p c b -> p b c"),
                                             kt[r, TP:T].unsqueeze(2).to_broadcast([HD, NS, NP]), ALU.mult))
                    dve.wait_ge(pe_step, 4)
                    step(V.scalar_tensor_tensor(s[:], s_ps[:], SCALE, rel[:, 0:WIN + 1], ALU.mult, ALU.add))
                    step(V.tensor_reduce(stat[:, 0:1], s[:], AX_X, ALU.max))
                    step(V.tensor_tensor(stat[:, 0:1], stat[:, 0:1], rel[:, WIN + 1:], ALU.max))
                    step(V.tensor_scalar(stat[:, 1:2], stat[:, 0:1], -1.0, None, ALU.mult))
                    step(V.tensor_tensor(stat[:, 3:4], rel[:, WIN + 1:], stat[:, 1:2], ALU.add))
                    dve.wait_ge(act_step, 5)
                    dve.wait_ge(sink_done, 2)
                    step(V.tensor_tensor(stat[:, 4:5], stat[:, 2:3], stat[:, 3:4], ALU.add))
                    step(V.reciprocal(stat[:, 5:6], stat[:, 4:5]))
                    step(V.tensor_scalar(s[:], s[:], stat[:, 5:6], None, ALU.mult))
                    dve.wait_ge(pe_step, 7)
                    step(V.tensor_tensor(part[:], self_ps[:], vt[:, TP:T].unsqueeze(2).unsqueeze(3).to_broadcast([P, NS, 2, NP]),
                                         ALU.mult))
                    for kv, r in enumerate(halves):
                        step(V.tensor_tensor(ob[r, :, TP:T].rearrange("p c b -> p b c"), part[r, :, kv], o_ps[r, :, kv], ALU.add))


def project(nc, w_dram, turns, w, w_loaded, w_free, summed, taken, ps, src, out, kd=KD, store=None):
    if store:
        buffer, dram, stored = store
    with nc.Block() as block:
        @block.sync
        def _(sp):
            with sp.Fori(0, turns) as i:
                for s in range(2):
                    sp.wait_ge(w_free, i * 2 + s + 2)
                    sp.dma_start(w[:, s], w_dram[bass.ds(i * 2 + s, 1)].rearrange("o p k n -> p (o k) n"))\
                        .then_inc(w_loaded[s], 16)

        @block.tensor
        def _(pe):
            pe.sem_inc(w_free, 2)
            with pe.Fori(0, turns) as i:
                for s in range(2):
                    pe.wait_ge(w_loaded[s], i * 16 + 17)
                    pe.wait_ge(taken, i * 2 + 1)
                    for t in range(NT):
                        for k in range(kd):
                            mm = nc.tensor.matmul(ps[s][:, t, 0:TN], w[:, s, k], src[:, k, t * TN:(t + 1) * TN],
                                                  start=k == 0, stop=k == kd - 1)
                    mm.then_inc(summed, 1)
                    pe.wait_ge(summed, i * 2 + s + 2)
                    pe.sem_inc(w_free, 1)

        @block.scalar
        def _(act):
            if store:
                for s in range(2):
                    act.sem_inc(stored[s], 16)
            with act.Fori(0, turns) as i:
                for s in range(2):
                    act.wait_ge(summed, i * 2 + s + 2)
                    if store:
                        act.wait_ge(stored[s], i * 16 + 17)
                        dst = buffer[:, s].rearrange("p (t n) -> p t n", t=NT)
                    else:
                        dst = out(bass.ds(i * 2 + s, 1))
                    nc.scalar.activation(dst, ps[s][:, :, 0:TN], ACT.Copy).then_inc(taken, 1)
                    if store:
                        act.wait_ge(taken, i * 2 + s + 2)
                        act.dma_start(dram[:, bass.ds(i * 2 + s, 1), :].rearrange("p o n -> p (o n)"), buffer[:, s])\
                            .then_inc(stored[s], 16)
            if store:
                for s in range(2):
                    act.wait_ge(stored[s], turns * 16 + 17)


def merge(nc, io, sb, pb, sm, ya, ob, merged, **_):
    SETS = 4
    with ExitStack() as ph:
        w = sb(ph, "w_merge", [P, 2, 2, NP, P])
        gate = sb(ph, "gate", [P, 2, 2, T])
        part = sb(ph, "merge_part", [P, 2, 2, TN])
        ps = [[pb(ph, f"merge_ps{s}{q}", [P, 512]) for q in range(2)] for s in range(SETS)]
        w0_loaded, w1_loaded, g0_loaded, g1_loaded, w_free, summed, gates_ready, parts_ready, used = sm(
            ph, "wm0_loaded", "wm1_loaded", "gate0_loaded", "gate1_loaded", "wm_free", "merge_summed", "gates_ready",
            "merge_parts", "merge_used")
        w_loaded, g_loaded = (w0_loaded, w1_loaded), (g0_loaded, g1_loaded)
        TURN = 4
        with nc.Block() as block:
            @block.sync
            def _(sp):
                with sp.Fori(0, KD // TURN) as i:
                    for m in range(TURN):
                        s = m % 2
                        sp.wait_ge(w_free, i * TURN + m + 2)
                        sp.dma_start(w[:, s].rearrange("p q k n -> p (q k n)"), io["w_merge"][bass.ds(i * TURN + m, 1)].rearrange("o p k n -> p (o k n)"))\
                            .then_inc(w_loaded[s], 16)
                        sp.dma_start(gate[:, s], io["side_saved"][:, bass.ds(i * (2 * TURN) + (2 * m + 6), 2), :])\
                            .then_inc(g_loaded[s], 16)

            @block.tensor
            def _(pe):
                pe.sem_inc(used, SETS)
                with pe.Fori(0, KD // TURN) as i:
                    for n in range(TURN * NT):
                        m, t = n // NT, n % NT
                        if t == 0:
                            pe.wait_ge(w_loaded[m % 2], i * (TURN * 8) + (m // 2 * 16 + 17))
                        pe.wait_ge(used, i * (TURN * NT) + (n + 2))
                        for q, src in enumerate((ya, ob)):
                            for k in range(NP):
                                mm = nc.tensor.matmul(ps[n % SETS][q][:, 0:TN], w[:, m % 2, q, k],
                                                      src[:, k, t * TN:(t + 1) * TN], start=k == 0, stop=k == NP - 1)
                        mm.then_inc(summed, 1)

            @block.scalar
            def _(act):
                with act.Fori(0, KD // TURN) as i:
                    for m in range(TURN):
                        act.wait_ge(g_loaded[m % 2], i * (TURN * 8) + (m // 2 * 16 + 17))
                        nc.scalar.activation(gate[:, m % 2], gate[:, m % 2], ACT.Sigmoid).then_inc(gates_ready, 1)

            @block.vector
            def _(dve):
                V = nc.vector
                dve.sem_inc(w_free, 2)
                with dve.Fori(0, KD // TURN) as i:
                    for n in range(TURN * NT):
                        m, t = n // NT, n % NT
                        tok = slice(t * TN, (t + 1) * TN)
                        if t == 0:
                            dve.wait_ge(gates_ready, i * TURN + (m + 2))
                        dve.wait_ge(summed, i * (TURN * NT) + (n + 2))
                        dve.wait_ge(used, i * (TURN * NT) + (n + SETS))
                        for q in range(2):
                            V.tensor_tensor(part[:, n % 2, q], gate[:, m % 2, q, tok], ps[n % SETS][q][:, 0:TN], ALU.mult)\
                                .then_inc(parts_ready, 1)
                        dve.wait_ge(parts_ready, i * (2 * TURN * NT) + (2 * n + 3))
                        V.tensor_tensor(merged[:, bass.ds(i * TURN + m, 1), tok], part[:, n % 2, 0:1],
                                        part[:, n % 2, 1:2], ALU.add).then_inc(used, 1)
                        if t == NT - 1:
                            dve.wait_ge(used, i * (TURN * NT) + (n + SETS + 2))
                            dve.sem_inc(w_free, 1)


def mixer_output(nc, io, sb, pb, sm, mod, x, merged, **_):
    with ExitStack() as ph:
        w = sb(ph, "w_o", [P, 2, KD, P])
        mix = sb(ph, "mix", [P, 2, T])
        ps = [pb(ph, f"o_ps{s}", [P, NT, 512]) for s in range(2)]
        w0_loaded, w1_loaded, w_free, summed, taken, x_loaded, chain = sm(
            ph, "wo0_loaded", "wo1_loaded", "wo_free", "wo_summed", "wo_taken", "x_back", "wo_chain")
        w_loaded = (w0_loaded, w1_loaded)
        with nc.Block() as block:
            @block.sync
            def _(sp):
                sp.dma_start(x[:], io["x_saved"]).then_inc(x_loaded, 16)
                with sp.Fori(0, KD // 2) as i:
                    for s in range(2):
                        sp.wait_ge(w_free, i * 2 + s + 2)
                        sp.dma_start(w[:, s], io["w_o"][bass.ds(i * 2 + s, 1)].rearrange("o p k n -> p (o k) n"))\
                            .then_inc(w_loaded[s], 16)

            @block.tensor
            def _(pe):
                pe.sem_inc(w_free, 2)
                with pe.Fori(0, KD // 2) as i:
                    for s in range(2):
                        pe.wait_ge(w_loaded[s], i * 16 + 17)
                        pe.wait_ge(taken, i * 2 + 1)
                        for t in range(NT):
                            for k in range(KD):
                                mm = nc.tensor.matmul(ps[s][:, t, 0:TN], w[:, s, k], merged[:, k, t * TN:(t + 1) * TN],
                                                      start=k == 0, stop=k == KD - 1)
                        mm.then_inc(summed, 1)
                        pe.wait_ge(summed, i * 2 + s + 2)
                        pe.sem_inc(w_free, 1)

            @block.vector
            def _(dve):
                link = Chain(dve, chain)
                V = nc.vector
                dve.wait_ge(x_loaded, 17)
                with dve.Fori(0, KD // 2) as i:
                    link.enter(i, 4)
                    for s in range(2):
                        dve.wait_ge(summed, i * 2 + s + 2)
                        m_ = bass.ds(i * 2 + s, 1)
                        gate = mod[:, bass.ds(i * 2 + (s + GT_M), 1), :].rearrange("p o n -> p (o n)")
                        link(V.tensor_scalar(mix[:, s].rearrange("p (t n) -> p t n", t=NT), ps[s][:, :, 0:TN], gate[:, 0:1],
                                             None, ALU.mult))
                        V.tensor_tensor(mix[:, s, TP:T], ps[s][:, NT - 1, TN - NS:TN], gate[:, 1:], ALU.mult)\
                            .then_inc(taken, 1)
                        dve.wait_ge(taken, i * 2 + s + 2)
                        xm = x[:, m_, :].rearrange("p o n -> p (o n)")
                        link(V.scalar_tensor_tensor(xm, xm, ALPHA, mix[:, s], ALU.mult, ALU.add))
                    link.leave(KD // 2)


TILES = -(-T // P)


def split_input(nc, sb, sm, h, hh, hl, **_):
    with ExitStack() as ph:
        high_ready, low_ready = sm(ph, "high_ready", "low_ready")
        with nc.Block() as block:
            @block.scalar
            def _(act):
                for k in range(KD):
                    nc.scalar.activation(hh[:, k], h[:, k], ACT.Copy).then_inc(high_ready, 1)

            @block.vector
            def _(dve):
                for k in range(KD):
                    dve.wait_ge(high_ready, k + 2)
                    nc.vector.tensor_tensor(hl[:, k], h[:, k], hh[:, k].bitcast(F32), ALU.subtract).then_inc(low_ready, 1)


def peer_queries(nc, io, sb, pb, sm, h, **_):
    with ExitStack() as ph:
        w = sb(ph, "wpq", [P, 2, KD, P])
        out = sb(ph, "query_out", [P, 2, T])
        ps = [pb(ph, f"wpq_ps{s}", [P, NT, 512]) for s in range(2)]
        w0_loaded, w1_loaded, w_free, summed, taken, stored0, stored1 = sm(
            ph, "wpq0_loaded", "wpq1_loaded", "wpq_free", "query_summed", "query_taken", "query0_stored", "query1_stored")
        project(nc, io["peer_wq"], NH, w, (w0_loaded, w1_loaded), w_free, summed, taken, ps, h, None,
                store=(out, io["query_saved"], (stored0, stored1)))


class Hidden:

    def __init__(self, nc, io, sb, pb, sm, ph, hh, hl, first, tag):
        self.nc, self.io, self.hh, self.hl, self.first = nc, io, hh, hl, first
        self.raw = sb(ph, f"u_raw_{tag}", [P, 2, KD, P])
        self.uh = sb(ph, f"u_high_{tag}", [P, 2, KD, P], F32R)
        self.ul = sb(ph, f"u_low_{tag}", [P, 2, KD, P], F32R)
        self.out = sb(ph, f"hidden_{tag}", [P, 2, NT, TN])
        self.ps = [pb(ph, f"hidden_ps{s}_{tag}", [P, NT, 512]) for s in range(2)]
        (u0, u1, self.high_ready, self.split, self.summed, self.ready, s0, s1) = sm(
            ph, *(f"{n}_{tag}" for n in ("u0_loaded", "u1_loaded", "u_high_ready", "u_split", "hidden_summed",
                                         "hidden_ready", "hidden0_stored", "hidden1_stored")))
        self.loaded, self.stored = (u0, u1), (s0, s1)

    def load(self, sp, n, slot):
        sp.wait_ge(self.split, n + 2)
        sp.dma_start(self.raw[:, slot], self.io["u"][bass.ds(n + self.first, 1)].rearrange("o p k n -> p (o k) n"))\
            .then_inc(self.loaded[slot], 16)

    def split_high(self, act, n, slot, turn):
        act.wait_ge(self.loaded[slot], turn * 16 + 17)
        act.wait_ge(self.summed, n + 2)
        self.nc.scalar.activation(self.uh[:, slot], self.raw[:, slot], ACT.Copy).then_inc(self.high_ready, 1)

    def split_low(self, pool, n, slot):
        pool.wait_ge(self.high_ready, n + 2)
        self.nc.gpsimd.tensor_tensor(self.ul[:, slot], self.raw[:, slot], self.uh[:, slot].bitcast(F32), ALU.subtract)\
            .then_inc(self.split, 1)

    def multiply(self, pe, n, slot, t):
        if t == 0:
            pe.wait_ge(self.split, n + 4)
            pe.wait_ge(self.ready, n + 2)
        tok = slice(t * TN, (t + 1) * TN)
        for k in range(KD):
            for u, h in ((self.uh, self.hh), (self.uh, self.hl), (self.ul, self.hh)):
                mm = self.nc.tensor.matmul(self.ps[slot][:, t, 0:TN], u[:, slot, k], h[:, k, tok],
                                           start=k == 0 and h is self.hh and u is self.uh, stop=k == KD - 1 and u is self.ul)
        if t == NT - 1:
            mm.then_inc(self.summed, 1)

    def gelu(self, act, n, slot, turn):
        act.wait_ge(self.summed, n + 4)
        act.wait_ge(self.stored[slot], turn * 16 + 17)
        self.nc.scalar.activation(self.out[:, slot], self.ps[slot][:, :, 0:TN], ACT.Gelu).then_inc(self.ready, 1)

    def store(self, sp, n, slot):
        sp.wait_ge(self.ready, n + 4)
        sp.dma_start(self.io["hidden_saved"][bass.ds(n + self.first, 1)].rearrange("o p n -> p (o n)"),
                     self.out[:, slot].rearrange("p t n -> p (t n)")).then_inc(self.stored[slot], 16)


E_FIRST, E_SEL, E_LAST = 8, 4, 6
FIRST_GATES = E_FIRST + (TILES - 2) * E_SEL + E_LAST


def peer_select(nc, io, sb, pb, sm, consts, hh, hl, slots, **_):
    with ExitStack() as ph:
        NJ = 2 * NH
        HJ = NJ // 2
        hid = Hidden(nc, io, sb, pb, sm, ph, hh, hl, 0, "s")
        keys = sb(ph, "keys", [P, 2, NKEY])
        qt = sb(ph, "qt", [P, NJ, P])
        s_in = sb(ph, "scores", [P, NJ, NKEY])
        s = sb(ph, "cands", [P, NJ, NKEY])
        s2 = sb(ph, "rest", [P, NJ, NKEY])
        best = sb(ph, "best", [P, NJ, TOPK])
        best_at = sb(ph, "best_at", [P, NJ, TOPK], U32)
        best_key = sb(ph, "best_key", [P, NJ, TOPK])
        cand, cand2 = (t[:].rearrange("p (h q) n -> p h (q n)", q=2) for t in (s, s2))
        top = sb(ph, "top", [P, NH, TOPK])
        top_at = sb(ph, "top_at", [P, NH, TOPK], U32)
        half_at = sb(ph, "half_at", [P, 2, NH, TOPK], U32)
        half_pos = sb(ph, "half_pos", [P, 2, NH, TOPK])
        pick = [s, s2]
        slot = sb(ph, "slot", [P, 3, NH, TOPK])
        total = sb(ph, "total", [P, 2, NH])
        s_ps = pb(ph, "score_ps", [P, HJ, NKEY])
        t_ps = s_ps[:].rearrange("p j n -> p (j n)")[:, 0:3 * P].rearrange("p (q n) -> p q n", q=3)
        (keys_loaded, q_loaded, scored, copied, read, chain, gate_ready, slots_ready, turned, slots_taken,
         exp_in, carried) = sm(ph, "keys_loaded", "query_loaded", "scored_keys", "scores_copied", "scores_read",
                               "select_chain", "gate_exp", "slots_ready", "slots_turned", "slots_taken", "exp_in",
                               "select_carried")
        LAST = TILES - 1

        def shape(t):
            return t[:].rearrange("p (h q) n -> p h (q n)", q=2).rearrange("p h (k a) -> p h k a", k=TOPK)

        def tiles(eng, body):
            body(0, P)
            with eng.Fori(1, LAST) as i:
                body(i, P)
            body(LAST, T - LAST * P)

        def is_(i, n):
            return isinstance(i, int) and i == n

        def chunks(i):
            if is_(i, 0):
                return [(j, j % 2, j // 2) for j in range(E_FIRST)]
            more = E_FIRST - E_SEL
            return [(i * E_SEL + (j + more), j % 2, i * (E_SEL // 2) + (j + more) // 2)
                    for j in range(E_LAST if is_(i, LAST) else E_SEL)]

        with nc.Block() as block:
            @block.sync
            def _(sp):
                def query(i, n):
                    sp.dma_start(qt[:, :, 0:n], io["query_saved"][:, :, bass.ds(i * P, n)]).then_inc(q_loaded, 16)

                def body(i, n):
                    for j, (m, s_, turn) in enumerate(chunks(i)):
                        if not (is_(i, LAST) and j >= E_LAST - 2):
                            hid.load(sp, m + 2, s_)
                        if j == 1 and n:
                            sp.wait_ge(scored, i * 2 + 3)
                            query(i + 1, n)
                        hid.store(sp, m, s_)

                sp.dma_start(keys[:], io["keys"]).then_inc(keys_loaded, 16)
                query(0, P)
                for s_ in range(2):
                    sp.sem_inc(hid.stored[s_], 16)
                    hid.load(sp, s_, s_)
                body(0, P)
                with sp.Fori(1, LAST - 1) as i:
                    body(i, P)
                body(LAST - 1, T - LAST * P)
                body(LAST, 0)
                for q in range(2):
                    sp.wait_ge(hid.stored[q], FIRST_GATES // 2 * 16 + 17)

            @block.gpsimd
            def _(pool):
                pool.sem_inc(hid.split, 2)

                def body(i, n):
                    for m, s_, turn in chunks(i):
                        hid.split_low(pool, m, s_)
                tiles(pool, body)

            @block.tensor
            def _(pe):
                pe.sem_inc(hid.summed, 2)
                pe.wait_ge(keys_loaded, 17)

                def score(i, n, half):
                    if half == 0:
                        pe.wait_ge(q_loaded, i * 16 + 17)
                        pe.wait_ge(slots_taken, i + 1)
                    else:
                        pe.wait_ge(copied, i * 2 + 2)
                    for j in range(HJ):
                        mm = nc.tensor.matmul(s_ps[0:n, j], qt[:, half * HJ + j, 0:n], keys[:, j % 2], start=True, stop=True)
                    mm.then_inc(scored, 1)

                def turn(i, n):
                    pe.wait_ge(slots_ready, i + 2)
                    for q in range(3):
                        mm = nc.tensor.transpose(t_ps[:, q, 0:n], slot[0:n, q].rearrange("p h k -> p (h k)"),
                                                 col(consts, "ident")[0:n, 0:n])
                    mm.then_inc(turned, 1)

                def body(i, n):
                    for j, (m, s_, _) in enumerate(chunks(i)):
                        if j < 2:
                            score(i, n, j)
                        if j == 3 and not is_(i, 0):
                            pe.wait_ge(copied, i * 2 + 3)
                            turn(i - 1, P)
                        for t in range(NT):
                            hid.multiply(pe, m, s_, t)
                tiles(pe, body)
                turn(LAST, T - LAST * P)

            @block.scalar
            def _(act):
                S = nc.scalar
                act.sem_inc(hid.ready, 2)
                act.sem_inc(slots_taken, 1)
                hid.split_high(act, 0, 0, 0)

                def copy(i, n, half):
                    act.wait_ge(scored, i * 2 + (half + 2))
                    act.wait_ge(read, i + 1)
                    S.activation(s_in[0:n, half * HJ:(half + 1) * HJ], s_ps[0:n], ACT.Copy).then_inc(copied, 1)

                def exp(i, n):
                    act.wait_ge(exp_in, i + 2)
                    S.activation(slot[0:n, 2], slot[0:n, 2], ACT.Exp).then_inc(gate_ready, 1)

                def take(i, n):
                    act.wait_ge(turned, i + 2)
                    S.activation(slots[:, :, bass.ds(i * P, n)], t_ps[:, :, 0:n], ACT.Copy).then_inc(slots_taken, 1)

                def body(i, n):
                    for j, (m, s_, turn) in enumerate(chunks(i)):
                        if not (is_(i, LAST) and j == E_LAST - 1):
                            hid.split_high(act, m + 1, 1 - s_, turn + s_)
                        if j < 2:
                            copy(i, n, j)
                        if j == 1 and not is_(i, 0):
                            exp(i - 1, P)
                        hid.gelu(act, m, s_, turn)
                        if j == 3 and not is_(i, 0):
                            take(i - 1, P)
                tiles(act, body)
                exp(LAST, T - LAST * P)
                take(LAST, T - LAST * P)

            @block.vector
            def _(dve):
                link = Chain(dve, chain)
                V = nc.vector

                def top16(n, values, rest, out, out_at, count):
                    carry(dve, carried)
                    for j in range(count):
                        ins = V.max(out=out[0:n, j, 0:8], in_=values[0:n, j])
                    link(ins)
                    carry(dve, carried)
                    for j in range(count):
                        V.max_index(out=out_at[0:n, j, 0:8], in_max=out[0:n, j, 0:8], in_values=values[0:n, j])
                        ins = V.match_replace(out=rest[0:n, j], in_to_replace=out[0:n, j, 0:8],
                                              in_values=values[0:n, j], imm_value=-3e38)
                    link(ins)
                    carry(dve, carried)
                    for j in range(count):
                        ins = V.max(out=out[0:n, j, 8:16], in_=rest[0:n, j])
                    link(ins)
                    carry(dve, carried)
                    for j in range(count):
                        ins = V.max_index(out=out_at[0:n, j, 8:16], in_max=out[0:n, j, 8:16], in_values=rest[0:n, j])
                    link(ins)

                def normalise(i, n):
                    dve.wait_ge(gate_ready, i + 2)
                    link(V.tensor_reduce(total[0:n, 0], slot[0:n, 2], AX_X, ALU.add))
                    link(V.reciprocal(total[0:n, 1], total[0:n, 0]))
                    V.tensor_tensor(slot[0:n, 2], slot[0:n, 2], total[0:n, 1].unsqueeze(2).to_broadcast([n, NH, TOPK]),
                                    ALU.mult).then_inc(slots_ready, 1)

                def body(i, n):
                    dve.wait_ge(copied, i * 2 + 3)
                    top16(n, s_in, s2, best, best_at, NJ)
                    dve.sem_inc(read, 1)
                    if not is_(i, 0):
                        normalise(i - 1, P)
                    link(V.tensor_copy(best_key[0:n], best_at[0:n]))
                    b4 = best[0:n].rearrange("p (h q) k -> p h q k", q=2)
                    k4 = best_key[0:n].rearrange("p (h q) k -> p h q k", q=2)
                    wide = [n, NH, TOPK, TOPK]
                    link(V.tensor_tensor(shape(s)[0:n], b4[:, :, 0].unsqueeze(3).to_broadcast(wide),
                                         b4[:, :, 1].unsqueeze(2).to_broadcast(wide), ALU.add))
                    top16(n, cand, cand2, top, top_at, NH)
                    if not is_(i, 0):
                        dve.wait_ge(turned, i + 1)
                    V.tensor_scalar(half_at[0:n, 0], top_at[0:n], 4, None, ALU.logical_shift_right)
                    link(V.tensor_scalar(half_at[0:n, 1], top_at[0:n], 15, None, ALU.bitwise_and))
                    V.tensor_copy(half_pos[0:n], half_at[0:n])
                    link(V.tensor_tensor(slot[0:n, 2], top[0:n], top[0:n, :, 0:1].to_broadcast([n, NH, TOPK]), ALU.subtract))
                    dve.sem_inc(exp_in, 1)
                    iota = col(consts, "iota16")[0:n].unsqueeze(1).unsqueeze(1).to_broadcast(wide)
                    for q in range(2):
                        ins = V.tensor_tensor(shape(pick[q])[0:n], half_pos[0:n, q].unsqueeze(3).to_broadcast(wide), iota,
                                              ALU.is_equal)
                    link(ins)
                    for q in range(2):
                        ins = V.tensor_tensor(shape(pick[q])[0:n], shape(pick[q])[0:n],
                                              k4[:, :, q].unsqueeze(2).to_broadcast(wide), ALU.mult)
                    link(ins)
                    for q in range(2):
                        ins = V.tensor_reduce(slot[0:n, q], shape(pick[q])[0:n], AX_X, ALU.add)
                    link(ins)

                body(0, P)
                per = link.n + 2
                with dve.Fori(1, LAST) as i:
                    link.enter(i - 1, per)
                    body(i, P)
                    link.leave(LAST - 1)
                body(LAST, T - LAST * P)
                normalise(LAST, T - LAST * P)


TB = 24
NTB = T // TB


def peer_gates(nc, io, sb, pb, sm, consts, hh, hl, slots, **_):
    GR = 4
    NG = TB // GR
    FIRST = FIRST_GATES
    assert NKEY - FIRST == 2 * NTB
    with ExitStack() as ph:
        hid = Hidden(nc, io, sb, pb, sm, ph, hh, hl, FIRST, "g")
        second = sb(ph, "second", [P, 2, GR, NKEY], BF16)
        first = sb(ph, "first", [P, 2, GR, 3, NKEY], BF16)
        iota = sb(ph, "iota_bf16", [P, NKEY], BF16)
        part_bf16 = sb(ph, "part_bf16", [P, T], BF16)
        part = sb(ph, "gate_parts", [P, 3, T])
        gates = sb(ph, "gates", [P, 2, NKEY, TB])
        ps = [pb(ph, f"gates_ps{s}", [P, GR, NKEY]) for s in range(2)]
        first_ready, second_ready, summed, taken, stored0, stored1, block_done, chain = sm(
            ph, "first_ready", "second_ready", "gates_summed", "gates_taken", "gates_stored0", "gates_stored1",
            "gates_done", "parts_chain")
        stored = (stored0, stored1)

        def blocks(eng, body):
            with eng.Fori(0, NTB // 2) as i:
                for half in range(2):
                    body(i * 2 + half, half, i * 2 + half, False)
            body(NTB - 1, 0, NTB - 1, True)

        with nc.Block() as block:
            @block.vector
            def _(dve):
                V = nc.vector
                link = Chain(dve, chain)
                link(V.tensor_copy(iota[:], col(consts, "iota")))
                rest = slots[:, 2]
                for q in range(2):
                    link(V.tensor_copy(part_bf16[:], rest))
                    link(V.tensor_copy(part[:, q], part_bf16[:]))
                    link(V.tensor_tensor(part[:, 2], rest, part[:, q], ALU.subtract))
                    rest = part[:, 2]

                def body(b, half, turn, last):
                    for g in range(NG):
                        dve.wait_ge(summed, b * NG + g + 2)
                        for t in range(GR):
                            at = bass.ds(b * TB + (g * GR + t), 1)
                            for q in range(3):
                                ins = V.tensor_scalar(first[:, g % 2, t, q], iota[:], slots[:, 0, at], part[:, q, at],
                                                      ALU.is_equal, ALU.mult)
                        ins.then_inc(first_ready, 1)
                        V.tensor_tensor(second[:, g % 2], iota[:].unsqueeze(1).to_broadcast([P, GR, NKEY]),
                                        slots[:, 1, bass.ds(b * TB + g * GR, GR)].unsqueeze(2).to_broadcast([P, GR, NKEY]),
                                        ALU.is_equal).then_inc(second_ready, 1)
                blocks(dve, body)

            @block.gpsimd
            def _(pool):
                pool.sem_inc(hid.split, 2)

                def body(b, half, turn, last):
                    for e in range(2):
                        hid.split_low(pool, b * 2 + e, e)
                blocks(pool, body)

            @block.tensor
            def _(pe):
                pe.sem_inc(summed, 2)
                pe.sem_inc(hid.summed, 2)

                def body(b, half, turn, last):
                    for g in range(NG):
                        hid.multiply(pe, b * 2 + g // NT, g // NT, g % NT)
                        pe.wait_ge(first_ready, b * NG + g + 2)
                        pe.wait_ge(second_ready, b * NG + g + 2)
                        pe.wait_ge(taken, b * NG + g + 2)
                        for t in range(GR):
                            for q in range(3):
                                mm = nc.tensor.matmul(ps[g % 2][:, t], second[:, g % 2, t], first[:, g % 2, t, q],
                                                      start=q == 0, stop=q == 2)
                        mm.then_inc(summed, 1)
                blocks(pe, body)

            @block.scalar
            def _(act):
                act.sem_inc(taken, 2)
                act.sem_inc(hid.ready, 2)
                hid.split_high(act, 0, 0, 0)

                def body(b, half, turn, last):
                    act.wait_ge(stored[half], (turn - half) * 8 + 17)
                    for g in range(NG):
                        e = g // NT
                        if g % NT == 0 and not (last and e == 1):
                            hid.split_high(act, b * 2 + (e + 1), (e + 1) % 2, b + (e + 1) // 2)
                        if g % NT == NT - 1:
                            hid.gelu(act, b * 2 + e, e, b)
                        act.wait_ge(summed, b * NG + g + 4)
                        nc.scalar.activation(gates[:, half, :, g * GR:(g + 1) * GR],
                                             ps[g % 2][:].rearrange("p t k -> p k t"), ACT.Copy).then_inc(taken, 1)
                    act.wait_ge(taken, b * NG + (NG + 3))
                    act.sem_inc(block_done, 1)
                blocks(act, body)

            @block.sync
            def _(sp):
                for s in (*stored, *hid.stored):
                    sp.sem_inc(s, 16)
                for e in range(2):
                    hid.load(sp, e, e)

                def body(b, half, turn, last):
                    for e in range(2):
                        if not last:
                            hid.load(sp, b * 2 + (e + 2), e)
                        hid.store(sp, b * 2 + e, e)
                    sp.wait_ge(block_done, b + 2)
                    out = io["gates"][:, bass.ds(b, 1)].rearrange("p o k t -> p (o k t)")
                    sp.dma_start(out, gates[:, half].rearrange("p k t -> p (k t)")).then_inc(stored[half], 16)
                blocks(sp, body)
                sp.wait_ge(stored0, (NTB // 2 + 1) * 16 + 17)
                sp.wait_ge(stored1, (NTB // 2) * 16 + 17)
                for q in range(2):
                    sp.wait_ge(hid.stored[q], (NKEY - FIRST) // 2 * 16 + 17)


def peer_experts(nc, io, sb, pb, sm, acc, **_):
    GR, NGRP, NG_LOAD = 2, 4, 4
    TURNS = NKEY // (GR * NGRP)
    CH = GR * NGRP
    NO = KD * NT
    NBANK = 8
    with ExitStack() as ph:
        v_raw = sb(ph, "v_raw", [P, 2, D])
        vh = sb(ph, "v_high", [P, 2, GR, D], F32R)
        vl = sb(ph, "v_low", [P, 2, GR, D], F32R)
        hid = sb(ph, "hidden_back", [P, 2, T])
        g = sb(ph, "g", [P, 2, NTB, NG_LOAD, TB])
        prod = sb(ph, "weighted_hidden", [P, 2, T])
        wh = sb(ph, "w_high", [P, 2, GR, T], F32R)
        wl = sb(ph, "w_low", [P, 2, GR, T], F32R)
        out_ps = [pb(ph, f"out_ps{s}", [P, 512]) for s in range(NBANK)]
        (v0, v1, h0, h1, g0, g1, v_high, v_split, g_free, weighted, w_high, w_split, summed, added, cleared) = sm(
            ph, "v0_loaded", "v1_loaded", "h0_loaded", "h1_loaded", "g0_loaded", "g1_loaded", "v_high_ready", "v_split",
            "g_free", "weighted", "w_high_ready", "w_split", "experts_summed", "experts_added", "acc_cleared")
        v_loaded, h_loaded, g_loaded = (v0, v1), (h0, h1), (g0, g1)

        with nc.Block() as block:
            @block.sync
            def _(sp):
                with sp.Fori(0, TURNS) as i:
                    for c in range(CH):
                        if c % NG_LOAD == 0:
                            half = c // NG_LOAD
                            sp.wait_ge(g_free, i * 2 + (half + 2))
                            sp.dma_start(g[:, half], io["gates"][:, :, bass.ds(i * CH + c, NG_LOAD), :])\
                                .then_inc(g_loaded[half], 16)
                        sp.wait_ge(w_split, i * CH + (c + 2))
                        sp.dma_start(hid[:, c % 2], io["hidden_saved"][bass.ds(i * CH + c, 1)].rearrange("o p n -> p (o n)"))\
                            .then_inc(h_loaded[c % 2], 16)
                        sp.wait_ge(v_split, i * CH + (c + 2))
                        sp.dma_start(v_raw[:, c % 2], io["v"][bass.ds(i * CH + c, 1)].rearrange("o p n -> p (o n)"))\
                            .then_inc(v_loaded[c % 2], 16)

            @block.gpsimd
            def _(pool):
                pool.sem_inc(v_split, 2)
                with pool.Fori(0, TURNS) as i:
                    for c in range(CH):
                        pool.wait_ge(v_high, i * CH + (c + 2))
                        half, j = c // GR % 2, c % GR
                        nc.gpsimd.tensor_tensor(vl[:, half, j], v_raw[:, c % 2], vh[:, half, j].bitcast(F32), ALU.subtract)\
                            .then_inc(v_split, 1)

            @block.scalar
            def _(act):
                with act.Fori(0, TURNS) as i:
                    for c in range(CH):
                        half, j = c // GR % 2, c % GR
                        if j == 0:
                            act.wait_ge(summed, i * (NGRP * NO) + ((c // GR + 1) * NO + 1))
                        act.wait_ge(v_loaded[c % 2], i * (CH * 8) + (c // 2 * 16 + 17))
                        nc.scalar.activation(vh[:, half, j], v_raw[:, c % 2], ACT.Copy).then_inc(v_high, 1)
                        act.wait_ge(weighted, i * CH + (c + 2))
                        nc.scalar.activation(wh[:, half, j], prod[:, c % 2], ACT.Copy).then_inc(w_high, 1)

            @block.tensor
            def _(pe):
                with pe.Fori(0, TURNS) as i:
                    for grp in range(NGRP):
                        half = grp % 2
                        pe.wait_ge(v_split, i * CH + (grp * GR + GR + 3))
                        pe.wait_ge(w_split, i * CH + (grp * GR + GR + 3))
                        for m in range(KD):
                            for t in range(NT):
                                o = m * NT + t
                                pe.wait_ge(added, i * (NGRP * NO) + (grp * NO + o + 2))
                                for j in range(GR):
                                    tok = slice(t * TN, (t + 1) * TN)
                                    feat = slice(m * P, (m + 1) * P)
                                    for q, (v, w) in enumerate(((vh, wh), (vh, wl), (vl, wh))):
                                        mm = nc.tensor.matmul(out_ps[o % NBANK][:, 0:TN], v[:, half, j, feat],
                                                              w[:, half, j, tok], start=j == 0 and q == 0,
                                                              stop=j == GR - 1 and q == 2)
                                mm.then_inc(summed, 1)

            @block.vector
            def _(dve):
                V = nc.vector
                dve.sem_inc(added, NBANK)
                dve.sem_inc(g_free, 2)
                dve.sem_inc(w_split, 2)
                dve.sem_inc(summed, 2 * NO)
                V.memset(acc[:], 0.0).then_inc(cleared, 1)
                dve.wait_ge(cleared, 2)

                def weigh(i, c):
                    dve.wait_ge(h_loaded[c % 2], i * (CH * 8) + (c // 2 * 16 + 17))
                    if c % NG_LOAD == 0:
                        dve.wait_ge(g_loaded[c // NG_LOAD], i * 16 + 17)
                    V.tensor_tensor(prod[:, c % 2].rearrange("p (b t) -> p b t", t=TB),
                                    hid[:, c % 2].rearrange("p (b t) -> p b t", t=TB),
                                    g[:, c // NG_LOAD, :, c % NG_LOAD], ALU.mult).then_inc(weighted, 1)

                def split(i, c):
                    dve.wait_ge(w_high, i * CH + (c + 2))
                    V.tensor_tensor(wl[:, c // GR % 2, c % GR], prod[:, c % 2], wh[:, c // GR % 2, c % GR].bitcast(F32),
                                    ALU.subtract).then_inc(w_split, 1)
                    if c % NG_LOAD == NG_LOAD - 1:
                        dve.sem_inc(g_free, 1)

                def add(i, grp, o):
                    dve.wait_ge(summed, i * (NGRP * NO) + (grp * NO + o + 2 + 2 * NO))
                    a = acc[:, o // NT, o % NT * TN:(o % NT + 1) * TN]
                    V.tensor_tensor(a, a, out_ps[o % NBANK][:, 0:TN], ALU.add).then_inc(added, 1)

                def turn(i, last):
                    for grp in range(NGRP):
                        for o in range(NO):
                            if o == 0:
                                dve.wait_ge(added, i * (NGRP * NO) + (grp * NO + 1 + NBANK))
                            add(i, grp, o)
                            nxt = (grp + 1) * GR
                            if not (last and grp == NGRP - 1):
                                at = {3: (weigh, 0), 7: (split, 0), 11: (weigh, 1), 15: (split, 1)}.get(o)
                                if at:
                                    c = nxt + at[1]
                                    at[0](i + c // CH, c % CH)

                for c in range(GR):
                    weigh(0, c)
                    split(0, c)
                with dve.Fori(0, TURNS - 1) as i:
                    turn(i, False)
                turn(TURNS - 1, True)


def peer_output(nc, sm, mod, x, acc, **_):
    with ExitStack() as ph:
        chain, = sm(ph, "peer_out_chain")
        with nc.Block() as block:
            @block.vector
            def _(dve):
                V = nc.vector
                for k in range(KD):
                    V.tensor_scalar(acc[:, k, 0:TP], acc[:, k, 0:TP], mod[:, GT_F + k, 0:1], None, ALU.mult).then_inc(chain, 1)
                    V.tensor_tensor(acc[:, k, TP:T], acc[:, k, TP:T], mod[:, GT_F + k, 1:], ALU.mult).then_inc(chain, 1)
                for k in range(KD):
                    dve.wait_ge(chain, 2 * k + 3)
                    V.scalar_tensor_tensor(x[:, k], x[:, k], ALPHA, acc[:, k], ALU.mult, ALU.add).then_inc(chain, 1)


def store_output(nc, io, sm, x, **_):
    with ExitStack() as ph:
        stored, = sm(ph, "y_stored")
        with nc.Block() as block:
            @block.sync
            def _(sp):
                sp.dma_start(io["y_out"], x[:]).then_inc(stored, 16)
                sp.wait_ge(stored, 17)


def _consts():
    import numpy as np
    t = np.zeros((P, NCONST), np.float32)

    def put(name, a):
        at, n = CONST[name]
        t[:, at:at + n] = a
    i64 = np.eye(HD)
    blocks = np.kron(np.eye(2), np.ones((HD, HD)))
    put("ident", np.eye(P))
    put("ident64", np.tile(i64, (2, 1)))
    put("headsum", blocks)
    put("mean", np.full((P, P), 1.0 / D))
    put("headmean", blocks / HD)
    r, c = np.arange(C)[:, None], np.arange(C)[None, :]
    put("upper", np.tile(c > r, (2, 1)))
    put("upper_incl", np.tile(c >= r, (2, 1)))
    put("first_u", np.tile((c == r + 1) & (r % 2 == 0), (2, 1)))
    put("first_l", np.tile((r == c + 1) & (c % 2 == 0), (2, 1)))
    for s in LEVELS:
        put(f"level{s}", np.tile((r // (2 * s) == c // (2 * s)) & (r % (2 * s) < s) & (c % (2 * s) >= s), (2, 1)))
    put("iota", np.tile(np.arange(P), (P, 1)))
    put("iota16", np.tile(np.arange(16), (P, 1)))
    put("ones", 1.0)
    put("ln_eps", LN_EPS)
    put("gn_eps", GN_EPS)
    return t


def _host_inputs(v):
    import numpy as np
    v = {k: np.asarray(a) for k, a in v.items()}

    def fm(a):
        return np.ascontiguousarray(a.T.reshape(-1, P, a.shape[0]).transpose(1, 0, 2))

    def colblocks(a, width=P):
        k, n = a.shape
        return np.ascontiguousarray(a.reshape(k // P, P, n // width, width).transpose(2, 1, 0, 3))

    def percol(a):
        return a.reshape(-1, P).T
    out = {}
    out["consts"] = _consts()
    out["x"] = fm(np.concatenate([v["x_prompt"][0], v["x_sample"][:, 0]]))
    out["c"] = fm(np.concatenate([v["c_prompt"], v["c_sample"]]))
    out["w_ada"] = colblocks(v["w_ada"][0], 512)
    vecs = np.zeros((P, NVEC), np.float32)
    for name, src in (("ln_in_g", "ln_in_g"), ("ln_in_b", "ln_in_b"), ("ln1_g", "ln1_g"), ("ln1_b", "ln1_b"),
                      ("ln2_g", "ln2_g"), ("ln2_b", "ln2_b"), ("b_ada", "b_ada"), ("mu", "mu_shift"),
                      ("w0", "rwkv_w0"), ("a0", "rwkv_a0"), ("k_k", "rwkv_k_k"), ("k_a", "rwkv_k_a"),
                      ("r_k", "rwkv_r_k"), ("gn_g", "rwkv_gn_g"), ("gn_b", "rwkv_gn_b")):
        at, n = VEC[name]
        vecs[:, at:at + n] = percol(v[src].reshape(-1))
    out["vecs"] = vecs
    blocks = colblocks(v["w_in"][0])
    order = [12, 13] + [b for p in range(NP) for b in (p, 4 + p, 8 + p)]
    out["w_in"] = np.ascontiguousarray(blocks[order])
    out["w_lora"] = np.ascontiguousarray(np.concatenate([v["rwkv_w2"][0], v["rwkv_a2"][0]]).reshape(P, NP, P).transpose(1, 0, 2))
    out["shift_before"] = fm(v["state_shift"][0])
    reset = np.ones((P, T), np.float32)
    reset[:, 0:TP:C] = 0.0
    reset[:, TP:] = 0.0
    out["reset"] = reset
    w = v["w_in"][0]
    q_at, k_at, v_at, ga_at, gb_at = 1792, 2304, 2432, 2560, 3584
    heads = [q_at + 64 * hd for c in range(NP) for hd in (c, 4 + c)]
    cols = np.concatenate([np.arange(a, a + 64) for a in heads] + [np.arange(k_at, v_at + 128)])
    gates = np.stack([colblocks(w[:, ga_at:gb_at]), colblocks(w[:, gb_at:])], 1).reshape(2 * KD, P, KD, P)
    out["w_side"] = np.ascontiguousarray(np.concatenate([colblocks(w[:, cols]), gates]))
    out["state_wkv"] = np.ascontiguousarray(
        v["state_wkv"][0].reshape(NS, NP, 2, HD, HD).transpose(2, 4, 1, 0, 3).reshape(P, NP, NS, HD))
    out["g2"] = np.ascontiguousarray(v["rwkv_g2"][0].reshape(P, NP, P))
    pa, pb_ = (colblocks(a) for a in (v["w_pa"][0], v["w_pb"][0].reshape(2, NP, HD, D).transpose(1, 0, 2, 3).reshape(-1, D)))
    out["w_merge"] = np.ascontiguousarray(np.concatenate([pa, pb_], axis=2))
    out["w_o"] = colblocks(v["w_o"][0])
    out["peer_wq"] = colblocks(v["peer_wq"][0])
    out["keys"] = np.ascontiguousarray(v["peer_sub_keys"][0].transpose(2, 0, 1))
    out["u"] = np.ascontiguousarray(v["peer_u"][0].reshape(NKEY, NKEY, KD, P).transpose(0, 3, 2, 1))
    out["v"] = v["peer_v"][0].reshape(NKEY, NKEY, D)
    slopes = 2.0 ** -np.arange(1.0, 9.0)
    rel = WIN + np.arange(WIN)[:, None] - np.arange(2 * WIN)[None, :]
    b = -slopes[None, :, None] * rel[:, None, :]
    b = np.where(((rel >= 0) & (rel <= WIN))[:, None, :], b, NEG)
    first = np.where(np.arange(2 * WIN) < WIN, NEG, b)
    out["att_bias"] = np.stack([first, b], 1).reshape(P, 2, -1).astype(np.float32)
    out["sinks"] = np.ascontiguousarray(np.broadcast_to(v["attn_sinks"][0], (P, NH)))
    out["k_cache"] = np.ascontiguousarray(v["cache_k_win"][0].reshape(NS, WIN, P).transpose(2, 0, 1))
    out["v_cache"] = np.ascontiguousarray(v["cache_v_win"][0].reshape(NS, WIN, P).transpose(1, 0, 2))
    sb_ = np.zeros((64, WIN + 2), np.float32)
    sb_[:, 0:WIN + 1] = np.tile(-slopes[:, None] * (WIN - np.arange(WIN + 1)), (NS, 1))
    sb_[:, WIN + 1] = np.tile(v["attn_sinks"][0], NS)
    out["sample_bias"] = sb_
    return out


_OUTS = {"shift_out": (P, 14, 1 + NS), "wkv_prompt_out": (P, NP, HD),
         "wkv_sample_out": (P, NP, NS, HD), "k_win_prompt_out": (P, WIN), "v_win_prompt_out": (P, WIN),
         "y_out": (P, KD, T), "k_win_sample_out": (P, NS, WIN), "v_win_sample_out": (WIN, NS, P)}


def kernel(**inputs):
    import numpy as np
    import concourse.bacc as bacc
    from concourse.bass_utils import run_bass_kernel_spmd

    nc = bacc.Bacc("TRN2", target_bir_lowering=False, num_devices=1)
    arrays = _host_inputs(inputs)
    io = {n: nc.dram_tensor("in_" + n, a.shape, mybir.dt.from_np(a.dtype), kind="ExternalInput").ap()
          for n, a in arrays.items()}
    io["x_saved"] = nc.dram_tensor("x_saved", [P, KD, T], F32, kind="Internal").ap()
    io["side_saved"] = nc.dram_tensor("side_saved", [P, SIDE, T], F32, kind="Internal").ap()
    io["gates"] = nc.dram_tensor("gates_saved", [P, NTB, NKEY, TB], F32, kind="Internal").ap()
    io["query_saved"] = nc.dram_tensor("query_saved", [P, 2 * NH, T], F32, kind="Internal").ap()
    io["hidden_saved"] = nc.dram_tensor("hidden_saved", [NKEY, P, T], F32, kind="Internal").ap()
    for n, shape in _OUTS.items():
        io[n] = nc.dram_tensor("out_" + n, shape, F32, kind="ExternalOutput").ap()
    kernel_program(nc, io)
    r = run_bass_kernel_spmd(nc, [{"in_" + n: a for n, a in arrays.items()}], core_ids=[0]).results[0]

    def rows(a):
        return a.transpose(2, 1, 0).reshape(a.shape[2], -1)

    out = {n: np.asarray(r["out_" + n]) for n in _OUTS}
    y = rows(out["y_out"])
    shift = rows(out["shift_out"])
    wkv_p = out["wkv_prompt_out"].reshape(2, HD, NP, HD).transpose(2, 0, 3, 1).reshape(1, 1, 8, HD, HD)
    wkv_s = out["wkv_sample_out"].reshape(2, HD, NP, NS, HD).transpose(3, 2, 0, 4, 1).reshape(1, NS, 8, HD, HD)
    k_p, v_p = (out[f"{n}_win_prompt_out"].T.reshape(1, 1, WIN, 2, HD) for n in "kv")
    k_s = out["k_win_sample_out"].transpose(1, 2, 0).reshape(1, NS, WIN, 2, HD)
    v_s = out["v_win_sample_out"].transpose(1, 0, 2).reshape(1, NS, WIN, 2, HD)
    return (y[:TP][None], y[TP:][:, None], wkv_p, wkv_s, shift[0][None, None], shift[1:][None], k_p, k_s, v_p, v_s)
```

```python
from contextlib import ExitStack

import concourse.bass as bass
from concourse import mybir

F32 = mybir.dt.float32
F32R = mybir.dt.float32r
BF16 = mybir.dt.bfloat16
U32 = mybir.dt.uint32
ALU = mybir.AluOpType
ACT = mybir.ActivationFunctionType
AX_X = mybir.AxisListType.X

P = 128
D = 1024
KD = D // P
TP = 1024
NS = 8
T = TP + NS
NT = 3
TN = T // NT
HD = 64
NP = 4
NMOD = 48
C = 64
NC = TP // C
DECAY = 0.6065306597126334
ALPHA = 2.0 ** 0.25
LN_EPS = 1e-5
GN_EPS = 64e-5
WIN = 128
NB = TP // WIN
NEG = -1e30
NH = 8
TOPK = 16
NKEY = 128
SCALE = HD ** -0.5

CONST = {}
VEC = {}


def _layout(table, names):
    at = 0
    for name, n in names:
        table[name] = (at, n)
        at += n
    return at


LEVELS = (2, 4, 8, 16, 32)
NCONST = _layout(CONST, [("ident", 128), ("ident64", 64), ("headsum", 128), ("mean", 128), ("headmean", 128),
                         ("upper", 64), ("upper_incl", 64), ("first_u", 64), ("first_l", 64)]
                 + [(f"level{s}", 64) for s in LEVELS]
                 + [("iota", 128), ("iota16", 16), ("ones", 1), ("ln_eps", 1), ("gn_eps", 1)])
NVEC = _layout(VEC, [("ln_in_g", 8), ("ln_in_b", 8), ("ln_1_g", 8), ("ln_1_b", 8), ("ln_2_g", 8), ("ln_2_b", 8),
                     ("b_ada", NMOD), ("mu", 14), ("w0", 4), ("a0", 4), ("k_k", 4), ("k_a", 4), ("r_k", 4),
                     ("gn_g", 4), ("gn_b", 4)])
SH_M, SC_M, GT_M, SH_F, SC_F, GT_F = (8 * i for i in range(6))


def carry(eng, sem):
    eng.sem_inc(sem, 1)


class Chain:

    def __init__(self, eng, sem):
        self.eng, self.sem, self.base, self.n = eng, sem, 0, 0

    def __call__(self, ins):
        self.n += 1
        ins.then_inc(self.sem, 1)
        self.eng.wait_ge(self.sem, self.base + self.n + 1)

    def enter(self, i, per):
        self.start = self.base + self.n
        self.base, self.n, self.per = i * per + self.start, 0, per

    def leave(self, turns):
        assert self.n == self.per, f"links per turn: {self.n}, not {self.per}"
        self.base, self.n = self.start + turns * self.per, 0


def kernel_program(nc, io):
    with ExitStack() as top:
        def sb(stack, name, shape, dt=F32):
            return stack.enter_context(nc.sbuf_tensor(name, shape, dt))

        def pb(stack, name, shape, dt=F32):
            return stack.enter_context(nc.psum_tensor(name, shape, dt))

        def sm(stack, *names):
            sems = [nc.alloc_semaphore(n) for n in names]
            for s in sems:
                nc.gpsimd.sem_inc(s, 1)
            nc.all_engine_barrier()
            stack.callback(nc.clear_and_free_semaphores, sems)
            return sems

        consts = sb(top, "consts", [P, NCONST])
        vecs = sb(top, "vecs", [P, NVEC])
        mod = sb(top, "mod", [P, NMOD, 1 + NS])
        x = sb(top, "x", [P, KD, T])
        env = dict(nc=nc, io=io, sb=sb, pb=pb, sm=sm, consts=consts, vecs=vecs, mod=mod, x=x)

        with ExitStack() as mix:
            env["h"] = sb(mix, "h", [P, KD, T])
            modulation_and_input(**env)
            env["ya"] = sb(mix, "ya", [P, NP, T])
            env["ob"] = sb(mix, "ob", [P, NP, T])
            with ExitStack() as rw:
                for n in ("kt", "kh", "bh", "vt"):
                    env[n] = sb(rw, n, [P, NP, T])
                env["sgd"] = sb(rw, "sgd", [P, T])
                env["pc"] = sb(rw, "pc", [P, NP, NC])
                env["ws"] = sb(rw, "ws", [P, NP, NS])
                rwkv_inputs(**env)
                rwkv_scan(**env)
                rwkv_samples(**env)
            attention(**env)
            for n in ("mh", "ml"):
                env[n] = sb(mix, n, [P, KD, T], F32R)
            merge(**env)
            mixer_output(**env)
        with ExitStack() as pr:
            env["hh"] = sb(pr, "hh", [P, KD, T], F32R)
            env["hl"] = sb(pr, "hl", [P, KD, T], F32R)
            with ExitStack() as q:
                env["h"] = sb(q, "h_peer", [P, KD, T])
                layernorm(**env, name="1", modulate=(SC_F, SH_F))
                split_input(**env)
                peer_queries(**env)
            env["slots"] = sb(pr, "slots", [P, 3, T])
            peer_select(**env)
            peer_gates(**env)
        with ExitStack() as ex:
            acc = sb(ex, "acc", [P, KD, T])
            peer_experts(**env, acc=acc)
            peer_output(**env, acc=acc)
        del env["h"]
        layernorm(**env, name="2", out=io["y_out"])


def col(consts, name):
    at, n = CONST[name]
    return consts[:, at:at + n]


def vec(vecs, name, k=None):
    at, n = VEC[name]
    return vecs[:, at:at + n] if k is None else vecs[:, at + k:at + k + 1]


def modulation_and_input(nc, io, sb, pb, sm, consts, vecs, mod, x, h, **_):
    TURNS, SLOTS = 6, 2
    with ExitStack() as ph:
        c = sb(ph, "c", [P, KD, 1 + NS])
        c_sig = sb(ph, "c_sig", [P, KD, 1 + NS])
        slab = sb(ph, "slab", [P, SLOTS, KD, 512])
        row = sb(ph, "row", [1 + NS, SLOTS, 512])
        row_ps = [pb(ph, f"row_ps{s}", [1 + NS, 512]) for s in range(SLOTS)]
        turned_ps = [pb(ph, f"turned_ps{s}", [P, 4, 1 + NS]) for s in range(SLOTS)]
        (c_loaded, small_loaded, x_loaded, slab0_loaded, slab1_loaded, sig_ready, silu_ready, slab_free,
         row_summed, row_free, row_ready, turned, turned_free, scales_ready, carried) = sm(
            ph, "c_loaded", "small_loaded", "x_loaded", "slab0_loaded", "slab1_loaded", "sig_ready", "silu_ready",
            "slab_free", "row_summed", "row_free", "row_ready", "turned", "turned_free", "scales_ready", "mod_carried")
        slab_loaded = (slab0_loaded, slab1_loaded)
        norm = Norm(nc, sb, pb, sm, ph, consts, vecs, x, "in")

        def turns(eng, turn, first, second):
            turn(0)
            first(eng)
            turn(1)
            second(eng)
            with eng.Fori(2, TURNS) as i:
                turn(i)

        with nc.Block() as block:
            @block.sync
            def _(sp):
                sp.dma_start(c[:], io["c"]).then_inc(c_loaded, 16)
                sp.dma_start(vecs[:], io["vecs"]).then_inc(small_loaded, 16)
                sp.dma_start(consts[:], io["consts"]).then_inc(small_loaded, 16)

                def turn(i):
                    for s in range(SLOTS):
                        sp.wait_ge(slab_free, i * SLOTS + s + 2)
                        sp.dma_start(slab[:, s], io["w_ada"][bass.ds(i * SLOTS + s, 1)].rearrange(
                            "o p k n -> p (o k) n")).then_inc(slab_loaded[s], 16)
                turn(0)
                sp.dma_start(x[:], io["x"]).then_inc(x_loaded, 16)
                with sp.Fori(1, TURNS) as i:
                    turn(i)

            @block.scalar
            def _(act):
                act.wait_ge(c_loaded, 17)
                nc.scalar.activation(c_sig[:], c[:], ACT.Sigmoid).then_inc(sig_ready, 1)

                def turn(i):
                    for s in range(SLOTS):
                        act.wait_ge(row_summed, i * SLOTS + s + 2)
                        act.wait_ge(row_free, i * SLOTS + s + 2)
                        nc.scalar.activation(row[:, s], row_ps[s][:], ACT.Copy).then_inc(row_ready, 1)
                turns(act, turn, norm.copy_and_square, norm.roots)
                act.wait_ge(scales_ready, 3)
                norm.modulate_prompt(act, mod, h, SC_M, SH_M)

            @block.vector
            def _(dve):
                dve.sem_inc(slab_free, SLOTS)
                dve.sem_inc(row_free, SLOTS)
                dve.wait_ge(sig_ready, 2)
                nc.vector.tensor_tensor(c[:], c[:], c_sig[:], ALU.mult).then_inc(silu_ready, 1)
                dve.wait_ge(small_loaded, 33)

                def turn(i):
                    for s in range(SLOTS):
                        dve.wait_ge(turned, i * SLOTS + s + 2)
                        at = VEC["b_ada"][0]
                        bias = vecs[:, bass.ds(i * (4 * SLOTS) + (4 * s + at), 4)].unsqueeze(2).to_broadcast([P, 4, 1 + NS])
                        nc.vector.tensor_tensor(mod[:, bass.ds(i * (4 * SLOTS) + 4 * s, 4), :], turned_ps[s][:], bias,
                                                ALU.add).then_inc(turned_free, 1)
                turns(dve, turn, norm.centre, norm.scale)
                dve.wait_ge(turned_free, TURNS * SLOTS + 1)
                for m in (SC_M, SC_F):
                    nc.vector.tensor_scalar_add(mod[:, m:m + 8, :], mod[:, m:m + 8, :], 1.0).then_inc(scales_ready, 1)
                dve.wait_ge(scales_ready, 3)
                norm.modulate_samples(dve, mod, h, SC_M, SH_M)

            @block.tensor
            def _(pe):
                pe.wait_ge(silu_ready, 2)
                pe.wait_ge(small_loaded, 33)

                def turn(i):
                    for s in range(SLOTS):
                        pe.wait_ge(slab_loaded[s], i * 16 + 17)
                        if s == 0:
                            pe.wait_ge(row_ready, i * SLOTS + 1)
                        for k in range(KD):
                            mm = nc.tensor.matmul(row_ps[s][:], c[:, k], slab[:, s, k], start=k == 0, stop=k == KD - 1)
                        mm.then_inc(row_summed, 1)
                        pe.wait_ge(row_summed, i * SLOTS + s + 2)
                        pe.sem_inc(slab_free, 1)
                    for s in range(SLOTS):
                        pe.wait_ge(row_ready, i * SLOTS + s + 2)
                        pe.wait_ge(turned_free, i * SLOTS + 1)
                        carry(pe, carried)
                        for j in range(4):
                            mm = nc.tensor.transpose(turned_ps[s][:, j], row[:, s, j * P:(j + 1) * P],
                                                     col(consts, "ident")[0:1 + NS, 0:1 + NS])
                        mm.then_inc(turned, 1)
                        pe.wait_ge(turned, i * SLOTS + s + 2)
                        pe.sem_inc(row_free, 1)

                def means(pe):
                    pe.wait_ge(x_loaded, 17)
                    norm.sum_means(pe)
                turns(pe, turn, means, norm.sum_squares)


class Norm:

    def __init__(self, nc, sb, pb, sm, ph, consts, vecs, x, name):
        self.nc, self.consts, self.vecs, self.x, self.name = nc, consts, vecs, x, name
        self.mean = sb(ph, f"mean_{name}", [P, NT, TN])
        self.rstd = sb(ph, f"rstd_{name}", [P, NT, TN])
        self.square = sb(ph, f"square_{name}", [P, NT, KD, TN])
        self.mean_ps = [pb(ph, f"mean_ps{s}_{name}", [P, 512]) for s in range(2)]
        self.var_ps = [pb(ph, f"var_ps{s}_{name}", [P, 512]) for s in range(2)]
        (self.mean_summed, self.mean_ready, self.centred, self.squared, self.var_summed, self.std_ready, self.scaled,
         self.chain, self.modulated, self.modulated_samples) = sm(
            ph, *(f"{n}_{name}" for n in ("mean_summed", "mean_ready", "centred", "squared", "var_summed", "std_ready",
                                          "scaled", "ln_chain", "modulated", "samples_modulated")))

    def tile(self, t):
        return self.x[:, :, t * TN:(t + 1) * TN]

    def sums(self, out, src):
        for k in range(KD):
            mm = self.nc.tensor.matmul(out[:, 0:TN], col(self.consts, "mean"), src[:, k], start=k == 0, stop=k == KD - 1)
        return mm

    def sum_means(self, pe):
        for t in range(NT):
            if t >= 2:
                pe.wait_ge(self.mean_ready, t)
            self.sums(self.mean_ps[t % 2], self.tile(t)).then_inc(self.mean_summed, 1)

    def sum_squares(self, pe):
        for t in range(NT):
            pe.wait_ge(self.squared, t + 2)
            if t >= 2:
                pe.wait_ge(self.std_ready, t)
            self.sums(self.var_ps[t % 2], self.square[:, t]).then_inc(self.var_summed, 1)

    def copy_and_square(self, act):
        for t in range(NT):
            act.wait_ge(self.mean_summed, t + 2)
            self.nc.scalar.activation(self.mean[:, t], self.mean_ps[t % 2][:, 0:TN], ACT.Copy).then_inc(self.mean_ready, 1)
        for t in range(NT):
            act.wait_ge(self.centred, t + 2)
            self.nc.scalar.activation(self.square[:, t], self.tile(t), ACT.Square).then_inc(self.squared, 1)

    def roots(self, act):
        for t in range(NT):
            act.wait_ge(self.var_summed, t + 2)
            self.nc.scalar.activation(self.rstd[:, t], self.var_ps[t % 2][:, 0:TN], ACT.Sqrt,
                                      bias=col(self.consts, "ln_eps")).then_inc(self.std_ready, 1)

    def centre(self, dve):
        for t in range(NT):
            dve.wait_ge(self.mean_ready, t + 2)
            self.nc.vector.tensor_tensor(self.tile(t), self.tile(t), self.mean[:, t].unsqueeze(1).to_broadcast([P, KD, TN]),
                                         ALU.subtract).then_inc(self.centred, 1)

    def scale(self, dve):
        link = Chain(dve, self.chain)
        V = self.nc.vector
        for t in range(NT):
            dve.wait_ge(self.std_ready, t + 2)
            link(V.reciprocal(self.rstd[:, t], self.rstd[:, t]))
            link(V.tensor_tensor(self.tile(t), self.tile(t), self.rstd[:, t].unsqueeze(1).to_broadcast([P, KD, TN]), ALU.mult))
            for k in range(KD):
                xk = self.tile(t)[:, k]
                V.tensor_scalar(xk, xk, vec(self.vecs, f"ln_{self.name}_g", k), vec(self.vecs, f"ln_{self.name}_b", k),
                                ALU.mult, ALU.add).then_inc(self.scaled, 1)

    def modulate_prompt(self, act, mod, h, sc, sh):
        for t in range(NT):
            tok = slice(t * TN, min((t + 1) * TN, TP))
            act.wait_ge(self.scaled, (t + 1) * KD + 1)
            for k in range(KD):
                self.nc.scalar.activation(h[:, k, tok], self.x[:, k, tok], ACT.Identity, scale=mod[:, sc + k, 0:1],
                                          bias=mod[:, sh + k, 0:1]).then_inc(self.modulated, 1)

    def modulate_samples(self, dve, mod, h, sc, sh):
        link = Chain(dve, self.modulated_samples)
        V = self.nc.vector
        dve.wait_ge(self.scaled, NT * KD + 1)
        link(V.tensor_tensor(h[:, :, TP:T], self.x[:, :, TP:T], mod[:, sc:sc + KD, 1:], ALU.mult))
        link(V.tensor_tensor(h[:, :, TP:T], h[:, :, TP:T], mod[:, sh:sh + KD, 1:], ALU.add))


def layernorm(nc, sb, pb, sm, consts, vecs, mod, x, name, h=None, modulate=None, out=None, **_):
    with ExitStack() as ph:
        norm = Norm(nc, sb, pb, sm, ph, consts, vecs, x, name)
        stored, = sm(ph, f"stored_{name}")
        with nc.Block() as block:
            @block.tensor
            def _(pe):
                norm.sum_means(pe)
                norm.sum_squares(pe)

            @block.scalar
            def _(act):
                norm.copy_and_square(act)
                norm.roots(act)
                if modulate:
                    norm.modulate_prompt(act, mod, h, *modulate)

            @block.vector
            def _(dve):
                norm.centre(dve)
                norm.scale(dve)
                if modulate:
                    norm.modulate_samples(dve, mod, h, *modulate)

            if out is not None:
                @block.sync
                def _(sp):
                    for t in range(NT):
                        sp.wait_ge(norm.scaled, (t + 1) * KD + 1)
                        sp.dma_start(out[:, :, t * TN:(t + 1) * TN], norm.tile(t)).then_inc(stored, 16)
                    sp.wait_ge(stored, NT * 16 + 1)


def rwkv_inputs(nc, io, sb, pb, sm, consts, vecs, mod, x, h, ya, ob, kt, kh, bh, vt, sgd, pc, ws, **_):
    with ExitStack() as ph:
        w = sb(ph, "w", [P, 3, KD, P])
        w_small = sb(ph, "w_small", [P, P])
        before = sb(ph, "before", [P, 14, NS])
        last = sb(ph, "last", [P, 14, 1 + NS])
        reset = sb(ph, "reset", [P, T])
        room = x[:].rearrange("p k n -> p (k n)")
        raw = [room[:, q * (1 + T):(q + 1) * (1 + T)] for q in range(3)]
        lora, tmp, sz = (room[:, 3 * (1 + T) + q * T:3 * (1 + T) + (q + 1) * T] for q in range(3))
        a = raw[0]
        norm, decay = raw[1], raw[2]
        one_minus_ka = sb(ph, "one_minus_ka", [P, NP])
        ps = [pb(ph, f"ps{s}", [P, NT, 512]) for s in range(2)]
        (loaded, w0_loaded, w1_loaded, w2_loaded, ws_loaded, w_free, summed, taken, mixed, tanh_ready, sq_ready,
         rk_ready, scan_ready, exp_ready, exp_used, bonus_taken, turn_done, small_free, chain, out_done, x_saved) = sm(
            ph, "loaded", "w0_loaded", "w1_loaded", "w2_loaded", "ws_loaded", "w_free", "summed", "taken", "mixed",
            "tanh_ready", "sq_ready", "rk_ready", "scan_ready", "exp_ready", "exp_used", "bonus_taken",
            "turn_done", "small_free", "in_chain", "out_done", "x_saved")
        w_loaded = (w0_loaded, w1_loaded, w2_loaded)

        def tiles(buf):
            return buf[:].rearrange("p (t n) -> p t n", t=NT)

        with nc.Block() as block:
            @block.sync
            def _(sp):
                sp.dma_start(io["x_saved"], x[:]).then_inc(x_saved, 16)
                sp.dma_start(before[:], io["shift_before"]).then_inc(loaded, 16)
                sp.dma_start(reset[:], io["reset"]).then_inc(loaded, 16)
                for q in range(2):
                    sp.dma_start(w[:, q], io["w_in"][q]).then_inc(w_loaded[q], 16)
                with sp.Fori(0, NP) as p:
                    sp.wait_ge(w_free, p * 5 + 3)
                    for q in range(3):
                        sp.dma_start(w[:, q], io["w_in"][bass.ds(p * 3 + (2 + q), 1)].rearrange(
                            "o p k n -> p (o k) n")).then_inc(w_loaded[q], 16)
                    sp.dma_start(w_small[:], io["w_lora"][bass.ds(p, 1)].rearrange("o p n -> p (o n)"))\
                        .then_inc(ws_loaded, 16)
                sp.wait_ge(turn_done, NP + 1)
                sp.dma_start(io["shift_out"], last[:]).then_inc(out_done, 16)
                sp.wait_ge(out_done, 17)

            @block.tensor
            def _(pe):
                def project(q, s):
                    for t in range(NT):
                        for k in range(KD):
                            mm = nc.tensor.matmul(ps[s][:, t, 0:TN], w[:, q, k], h[:, k, t * TN:(t + 1) * TN],
                                                  start=k == 0, stop=k == KD - 1)
                    return mm

                for q in range(2):
                    pe.wait_ge(w_loaded[q], 17)
                    project(q, q).then_inc(summed, 1)
                    pe.wait_ge(summed, q + 2)
                    pe.sem_inc(w_free, 1)
                pe.wait_ge(tanh_ready, 2)
                with pe.Fori(0, NP) as p:
                    for q in range(3):
                        pe.wait_ge(w_loaded[q], p * 16 + (33 if q < 2 else 17))
                        if q == 0:
                            pe.wait_ge(bonus_taken, p + 1)
                        pe.wait_ge(taken, p * 6 + (3, 3, 4)[q])
                        project(q, q % 2).then_inc(summed, 1)
                        pe.wait_ge(summed, p * 7 + (q + 4))
                        pe.sem_inc(w_free, 1)
                    pe.wait_ge(ws_loaded, p * 16 + 17)
                    pe.wait_ge(taken, p * 6 + 5)
                    for t in range(NT):
                        mm = nc.tensor.matmul(ps[1][:, t, 0:TN], w_small[0:HD], lora[0:HD, t * TN:(t + 1) * TN],
                                              start=True, stop=True)
                    mm.then_inc(summed, 1)
                    pe.wait_ge(taken, p * 6 + 6)
                    for t in range(NT):
                        mm = nc.tensor.matmul(ps[0][:, t, 0:TN], w_small[HD:P], lora[HD:P, t * TN:(t + 1) * TN],
                                              start=True, stop=True)
                    mm.then_inc(summed, 1)
                    pe.wait_ge(summed, p * 7 + 8)
                    pe.sem_inc(w_free, 2)
                    pe.wait_ge(taken, p * 6 + 7)
                    pe.wait_ge(sq_ready, p + 2)
                    for t in range(NT):
                        mm = nc.tensor.matmul(ps[1][:, t, 0:TN], col(consts, "headsum"), tmp[:, t * TN:(t + 1) * TN],
                                              start=True, stop=True)
                    mm.then_inc(summed, 1)
                    pe.wait_ge(taken, p * 6 + 8)
                    pe.wait_ge(rk_ready, p + 2)
                    for t in range(NT):
                        mm = nc.tensor.matmul(ps[0][:, t, 0:TN], col(consts, "headsum"), tmp[:, t * TN:(t + 1) * TN],
                                              start=True, stop=True)
                    mm.then_inc(summed, 1)

            @block.scalar
            def _(act):
                act.wait_ge(x_saved, 17)
                for q in range(2):
                    act.wait_ge(summed, q + 2)
                    nc.scalar.activation(raw[q][:, 1:].rearrange("p (t n) -> p t n", t=NT), ps[q][:, :, 0:TN], ACT.Copy)\
                        .then_inc(taken, 1)
                act.wait_ge(mixed, 2)
                nc.scalar.activation(lora[0:HD], lora[0:HD], ACT.Tanh).then_inc(tanh_ready, 1)
                act.wait_ge(mixed, 3)
                nc.scalar.activation(sgd[:], sgd[:], ACT.Sigmoid).then_inc(tanh_ready, 1)
                with act.Fori(0, NP) as p:
                    act.wait_ge(turn_done, p + 1)
                    for q in range(3):
                        act.wait_ge(summed, p * 7 + (q + 4))
                        nc.scalar.activation(raw[q][:, 1:].rearrange("p (t n) -> p t n", t=NT), ps[q % 2][:, :, 0:TN],
                                             ACT.Copy).then_inc(taken, 1)
                    act.wait_ge(summed, p * 7 + 7)
                    nc.scalar.activation(tiles(sz), ps[1][:, :, 0:TN], ACT.Sigmoid,
                                         bias=vecs[:, bass.ds(p + VEC["w0"][0], 1)]).then_inc(taken, 1)
                    act.wait_ge(summed, p * 7 + 8)
                    act.wait_ge(mixed, p * 3 + 4)
                    nc.scalar.activation(a[:, 1:].rearrange("p (t n) -> p t n", t=NT), ps[0][:, :, 0:TN], ACT.Sigmoid,
                                         bias=vecs[:, bass.ds(p + VEC["a0"][0], 1)]).then_inc(taken, 1)
                    act.wait_ge(summed, p * 7 + 9)
                    act.wait_ge(mixed, p * 3 + 5)
                    nc.scalar.activation(norm[:, 1:].rearrange("p (t n) -> p t n", t=NT), ps[1][:, :, 0:TN], ACT.Sqrt)\
                        .then_inc(taken, 1)
                    act.wait_ge(mixed, p * 3 + 6)
                    for n, sign in enumerate((-DECAY, DECAY, -DECAY)):
                        act.wait_ge(scan_ready, p * 2 + (2, 2, 3)[n])
                        if n:
                            act.wait_ge(exp_used, p * 2 + n + 1)
                        nc.scalar.activation(decay[:, 1:], sz[:], ACT.Exp, scale=sign).then_inc(exp_ready, 1)

            @block.gpsimd
            def _(pool):
                pool.wait_ge(x_saved, 17)
                for q in range(3):
                    nc.gpsimd.memset(raw[q][:, 0:1], 0.0).then_inc(small_free, 1)

            @block.vector
            def _(dve):
                link = Chain(dve, chain)
                V = nc.vector

                def mix(q, dst, m):
                    mu = vecs[:, bass.ds(m + VEC["mu"][0], 1)] if not isinstance(m, int) else vec(vecs, "mu", m)
                    m_ = bass.ds(m, 1)
                    V.tensor_tensor(tmp[:, 0:TP], raw[q][:, 0:TP], raw[q][:, 1:1 + TP], ALU.subtract).then_inc(chain, 1)
                    link.n += 1
                    V.tensor_copy(last[:, m_, :], raw[q][:, TP:1 + T].unsqueeze(1)).then_inc(chain, 1)
                    link.n += 1
                    link(V.tensor_tensor(tmp[:, TP:T].unsqueeze(1), before[:, m_, :], raw[q][:, 1 + TP:1 + T].unsqueeze(1),
                                         ALU.subtract))
                    ins = V.scalar_tensor_tensor(dst, tmp[:], mu, raw[q][:, 1:], ALU.mult, ALU.add)
                    ins.then_inc(mixed, 1)

                dve.wait_ge(loaded, 33)
                dve.wait_ge(small_free, 4)
                link(V.tensor_scalar(one_minus_ka[:], vec(vecs, "k_a"), -1.0, 1.0, ALU.mult, ALU.add))
                for q in range(2):
                    dve.wait_ge(taken, q + 2)
                    mix(q, (lora, sgd)[q][:], 12 + q)
                    dve.wait_ge(mixed, q + 2)
                with dve.Fori(0, NP) as p:
                    link.enter(p, 25)

                    def at(t):
                        return t[:, bass.ds(p, 1), :].rearrange("p o n -> p (o n)")

                    def prompt(t):
                        return t[:, bass.ds(p, 1), 0:TP].rearrange("p o n -> p (o n)")

                    def feature(name):
                        return vecs[:, bass.ds(p + VEC[name][0], 1)]

                    for q, dst in enumerate((ya, kh, vt)):
                        dve.wait_ge(taken, p * 6 + (q + 4))
                        mix(q, at(dst), p + 4 * q)
                        dve.wait_ge(mixed, p * 3 + (q + 4))
                    link(V.tensor_scalar(at(kt), at(kh), feature("k_k"), None, ALU.mult))
                    V.tensor_tensor(tmp[:], at(kt), at(kt), ALU.mult).then_inc(sq_ready, 1)
                    dve.wait_ge(taken, p * 6 + 7)
                    link(V.tensor_tensor_scan(decay[:, 1:], reset[:], sz[:], 0.0, ALU.mult, ALU.add))
                    dve.wait_ge(taken, p * 6 + 8)
                    dve.wait_ge(sq_ready, p + 2)
                    link(V.tensor_scalar(at(bh), a[:, 1:], feature("k_a"), one_minus_ka[:, bass.ds(p, 1)], ALU.mult, ALU.add))
                    link(V.tensor_tensor(at(kh), at(kh), at(bh), ALU.mult))
                    dve.wait_ge(taken, p * 6 + 9)
                    ins = V.scalar_tensor_tensor(tmp[:], at(ya), feature("r_k"), at(kh), ALU.mult, ALU.mult)
                    ins.then_inc(rk_ready, 1)
                    link(V.tensor_scalar_max(norm[:, 1:], norm[:, 1:], 1e-12))
                    dve.wait_ge(summed, p * 7 + 10)
                    ins = V.tensor_tensor(at(ob).rearrange("p (t n) -> p t n", t=NT), ps[0][:, :, 0:TN],
                                          at(vt).rearrange("p (t n) -> p t n", t=NT), ALU.mult)
                    ins.then_inc(bonus_taken, 1)
                    link(V.reciprocal(norm[:, 1:], norm[:, 1:]))
                    link(V.tensor_tensor(at(kt), at(kt), norm[:, 1:], ALU.mult))
                    link(V.tensor_tensor(at(bh), at(kt), a[:, 1:], ALU.mult))
                    link(V.tensor_tensor(norm[:, 1:], decay[:, 1:], sz[:], ALU.subtract))
                    ins = V.tensor_copy(sz[:], decay[:, 1:])
                    ins.then_inc(scan_ready, 1)
                    dve.wait_ge(exp_ready, p * 3 + 2)
                    V.tensor_tensor(prompt(ya), prompt(ya), decay[:, 1:1 + TP], ALU.mult).then_inc(chain, 1)
                    link.n += 1
                    V.tensor_copy(ws[:, bass.ds(p, 1), :], decay[:, 1 + TP:1 + T].unsqueeze(1)).then_inc(chain, 1)
                    link.n += 1
                    link(V.tensor_copy(pc[:, bass.ds(p, 1), :], decay[:, 1:1 + TP].rearrange("p (c s) -> p c s", s=C)[:, :, C - 1].unsqueeze(1)))
                    dve.sem_inc(exp_used, 1)
                    dve.wait_ge(exp_ready, p * 3 + 3)
                    V.tensor_tensor(prompt(bh), prompt(bh), decay[:, 1:1 + TP], ALU.mult).then_inc(chain, 1)
                    link.n += 1
                    link(V.tensor_tensor(prompt(kh), prompt(kh), decay[:, 1:1 + TP], ALU.mult))
                    link(V.tensor_copy(sz[:], norm[:, 1:]))
                    dve.sem_inc(scan_ready, 1)
                    dve.sem_inc(exp_used, 1)
                    dve.wait_ge(exp_ready, p * 3 + 4)
                    link(V.tensor_tensor(prompt(kt), prompt(kt), decay[:, 1:1 + TP], ALU.mult))
                    dve.wait_ge(rk_ready, p + 2)
                    dve.wait_ge(bonus_taken, p + 2)
                    dve.sem_inc(turn_done, 1)
                    link.leave(NP)


SIDE = 6 + 2 * KD


class Side:

    def __init__(self, nc, io, sb, pb, sm, ph, h, first, tag):
        self.nc, self.io, self.h, self.first = nc, io, h, first
        self.w = sb(ph, f"w_side_{tag}", [P, KD, P])
        self.out = sb(ph, f"side_{tag}", [P, NT, TN])
        self.ps = pb(ph, f"side_ps_{tag}", [P, 512])
        self.loaded, self.summed, self.taken, self.stored = sm(
            ph, *(f"side_{n}_{tag}" for n in ("loaded", "summed", "taken", "stored")))

    def load(self, sp, n):
        sp.wait_ge(self.summed, n * NT + 1)
        sp.dma_start(self.w[:], self.io["w_side"][bass.ds(n + self.first, 1)].rearrange("o p k n -> p (o k) n"))\
            .then_inc(self.loaded, 16)

    def store(self, sp, n):
        sp.wait_ge(self.taken, n * NT + (NT + 1))
        sp.dma_start(self.io["side_saved"][:, bass.ds(n + self.first, 1), :].rearrange("p o n -> p (o n)"),
                     self.out[:].rearrange("p t n -> p (t n)")).then_inc(self.stored, 16)

    def transfer(self, sp, count):
        sp.sem_inc(self.stored, 16)
        self.load(sp, 0)
        with sp.Fori(0, count - 1) as n:
            self.load(sp, n + 1)
            self.store(sp, n)
        self.store(sp, count - 1)
        sp.wait_ge(self.stored, count * 16 + 17)

    def multiply(self, pe, n, products):
        for at in products:
            t, k = at // KD, at % KD
            if at == 0:
                pe.wait_ge(self.loaded, n * 16 + 17)
            if k == 0:
                pe.wait_ge(self.taken, n * NT + (t + 1))
            mm = self.nc.tensor.matmul(self.ps[:, 0:TN], self.w[:, k], self.h[:, k, t * TN:(t + 1) * TN],
                                       start=k == 0, stop=k == KD - 1)
            if k == KD - 1:
                mm.then_inc(self.summed, 1)

    def take(self, act, n, t):
        act.wait_ge(self.summed, n * NT + (t + 2))
        if t == 0:
            act.wait_ge(self.stored, n * 16 + 17)
        self.nc.scalar.activation(self.out[:, t], self.ps[:, 0:TN], ACT.Copy).then_inc(self.taken, 1)


def rwkv_scan(nc, io, sb, pb, sm, consts, x, h, ya, kt, kh, bh, vt, pc, **_):
    NL = len(LEVELS)
    with ExitStack() as ph:
        room = x[:].rearrange("p k n -> p (k n)")
        at = [0]

        def rows(*shape):
            n = 1
            for v in shape:
                n *= v
            ap = room[:, at[0]:at[0] + n]
            at[0] += n
            if len(shape) == 3:
                ap = ap.rearrange("p (a b c) -> p a b c", a=shape[0], b=shape[1])
            elif len(shape) == 2:
                ap = ap.rearrange("p (a b) -> p a b", a=shape[0])
            return ap

        kr = [rows(NP, 2, C) for _ in range(2)]
        bhc, khc, vtc = rows(NP, C), rows(NP, C), rows(NP, C)
        tb_up = rows(NP, C)
        tk_up, ab_up, ak_up = ([rows(NP, C) for _ in range(2)] for _ in range(3))
        inv = [rows(2, NP, C) for _ in range(2)]
        level = rows(NL, NP, C)
        q_sb = sb(ph, "q_sb", [P, NP, C])
        tok = [rows(3, NP, C) for _ in range(2)]
        rhs, sa, state = rows(NP, C), rows(NP, C), rows(NP, C)
        b_ps = pb(ph, "b_ps", [P, NP, 2, C])
        k_ps = pb(ph, "k_ps", [P, NP, 2, C])
        t_ps = pb(ph, "t_ps", [P, 2, NP, C])
        tok_ps = pb(ph, "tok_ps", [P, 4, NP, C])
        q_ps = tok_ps[:, 3]
        inv_ps = pb(ph, "inv_ps", [P, 2, NP, C])
        seq_ps = pb(ph, "seq_ps", [P, 2, NP, C])
        (staged, scores, masked, tok_turned, tok_ready, levels_ready, q_summed, q_ready, inv_summed, inv_grown,
         rhs_summed, rhs_ready, sa_summed, sa_ready, out_summed, y_ready, state_ready, chain, saved, carried) = sm(
            ph, "staged", "scores", "masked", "tok_turned", "tok_ready", "levels_ready", "q_summed", "q_ready",
            "inv_summed", "inv_grown", "rhs_summed", "rhs_ready", "sa_summed", "sa_ready", "out_summed", "y_ready",
            "state_ready", "scan_chain", "state_saved", "scan_carried")
        side = Side(nc, io, sb, pb, sm, ph, h, 0, "scan")
        halves = [slice(0, HD), slice(HD, P)]

        def mask(name, n=NP):
            return col(consts, name).unsqueeze(1).to_broadcast([P, n, C])

        def chunk(t, c):
            return t[:, :, bass.ds(c * C, C)]

        PAUSES = (3, 1, 4, 2, 2, 2, 2, 2, 2, 2, 2)
        assert sum(PAUSES) == NT * KD

        def beside(pause):
            return range(sum(PAUSES[:pause]), sum(PAUSES[:pause + 1]))

        def takes(*pauses):
            return [t for pause in pauses for t in range(NT) if (t + 1) * KD - 1 in beside(pause)]

        def steps(step):
            def run(eng):
                step(0, None, 0)
                with eng.Fori(0, NC // 2 - 1) as i:
                    for q in range(2):
                        step(i * 2 + (q + 1), i * 2 + q, 1 - q)
                step(NC - 1, NC - 2, 1)
                step(None, NC - 1, 0)
            return run

        def is_(n, value):
            return isinstance(n, int) and n == value

        with nc.Block() as block:
            @block.gpsimd
            def _(pool):
                G = nc.gpsimd

                def stage(n, slot):
                    if not is_(n, 0):
                        pool.wait_ge(tok_turned, n + 1)
                    G.tensor_copy(bhc, chunk(bh, n)).then_inc(staged, 1)
                    G.tensor_copy(khc, chunk(kh, n)).then_inc(staged, 1)
                    G.tensor_copy(vtc, chunk(vt, n)).then_inc(staged, 1)
                    if not (is_(n, 0) or is_(n, 1)):
                        pool.wait_ge(out_summed, n)
                    G.tensor_copy(kr[slot][:, :, 0], chunk(kt, n)).then_inc(staged, 1)
                    G.tensor_copy(kr[slot][:, :, 1], chunk(ya, n)).then_inc(staged, 1)

                def step(n, c, slot):
                    if n is None:
                        return
                    pool.wait_ge(masked, n * 6 + 2)
                    pool.wait_ge(q_summed, n * NL + 1)
                    for l, size in enumerate(LEVELS):
                        G.tensor_tensor(level[:, l], tb_up, mask(f"level{size}"), ALU.mult).then_inc(levels_ready, 1)
                    if not is_(n, NC - 1):
                        stage(n + 1, 1 - slot)
                stage(0, 0)
                steps(step)(pool)

            @block.tensor
            def _(pe):
                def heads(out, lhsT, rhs, start=True, stop=True):
                    for p in range(NP):
                        for half in halves:
                            mm = nc.tensor.matmul(out(p, half), lhsT(p, half), rhs(p, half), start=start, stop=stop)
                    return mm

                def of(t, *idx):
                    return lambda p, half: t[(half,) + idx + (p,)]

                def both(t):
                    return lambda p, r: t[r, p].rearrange("q a b -> q (a b)")

                def score(n, c, slot):
                    pe.wait_ge(staged, n * 5 + 6)
                    pe.wait_ge(masked, n * 6 + 1)
                    if c is not None:
                        pe.wait_ge(state_ready, c + 2)
                    carry(pe, carried)
                    heads(both(b_ps), of(bhc), both(kr[slot]))
                    heads(both(k_ps), of(khc), both(kr[slot]))
                    heads(of(t_ps, 0), lambda p, r: kr[slot][r, p, 0], of(bhc)).then_inc(scores, 1)
                    for m, src in enumerate((vtc, bhc, khc)):
                        mm = heads(of(tok_ps, m), of(src), lambda p, r: col(consts, "ident64")[r])
                    mm.then_inc(tok_turned, 1)

                def sum_rhs(c, slot):
                    pe.wait_ge(state_ready, c + 2)
                    pe.wait_ge(y_ready, c + 1)
                    pe.wait_ge(tok_ready, c + 2)
                    carry(pe, carried)
                    for p in range(NP):
                        for r in halves:
                            nc.tensor.matmul(seq_ps[r, 0, p], kr[slot][r, p, 0], state[r, p], start=True, stop=False)
                            mm = nc.tensor.matmul(seq_ps[r, 0, p], tk_up[slot][r, p], tok[slot][r, 0, p], start=False, stop=True)
                    mm.then_inc(rhs_summed, 1)

                def sum_sa(c, slot):
                    pe.wait_ge(rhs_ready, c + 2)
                    pe.wait_ge(inv_grown, c * NL + (NL + 1))
                    carry(pe, carried)
                    heads(of(seq_ps, 1), of(inv[slot], 1), of(rhs)).then_inc(sa_summed, 1)

                def sum_out(c, slot):
                    pe.wait_ge(sa_ready, c + 2)
                    carry(pe, carried)
                    for p in range(NP):
                        for r in halves:
                            nc.tensor.matmul(seq_ps[r, 0, p], state[r, p], kr[slot][r, p, 1], start=True, stop=False)
                            nc.tensor.matmul(seq_ps[r, 0, p], sa[r, p], ab_up[slot][r, p], start=False, stop=False)
                            nc.tensor.matmul(seq_ps[r, 0, p], tok[slot][r, 0, p], ak_up[slot][r, p], start=False, stop=True)
                    for p in range(NP):
                        for r in halves:
                            nc.tensor.matmul(t_ps[r, 1, p], tok[slot][r, 1, p], sa[r, p], start=True, stop=False)
                            mm = nc.tensor.matmul(t_ps[r, 1, p], tok[slot][r, 2, p], tok[slot][r, 0, p], start=False, stop=True)
                    mm.then_inc(out_summed, 1)

                def step(n, c, slot):
                    if n is not None:
                        score(n, c, slot)
                    if c is not None:
                        sum_rhs(c, 1 - slot)
                    if n is None:
                        sum_sa(c, 1 - slot)
                        sum_out(c, 1 - slot)
                        return
                    side.multiply(pe, n, beside(0))
                    for l in range(NL):
                        pe.wait_ge(levels_ready, n * NL + (l + 2))
                        if l == 0:
                            pe.wait_ge(masked, n * 6 + 7)
                            pe.wait_ge(tok_ready, n + 2)
                        else:
                            pe.wait_ge(inv_grown, n * NL + (l + 1))
                        carry(pe, carried)
                        heads(of(q_ps), of(level, l), of(inv[slot], 0)).then_inc(q_summed, 1)
                        if l == 0 and c is not None:
                            sum_sa(c, 1 - slot)
                        side.multiply(pe, n, beside(1 + 2 * l))
                        pe.wait_ge(q_ready, n * NL + (l + 2))
                        carry(pe, carried)
                        if l < NL - 1:
                            heads(of(inv_ps, 0), of(inv[slot], 1), of(q_sb))
                        heads(of(inv_ps, 1), of(q_sb), of(inv[slot], 1)).then_inc(inv_summed, 1)
                        if l == 0 and c is not None:
                            sum_out(c, 1 - slot)
                        side.multiply(pe, n, beside(2 + 2 * l))
                steps(step)(pe)

            @block.scalar
            def _(act):
                S = nc.scalar

                def step(n, c, slot):
                    if n is not None:
                        act.wait_ge(tok_turned, n + 2)
                        if not (is_(n, 0) or is_(n, 1)):
                            act.wait_ge(out_summed, n)
                        S.activation(tok[slot], tok_ps[:, 0:3], ACT.Copy).then_inc(tok_ready, 1)
                    if c is not None:
                        act.wait_ge(rhs_summed, c + 2)
                        S.activation(rhs, seq_ps[:, 0], ACT.Copy, scale=-1.0).then_inc(rhs_ready, 1)
                    for t in takes(0) if n is not None else ():
                        side.take(act, n, t)
                    for l in range(NL):
                        if n is not None:
                            act.wait_ge(q_summed, n * NL + (l + 2))
                            S.activation(q_sb[:], q_ps, ACT.Copy).then_inc(q_ready, 1)
                        if l == 0 and c is not None:
                            act.wait_ge(sa_summed, c + 2)
                            S.activation(sa, seq_ps[:, 1], ACT.Copy).then_inc(sa_ready, 1)
                            act.wait_ge(out_summed, c + 2)
                            S.activation(chunk(ya, c), seq_ps[:, 0], ACT.Copy).then_inc(y_ready, 1)
                        for t in takes(1 + 2 * l, 2 + 2 * l) if n is not None else ():
                            side.take(act, n, t)
                steps(step)(act)

            @block.vector
            def _(dve):
                link = Chain(dve, chain)
                V = nc.vector

                def prepare(n, slot):
                    dve.wait_ge(scores, n + 2)
                    dve.wait_ge(levels_ready, n * NL + 1)
                    V.tensor_tensor(tb_up, b_ps[:, :, 0], mask("upper"), ALU.mult).then_inc(masked, 1)
                    V.tensor_tensor(inv[slot][:, 0], t_ps[:, 0], mask("first_l"), ALU.mult).then_inc(chain, 1)
                    link.n += 1
                    link(V.tensor_tensor(inv[slot][:, 1], b_ps[:, :, 0], mask("first_u"), ALU.mult))
                    for q in range(2):
                        V.scalar_tensor_tensor(inv[slot][:, q], inv[slot][:, q], -1.0, mask("ident64"), ALU.mult, ALU.add)\
                            .then_inc(masked, 1)
                    V.tensor_tensor(ab_up[slot], b_ps[:, :, 1], mask("upper_incl"), ALU.mult).then_inc(masked, 1)
                    V.tensor_tensor(tk_up[slot], k_ps[:, :, 0], mask("upper"), ALU.mult).then_inc(masked, 1)
                    V.tensor_tensor(ak_up[slot], k_ps[:, :, 1], mask("upper_incl"), ALU.mult).then_inc(masked, 1)

                def grow(n, slot, l):
                    dve.wait_ge(inv_summed, n * NL + (l + 2))
                    if l == 0:
                        dve.wait_ge(masked, n * 6 + 7)
                    else:
                        dve.wait_ge(inv_grown, n * NL + (l + 1))
                    part = inv[slot] if l < NL - 1 else inv[slot][:, 1]
                    V.tensor_tensor(part, part, inv_ps[:] if l < NL - 1 else inv_ps[:, 1], ALU.subtract).then_inc(inv_grown, 1)

                def advance(c):
                    dve.wait_ge(out_summed, c + 2)
                    link(V.tensor_tensor(state, state, t_ps[:, 1], ALU.add))
                    through = pc[:, :, bass.ds(c, 1)].to_broadcast([P, NP, C])
                    V.tensor_tensor(state, state, through, ALU.mult).then_inc(state_ready, 1)
                    dve.wait_ge(state_ready, c + 3)

                V.memset(state, 0.0).then_inc(state_ready, 1)
                dve.wait_ge(state_ready, 2)
                prepare(0, 0)
                for l in range(NL):
                    grow(0, 0, l)

                def step(n, c, slot):
                    if n is not None:
                        prepare(n, slot)
                        grow(n, slot, 0)
                    advance(c)
                    for l in range(1, NL if n is not None else 0):
                        grow(n, slot, l)
                with dve.Fori(0, NC // 2 - 1) as i:
                    link.enter(i, 6)
                    for q in range(2):
                        step(i * 2 + (q + 1), i * 2 + q, 1 - q)
                    link.leave(NC // 2 - 1)
                step(NC - 1, NC - 2, 1)
                step(None, NC - 1, 0)

            @block.sync
            def _(sp):
                side.transfer(sp, NC)
                sp.wait_ge(state_ready, NC + 2)
                sp.dma_start(io["wkv_prompt_out"], state).then_inc(saved, 16)
                sp.wait_ge(saved, 17)


def rwkv_samples(nc, io, sb, pb, sm, consts, vecs, x, ya, ob, kt, kh, bh, vt, sgd, ws, **_):
    with ExitStack() as ph:
        room = x[:].rearrange("p k n -> p (k n)")
        n_state = NP * NS * HD
        state, part, part2 = (room[:, q * n_state:(q + 1) * n_state].rearrange("p (a b c) -> p a b c", a=NP, b=NS)
                              for q in range(3))
        sum_ps = pb(ph, "sum_ps", [P, NP, NS, HD])
        spread_ps = pb(ph, "spread_ps", [P, NP, NS, HD])
        loaded, part_ready, summed, used, state_ready, chain, stored = sm(
            ph, "state_loaded", "part_ready", "part_summed", "sums_used", "new_state", "samples_chain", "new_state_stored")

        def spread(t):
            return t[:, :, TP:T].unsqueeze(3).to_broadcast([P, NP, NS, HD])

        unit = col(consts, "ident64").unsqueeze(1).unsqueeze(1).to_broadcast([P, NP, NS, HD])
        with nc.Block() as block:
            @block.sync
            def _(sp):
                sp.dma_start(state, io["state_wkv"]).then_inc(loaded, 16)
                sp.wait_ge(state_ready, 2)
                sp.dma_start(io["wkv_sample_out"], state).then_inc(stored, 16)
                sp.wait_ge(stored, 17)

            @block.tensor
            def _(pe):
                for n, (src, out) in enumerate(((part, sum_ps), (part2, spread_ps), (part, sum_ps))):
                    pe.wait_ge(part_ready, n + 2)
                    for p in range(NP):
                        mm = nc.tensor.matmul(out[:, p].rearrange("p a b -> p (a b)"), col(consts, "headsum"),
                                              src[:, p].rearrange("p a b -> p (a b)"), start=True, stop=True)
                    mm.then_inc(summed, 1)

            @block.vector
            def _(dve):
                link = Chain(dve, chain)
                V = nc.vector
                dve.wait_ge(loaded, 17)
                V.tensor_tensor(part, state, spread(kt), ALU.mult).then_inc(part_ready, 1)
                V.tensor_tensor(part2, unit, spread(vt), ALU.mult).then_inc(part_ready, 1)
                decay = ws[:].unsqueeze(3).to_broadcast([P, NP, NS, HD])
                link(V.tensor_tensor(state, state, decay, ALU.mult))
                dve.wait_ge(summed, 2)
                link(V.tensor_tensor(part, sum_ps[:], spread(bh), ALU.mult))
                link(V.tensor_tensor(state, state, part, ALU.subtract))
                dve.wait_ge(summed, 3)
                link(V.tensor_tensor(part2, spread_ps[:], spread(kh), ALU.mult))
                link(V.tensor_tensor(state, state, part2, ALU.add))
                dve.sem_inc(state_ready, 1)
                V.tensor_tensor(part, state, spread(ya), ALU.mult).then_inc(part_ready, 1)
                dve.wait_ge(summed, 4)
                link(V.tensor_tensor(part2, sum_ps[:], unit, ALU.mult))
                V.tensor_reduce(ya[:, :, TP:T], part2, AX_X, ALU.add).then_inc(used, 1)
    with ExitStack() as ph:
        square, rstd = ([sb(ph, f"gn_{what}{q}", [P, NT, TN]) for q in range(2)] for what in ("square", "rstd"))
        g2 = sb(ph, "g2_gn", [P, NP, P])
        ps = [pb(ph, f"gn_ps{q}", [P, NT, 512]) for q in range(2)]
        (g2_loaded, mean_summed, centred, squared, var_summed, std_ready, std_used, gate_summed, gated, chain) = sm(
            ph, "g2_loaded", "gn_mean_summed", "gn_centred", "gn_squared", "gn_var_summed", "gn_std_ready",
            "gn_std_used", "gate_summed", "gated", "gn_chain")

        def tiles(t):
            return t.rearrange("p (t n) -> p t n", t=NT)

        with nc.Block() as block:
            @block.sync
            def _(sp):
                sp.dma_start(g2[:], io["g2"]).then_inc(g2_loaded, 16)

            @block.tensor
            def _(pe):
                def head_sums(out, src):
                    for t in range(NT):
                        mm = nc.tensor.matmul(out[:, t, 0:TN], col(consts, "headmean"), src[:, t], start=True, stop=True)
                    return mm

                for p in range(NP):
                    if p >= 2:
                        pe.wait_ge(centred, p)
                    head_sums(ps[p % 2], tiles(ya[:, p])).then_inc(mean_summed, 1)
                pe.wait_ge(g2_loaded, 17)
                pe.wait_ge(centred, NP + 1)
                for p in range(NP):
                    pe.wait_ge(squared, p + 2)
                    if p:
                        pe.wait_ge(std_ready, p + 1)
                    head_sums(ps[0], square[p % 2]).then_inc(var_summed, 1)
                    if p:
                        pe.wait_ge(gated, p + 1)
                    for t in range(NT):
                        mm = nc.tensor.matmul(ps[1][:, t, 0:TN], g2[:, p], sgd[:, t * TN:(t + 1) * TN],
                                              start=True, stop=True)
                    mm.then_inc(gate_summed, 1)

            @block.scalar
            def _(act):
                def squares(p):
                    act.wait_ge(centred, p + 2)
                    if p >= 2:
                        act.wait_ge(var_summed, p)
                    nc.scalar.activation(square[p % 2][:], tiles(ya[:, p]), ACT.Square).then_inc(squared, 1)

                squares(0)
                squares(1)
                for p in range(NP):
                    act.wait_ge(var_summed, p + 2)
                    if p >= 2:
                        act.wait_ge(std_used, p)
                    nc.scalar.activation(rstd[p % 2][:], ps[0][:, :, 0:TN], ACT.Sqrt, bias=col(consts, "gn_eps"))\
                        .then_inc(std_ready, 1)
                    if p + 2 < NP:
                        squares(p + 2)

            @block.vector
            def _(dve):
                link = Chain(dve, chain)
                V = nc.vector
                for p in range(NP):
                    dve.wait_ge(mean_summed, p + 2)
                    V.tensor_tensor(tiles(ya[:, p]), tiles(ya[:, p]), ps[p % 2][:, :, 0:TN], ALU.subtract)\
                        .then_inc(centred, 1)
                dve.wait_ge(centred, NP + 1)
                for p in range(NP):
                    y, r = ya[:, p], rstd[p % 2][:]
                    dve.wait_ge(squared, p + 2)
                    dve.wait_ge(std_ready, p + 2)
                    link(V.reciprocal(r, r))
                    V.tensor_tensor(tiles(y), tiles(y), r, ALU.mult).then_inc(std_used, 1)
                    dve.wait_ge(std_used, p + 2)
                    link(V.tensor_scalar(y, y, vec(vecs, "gn_g", p), vec(vecs, "gn_b", p), ALU.mult, ALU.add))
                    link(V.tensor_tensor(y, y, ob[:, p], ALU.add))
                    dve.wait_ge(gate_summed, p + 2)
                    V.tensor_tensor(tiles(y), tiles(y), ps[1][:, :, 0:TN], ALU.mult).then_inc(gated, 1)


def attention(nc, io, sb, pb, sm, consts, x, h, ob, **_):
    room = x[:].rearrange("p k n -> p (k n)")
    with ExitStack() as at:
        qkv = sb(at, "qkv", [P, 6, T])
        kt, vt = qkv[:, 4], qkv[:, 5]
        with ExitStack() as ph:
            k_pad = room[:, 0:WIN + TP]
            def score_rows(n):
                first = WIN + TP + n * NH * 2 * WIN
                return room[:, first:first + NH * 2 * WIN].rearrange("p (h k) -> p h k", h=NH)
            s = [score_rows(0), score_rows(1)]
            prob = [score_rows(2), sb(ph, "prob", [P, NH, 2 * WIN])[:]]
            bias = sb(ph, "bias", [P, 2, NH * 2 * WIN])
            vtok = sb(ph, "vtok", [P, 1 + NB, P])
            qs = sb(ph, "qs", [P, 2, NP, WIN])
            ks = sb(ph, "ks", [P, 2, 2 * WIN])
            vs = sb(ph, "vs", [P, 2, 2, P])
            prob_t = sb(ph, "prob_t", [P, NH, 2, P])
            stat = sb(ph, "att_stat", [P, 2, 6, NH])
            sinks = sb(ph, "sinks", [P, NH])
            o = sb(ph, "o", [P, NP, 2, HD])
            s_ps = pb(ph, "s_ps", [P, NH, 2 * WIN])
            pt_ps = pb(ph, "pt_ps", [P, 4, 2, P])
            o_ps = pb(ph, "o_ps", [P, 2, NP, HD])
            ot_ps = o_ps[:].rearrange("p k c d -> p (k c d)").rearrange("p (c n) -> p c n", c=NP)
            (loaded, padded, v_turned, v_taken, staged, scored, biased, chain, max_ready, exped, p_turned,
             p_taken, o_summed, o_ready, o_turned, o_taken, kv_stored) = sm(
                ph, "att_loaded", "padded", "v_turned", "v_taken", "att_staged", "scored", "biased", "att_chain",
                "max_ready", "exped", "p_turned", "p_taken", "o_summed", "o_ready", "o_turned",
                "o_taken", "kv_stored")
            q_loaded, kv_loaded = sm(ph, "att_q_loaded", "att_kv_loaded")
            side = Side(nc, io, sb, pb, sm, ph, h, NC, "att")
            LEFT = SIDE - NC
            with nc.Block() as block:
                @block.sync
                def _(sp):
                    sp.dma_start(qkv[:, NP:], io["side_saved"][:, NP:6]).then_inc(kv_loaded, 16)
                    sp.dma_start(qkv[:, 0:NP], io["side_saved"][:, 0:NP]).then_inc(q_loaded, 16)
                    sp.dma_start(bias[:], io["att_bias"]).then_inc(loaded, 16)
                    sp.dma_start(sinks[:], io["sinks"]).then_inc(loaded, 16)
                    sp.wait_ge(kv_loaded, 17)
                    sp.dma_start(io["k_win_prompt_out"], qkv[:, 4, TP - WIN:TP]).then_inc(kv_stored, 16)
                    sp.dma_start(io["v_win_prompt_out"], qkv[:, 5, TP - WIN:TP]).then_inc(kv_stored, 16)
                    side.transfer(sp, LEFT)
                    sp.wait_ge(kv_stored, 33)

                def blocks(eng, body):
                    body(0, 0, False)
                    with eng.Fori(0, LEFT // 2) as i:
                        for q in range(2):
                            body(i * 2 + (q + 1), 1 - q, True)
                    body(NB - 1, 1, False)

                def is_last(b):
                    return isinstance(b, int) and b == NB - 1

                @block.gpsimd
                def _(pool):
                    G = nc.gpsimd
                    pool.wait_ge(kv_loaded, 17)
                    G.memset(k_pad[:, 0:WIN], 0.0).then_inc(padded, 1)
                    G.tensor_copy(k_pad[:, WIN:], kt[:, 0:TP]).then_inc(padded, 1)
                    G.memset(vtok[:, 0], 0.0).then_inc(padded, 1)
                    pool.wait_ge(padded, 4)
                    pool.wait_ge(v_taken, 3)
                    pool.wait_ge(q_loaded, 17)

                    def body(b, slot, _):
                        if not (isinstance(b, int) and b == 0):
                            pool.wait_ge(scored, b)
                            pool.wait_ge(o_summed, b)
                        G.tensor_copy(qs[:, slot], qkv[:, 0:NP, bass.ds(b * WIN, WIN)]).then_inc(staged, 1)
                        G.tensor_copy(ks[:, slot], k_pad[:, bass.ds(b * WIN, 2 * WIN)]).then_inc(staged, 1)
                        G.tensor_copy(vs[:, slot], vtok[:, bass.ds(b, 2), :]).then_inc(staged, 1)
                    blocks(pool, body)

                @block.tensor
                def _(pe):
                    pe.wait_ge(kv_loaded, 17)
                    for r in range(2):
                        for b in range(4):
                            mm = nc.tensor.transpose(pt_ps[:, b, 0], vt[:, (4 * r + b) * P:(4 * r + b + 1) * P], col(consts, "ident"))
                        mm.then_inc(v_turned, 1)
                        pe.wait_ge(v_taken, r + 2)

                    def score(b, slot):
                        pe.wait_ge(staged, b * 3 + 4)
                        pe.wait_ge(biased, b + 1)
                        for kv, r in enumerate((slice(0, HD), slice(HD, P))):
                            for c in range(NP):
                                mm = nc.tensor.matmul(s_ps[:, 4 * kv + c], qs[r, slot, c], ks[r, slot], start=True, stop=True)
                        mm.then_inc(scored, 1)

                    def body(b, slot, beside):
                        def fill(*products):
                            if beside:
                                side.multiply(pe, b - 1, range(*products))

                        fill(0, 6)
                        if not is_last(b):
                            score(b + 1, 1 - slot)
                        fill(6, 16)
                        pe.wait_ge(exped, b * 9 + 9)
                        for half in range(2):
                            if half or not isinstance(b, int):
                                pe.wait_ge(p_taken, b * 2 + half + 1)
                            for c in range(4):
                                for q in range(2):
                                    mm = nc.tensor.transpose(pt_ps[:, c, q], prob[slot][:, 4 * half + c, q * WIN:(q + 1) * WIN],
                                                             col(consts, "ident"))
                            mm.then_inc(p_turned, 1)
                            fill(16 + 2 * half, 18 + 2 * half)
                        pe.wait_ge(p_taken, b * 2 + 3)
                        pe.wait_ge(o_taken, b + 1)
                        for kv in range(2):
                            for c in range(NP):
                                for q in range(2):
                                    mm = nc.tensor.matmul(o_ps[:, kv, c], prob_t[:, 4 * kv + c, q],
                                                          vs[:, slot, q, kv * HD:(kv + 1) * HD], start=q == 0, stop=q == 1)
                        mm.then_inc(o_summed, 1)
                        fill(20, 22)
                        pe.wait_ge(o_ready, b + 2)
                        for c in range(NP):
                            mm = nc.tensor.transpose(ot_ps[:, c], o[:, c].rearrange("p a b -> p (a b)"), col(consts, "ident"))
                        mm.then_inc(o_turned, 1)
                        fill(22, 24)
                    score(0, 0)
                    blocks(pe, body)

                @block.scalar
                def _(act):
                    S = nc.scalar
                    for r in range(2):
                        act.wait_ge(v_turned, r + 2)
                        S.activation(vtok[:, 1 + 4 * r:5 + 4 * r], pt_ps[:, :, 0], ACT.Copy).then_inc(v_taken, 1)

                    def exp(b, slot):
                        act.wait_ge(max_ready, b + 2)
                        for n in range(NH):
                            S.activation(prob[slot][:, n], s[slot][:, n], ACT.Exp, bias=stat[:, slot, 1, n:n + 1],
                                         accum_out=stat[:, slot, 2, n:n + 1]).then_inc(exped, 1)
                        S.activation(stat[:, slot, 3], stat[:, slot, 3], ACT.Exp).then_inc(exped, 1)

                    def body(b, slot, beside):
                        for t in range(2 if beside else 0):
                            side.take(act, b - 1, t)
                        for half in range(2):
                            act.wait_ge(p_turned, b * 2 + half + 2)
                            S.activation(prob_t[:, 4 * half:4 * half + 4], pt_ps[:], ACT.Copy).then_inc(p_taken, 1)
                        if not is_last(b):
                            exp(b + 1, 1 - slot)
                        act.wait_ge(o_turned, b + 2)
                        S.activation(ob[:, :, bass.ds(b * WIN, WIN)], ot_ps, ACT.Copy).then_inc(o_taken, 1)
                        if beside:
                            side.take(act, b - 1, 2)
                    exp(0, 0)
                    blocks(act, body)

                @block.vector
                def _(dve):
                    link = Chain(dve, chain)
                    V = nc.vector
                    dve.wait_ge(loaded, 33)

                    def bias_and_max(b, slot, first=False):
                        m = stat[:, slot]
                        dve.wait_ge(scored, b + 2)
                        V.scalar_tensor_tensor(s[slot].rearrange("p a b -> p (a b)"), s_ps[:].rearrange("p a b -> p (a b)"),
                                               SCALE, bias[:, 0 if first else 1], ALU.mult, ALU.add).then_inc(biased, 1)
                        dve.wait_ge(biased, b + 2)
                        link(V.tensor_reduce(m[:, 0], s[slot], AX_X, ALU.max))
                        link(V.tensor_tensor(m[:, 0], m[:, 0], sinks[:], ALU.max))
                        link(V.tensor_tensor(m[:, 3], sinks[:], m[:, 0], ALU.subtract))
                        link(V.tensor_scalar(m[:, 1], m[:, 0], -1.0, None, ALU.mult))
                        dve.sem_inc(max_ready, 1)

                    def body(b, slot, _):
                        m = stat[:, slot]
                        if not is_last(b):
                            bias_and_max(b + 1, 1 - slot)
                        dve.wait_ge(exped, b * 9 + 10)
                        link(V.tensor_tensor(m[:, 4], m[:, 2], m[:, 3], ALU.add))
                        link(V.reciprocal(m[:, 5], m[:, 4]))
                        dve.wait_ge(o_summed, b + 2)
                        dve.wait_ge(o_turned, b + 1)
                        V.tensor_tensor(o[:].rearrange("p c k d -> p k c d"), o_ps[:],
                                        m[:, 5].rearrange("p (k c) -> p k c", k=2).unsqueeze(3).to_broadcast([P, 2, NP, HD]),
                                        ALU.mult).then_inc(o_ready, 1)

                    bias_and_max(0, 0, True)
                    body(0, 0, False)
                    with dve.Fori(0, LEFT // 2) as i:
                        link.enter(i, 12)
                        for q in range(2):
                            body(i * 2 + (q + 1), 1 - q, True)
                        link.leave(LEFT // 2)
                    body(NB - 1, 1, False)
        with ExitStack() as ph:
            kc = sb(ph, "kc", [P, NS, WIN])
            vc = sb(ph, "vc", [P, NS, P])
            kw = sb(ph, "kw", [P, NS, WIN])
            prod = sb(ph, "prod", [P, NS, 2, NP])
            s_t = sb(ph, "s_t", [P, NS, 2, NP])
            s = sb(ph, "ss", [64, WIN + 1])
            rel = sb(ph, "rel", [64, WIN + 2])
            stat = sb(ph, "ss_stat", [64, 6])
            pt = sb(ph, "pt", [P, NS, 2, NP])
            row = sb(ph, "self_row", [1, 64])
            ones = sb(ph, "ones_row", [1, P])
            vrow = sb(ph, "vrow", [NS, P])
            part = sb(ph, "self_part", [P, NS, 2, NP])
            st_ps = [pb(ph, f"st_ps{kv}", [P, NS, NP]) for kv in range(2)]
            s_ps = pb(ph, "ss_ps", [64, WIN + 1])
            pt_ps = pb(ph, "pts_ps", [P, 64])
            row_ps = pb(ph, "srow_ps", [1, 64])
            self_ps = pb(ph, "self_ps", [P, NS, 2, NP])
            o_ps = pb(ph, "os_ps", [P, NS, 2, NP])
            v_ps = pb(ph, "vr_ps", [NS, P])
            loaded, pe_step, act_step, dve_step, kv_stored, sink_done, kw_ready, st_copied = sm(
                ph, "cache_loaded", "samples_pe_step", "samples_act_step", "samples_dve_step", "cache_stored",
                "sample_sinks", "kw_ready", "st_copied")
            flat = "p a b c -> p (a b c)"
            halves = (slice(0, HD), slice(HD, P))
            with nc.Block() as block:
                @block.sync
                def _(sp):
                    sp.dma_start(kc[:], io["k_cache"]).then_inc(loaded, 16)
                    sp.dma_start(vc[:], io["v_cache"]).then_inc(loaded, 16)
                    sp.dma_start(rel[:], io["sample_bias"]).then_inc(loaded, 16)
                    sp.wait_ge(loaded, 49)
                    sp.dma_start(io["v_win_sample_out"][0:WIN - 1], vc[1:WIN]).then_inc(kv_stored, 16)
                    sp.wait_ge(act_step, 4)
                    sp.dma_start(io["v_win_sample_out"][WIN - 1], vrow[:]).then_inc(kv_stored, 16)
                    sp.wait_ge(kw_ready, 3)
                    sp.dma_start(io["k_win_sample_out"], kw[:]).then_inc(kv_stored, 16)
                    sp.wait_ge(kv_stored, 49)

                @block.tensor
                def _(pe):
                    M = nc.tensor.matmul
                    pe.wait_ge(loaded, 49)
                    for kv, r in enumerate(halves):
                        for b in range(NS):
                            mm = M(st_ps[kv][:, b], kc[r, b], qkv[r, 0:NP, TP + b], start=True, stop=True)
                    mm.then_inc(pe_step, 1)
                    nc.tensor.transpose(v_ps[:], vt[:, TP:T], col(consts, "ident")).then_inc(pe_step, 1)
                    pe.wait_ge(dve_step, 5)
                    pe.wait_ge(act_step, 2)
                    nc.tensor.transpose(s_ps[:, 0:WIN], s_t[:].rearrange(flat), col(consts, "ident"))
                    M(s_ps[:, WIN:], prod[:].rearrange(flat), col(consts, "ones"), start=True, stop=True)\
                        .then_inc(pe_step, 1)
                    pe.wait_ge(dve_step, 13)
                    nc.tensor.transpose(pt_ps[:], s[:, 0:WIN], col(consts, "ident")[0:64, 0:64]).then_inc(pe_step, 1)
                    nc.tensor.transpose(row_ps[:], s[:, WIN:], col(consts, "ident")[0:64, 0:64]).then_inc(pe_step, 1)
                    pe.wait_ge(act_step, 7)
                    M(self_ps[:].rearrange(flat), ones[:], row[:], start=True, stop=True)
                    for b in range(NS):
                        mm = M(o_ps[:, b].rearrange("p a b -> p (a b)"), vc[:, b], pt[:, b].rearrange("p a b -> p (a b)"),
                               start=True, stop=True)
                    mm.then_inc(pe_step, 1)

                @block.scalar
                def _(act):
                    S = nc.scalar
                    act.wait_ge(pe_step, 2)
                    for kv in range(2):
                        act.wait_ge(pe_step, 2)
                        S.activation(s_t[:, :, kv], st_ps[kv][:], ACT.Copy).then_inc(st_copied, 1)
                    act.wait_ge(st_copied, 3)
                    act.sem_inc(act_step, 1)
                    act.wait_ge(pe_step, 3)
                    S.activation(vrow[:], v_ps[:], ACT.Copy).then_inc(act_step, 2)
                    act.wait_ge(dve_step, 10)
                    S.activation(stat[:, 3:4], stat[:, 3:4], ACT.Exp).then_inc(sink_done, 1)
                    S.activation(s[:], s[:], ACT.Exp, bias=stat[:, 1:2], accum_out=stat[:, 2:3]).then_inc(act_step, 1)
                    act.wait_ge(pe_step, 5)
                    S.activation(pt[:].rearrange(flat), pt_ps[:], ACT.Copy).then_inc(act_step, 1)
                    act.wait_ge(pe_step, 6)
                    S.activation(row[:], row_ps[:], ACT.Copy).then_inc(act_step, 1)

                @block.vector
                def _(dve):
                    V = nc.vector
                    step = Chain(dve, dve_step)
                    step(V.memset(prod[:], 0.0))
                    step(V.memset(ones[:], 1.0))
                    dve.wait_ge(loaded, 49)
                    V.tensor_copy(kw[:, :, 0:WIN - 1], kc[:, :, 1:WIN]).then_inc(kw_ready, 1)
                    V.tensor_copy(kw[:, :, WIN - 1], kt[:, TP:T]).then_inc(kw_ready, 1)
                    for kv, r in enumerate(halves):
                        step(V.tensor_tensor(prod[r, :, kv], qkv[r, 0:NP, TP:T].rearrange("p c b -> p b c"),
                                             kt[r, TP:T].unsqueeze(2).to_broadcast([HD, NS, NP]), ALU.mult))
                    dve.wait_ge(pe_step, 4)
                    step(V.scalar_tensor_tensor(s[:], s_ps[:], SCALE, rel[:, 0:WIN + 1], ALU.mult, ALU.add))
                    step(V.tensor_reduce(stat[:, 0:1], s[:], AX_X, ALU.max))
                    step(V.tensor_tensor(stat[:, 0:1], stat[:, 0:1], rel[:, WIN + 1:], ALU.max))
                    step(V.tensor_scalar(stat[:, 1:2], stat[:, 0:1], -1.0, None, ALU.mult))
                    step(V.tensor_tensor(stat[:, 3:4], rel[:, WIN + 1:], stat[:, 1:2], ALU.add))
                    dve.wait_ge(act_step, 5)
                    dve.wait_ge(sink_done, 2)
                    step(V.tensor_tensor(stat[:, 4:5], stat[:, 2:3], stat[:, 3:4], ALU.add))
                    step(V.reciprocal(stat[:, 5:6], stat[:, 4:5]))
                    step(V.tensor_scalar(s[:], s[:], stat[:, 5:6], None, ALU.mult))
                    dve.wait_ge(pe_step, 7)
                    step(V.tensor_tensor(part[:], self_ps[:], vt[:, TP:T].unsqueeze(2).unsqueeze(3).to_broadcast([P, NS, 2, NP]),
                                         ALU.mult))
                    for kv, r in enumerate(halves):
                        step(V.tensor_tensor(ob[r, :, TP:T].rearrange("p c b -> p b c"), part[r, :, kv], o_ps[r, :, kv], ALU.add))


def merge(nc, io, sb, pb, sm, x, ya, ob, mh, ml, **_):
    SETS = 4
    with ExitStack() as ph:
        w = sb(ph, "w_merge", [P, 2, 2, NP, P])
        gate = sb(ph, "gate", [P, 2, 2, T])
        part = sb(ph, "merge_part", [P, 2, 2, TN])
        whole = sb(ph, "merged", [P, 2, TN])
        ps = [[pb(ph, f"merge_ps{s}{q}", [P, 512]) for q in range(2)] for s in range(SETS)]
        (w0_loaded, w1_loaded, g0_loaded, g1_loaded, w_free, summed, gates_ready, parts_ready, used, high, low,
         x_back) = sm(
            ph, "wm0_loaded", "wm1_loaded", "gate0_loaded", "gate1_loaded", "wm_free", "merge_summed", "gates_ready",
            "merge_parts", "merge_used", "merged_high", "merged_low", "x_back")
        w_loaded, g_loaded = (w0_loaded, w1_loaded), (g0_loaded, g1_loaded)
        TURN = 4
        with nc.Block() as block:
            @block.sync
            def _(sp):
                with sp.Fori(0, KD // TURN) as i:
                    for m in range(TURN):
                        s = m % 2
                        sp.wait_ge(w_free, i * TURN + m + 2)
                        sp.dma_start(w[:, s].rearrange("p q k n -> p (q k n)"), io["w_merge"][bass.ds(i * TURN + m, 1)].rearrange("o p k n -> p (o k n)"))\
                            .then_inc(w_loaded[s], 16)
                        sp.dma_start(gate[:, s], io["side_saved"][:, bass.ds(i * (2 * TURN) + (2 * m + 6), 2), :])\
                            .then_inc(g_loaded[s], 16)
                sp.dma_start(x[:], io["x_saved"]).then_inc(x_back, 16)
                sp.wait_ge(x_back, 17)

            @block.tensor
            def _(pe):
                pe.sem_inc(used, SETS)
                with pe.Fori(0, KD // TURN) as i:
                    for n in range(TURN * NT):
                        m, t = n // NT, n % NT
                        if t == 0:
                            pe.wait_ge(w_loaded[m % 2], i * (TURN * 8) + (m // 2 * 16 + 17))
                        pe.wait_ge(used, i * (TURN * NT) + (n + 2))
                        for q, src in enumerate((ya, ob)):
                            for k in range(NP):
                                mm = nc.tensor.matmul(ps[n % SETS][q][:, 0:TN], w[:, m % 2, q, k],
                                                      src[:, k, t * TN:(t + 1) * TN], start=k == 0, stop=k == NP - 1)
                        mm.then_inc(summed, 1)

            @block.scalar
            def _(act):
                with act.Fori(0, KD // TURN) as i:
                    for m in range(TURN):
                        act.wait_ge(g_loaded[m % 2], i * (TURN * 8) + (m // 2 * 16 + 17))
                        nc.scalar.activation(gate[:, m % 2], gate[:, m % 2], ACT.Sigmoid).then_inc(gates_ready, 1)
                        for n in range(m * NT, (m + 1) * NT):
                            act.wait_ge(used, i * (TURN * NT) + (n + SETS + 2))
                            nc.scalar.activation(mh[:, bass.ds(i * TURN + m, 1), n % NT * TN:(n % NT + 1) * TN],
                                                 whole[:, n % 2].unsqueeze(1), ACT.Copy).then_inc(high, 1)

            @block.vector
            def _(dve):
                V = nc.vector
                dve.sem_inc(w_free, 2)
                with dve.Fori(0, KD // TURN) as i:
                    for n in range(TURN * NT):
                        m, t = n // NT, n % NT
                        tok = slice(t * TN, (t + 1) * TN)
                        if t == 0:
                            dve.wait_ge(gates_ready, i * TURN + (m + 2))
                        dve.wait_ge(summed, i * (TURN * NT) + (n + 2))
                        dve.wait_ge(used, i * (TURN * NT) + (n + SETS))
                        for q in range(2):
                            V.tensor_tensor(part[:, n % 2, q], gate[:, m % 2, q, tok], ps[n % SETS][q][:, 0:TN], ALU.mult)\
                                .then_inc(parts_ready, 1)
                        dve.wait_ge(parts_ready, i * (2 * TURN * NT) + (2 * n + 3))
                        V.tensor_tensor(whole[:, n % 2], part[:, n % 2, 0], part[:, n % 2, 1], ALU.add).then_inc(used, 1)
                        dve.wait_ge(used, i * (TURN * NT) + (n + SETS + 2))
                        dve.wait_ge(high, i * (TURN * NT) + (n + 2))
                        V.tensor_tensor(ml[:, bass.ds(i * TURN + m, 1), tok], whole[:, n % 2].unsqueeze(1),
                                        mh[:, bass.ds(i * TURN + m, 1), tok].bitcast(F32), ALU.subtract).then_inc(low, 1)
                        dve.wait_ge(low, i * (TURN * NT) + (n + 2))
                        if t == NT - 1:
                            dve.sem_inc(w_free, 1)


TILES = -(-T // P)


def split_input(nc, sb, sm, h, hh, hl, **_):
    with ExitStack() as ph:
        high_ready, low_ready = sm(ph, "high_ready", "low_ready")
        with nc.Block() as block:
            @block.scalar
            def _(act):
                for k in range(KD):
                    nc.scalar.activation(hh[:, k], h[:, k], ACT.Copy).then_inc(high_ready, 1)

            @block.vector
            def _(dve):
                for k in range(KD):
                    dve.wait_ge(high_ready, k + 2)
                    nc.vector.tensor_tensor(hl[:, k], h[:, k], hh[:, k].bitcast(F32), ALU.subtract).then_inc(low_ready, 1)


def peer_queries(nc, io, sb, pb, sm, hh, hl, **_):
    with ExitStack() as ph:
        query = Product(nc, io["peer_wq"], io["query_saved"], ACT.Copy, sb, pb, sm, ph, hh, hl, 0, "q")
        COUNT = 2 * NH

        def pairs(eng, body):
            with eng.Fori(0, COUNT // 2) as i:
                for s in range(2):
                    body(i * 2 + s, s, i)

        with nc.Block() as block:
            @block.sync
            def _(sp):
                for s in range(2):
                    sp.sem_inc(query.stored[s], 16)
                    query.load(sp, s, s)

                def body(n, s, last=False):
                    if not last:
                        query.load(sp, n + 2, s)
                    query.store(sp, n, s)
                with sp.Fori(0, COUNT // 2 - 1) as i:
                    for s in range(2):
                        body(i * 2 + s, s)
                for s in range(2):
                    body(COUNT - 2 + s, s, True)
                for s in range(2):
                    sp.wait_ge(query.stored[s], COUNT // 2 * 16 + 17)

            @block.gpsimd
            def _(pool):
                pool.sem_inc(query.split, 2)
                pairs(pool, lambda n, s, turn: query.split_low(pool, n, s))

            @block.tensor
            def _(pe):
                pe.sem_inc(query.summed, 2)

                def body(n, s, turn):
                    for t in range(NT):
                        query.multiply(pe, n, s, t)
                pairs(pe, body)

            @block.scalar
            def _(act):
                act.sem_inc(query.ready, 2)
                query.split_high(act, 0, 0, 0)

                def body(n, s, turn, last=False):
                    if not last:
                        query.split_high(act, n + 1, 1 - s, turn + s)
                    query.finish(act, n, s, turn)
                with act.Fori(0, COUNT // 2 - 1) as i:
                    for s in range(2):
                        body(i * 2 + s, s, i)
                body(COUNT - 2, 0, COUNT // 2 - 1)
                body(COUNT - 1, 1, COUNT // 2 - 1, True)


class Product:

    def __init__(self, nc, w, saved, function, sb, pb, sm, ph, hh, hl, first, tag):
        self.nc, self.w, self.saved, self.function = nc, w, saved, function
        self.hh, self.hl, self.first = hh, hl, first
        self.raw = sb(ph, f"w_raw_{tag}", [P, 2, KD, P])
        self.uh = sb(ph, f"w_high_{tag}", [P, 2, KD, P], F32R)
        self.ul = sb(ph, f"w_low_{tag}", [P, 2, KD, P], F32R)
        self.out = sb(ph, f"product_{tag}", [P, 2, NT, TN])
        self.ps = [pb(ph, f"product_ps{s}_{tag}", [P, NT, 512]) for s in range(2)]
        (u0, u1, self.high_ready, self.split, self.summed, self.ready, s0, s1) = sm(
            ph, *(f"{n}_{tag}" for n in ("w0_loaded", "w1_loaded", "w_high_ready", "w_split", "product_summed",
                                         "product_ready", "product0_stored", "product1_stored")))
        self.loaded, self.stored = (u0, u1), (s0, s1)

    def load(self, sp, n, slot):
        sp.wait_ge(self.split, n + 2)
        sp.dma_start(self.raw[:, slot], self.w[bass.ds(n + self.first, 1)].rearrange("o p k n -> p (o k) n"))\
            .then_inc(self.loaded[slot], 16)

    def split_high(self, act, n, slot, turn):
        act.wait_ge(self.loaded[slot], turn * 16 + 17)
        act.wait_ge(self.summed, n + 2)
        self.nc.scalar.activation(self.uh[:, slot], self.raw[:, slot], ACT.Copy).then_inc(self.high_ready, 1)

    def split_low(self, pool, n, slot):
        pool.wait_ge(self.high_ready, n + 2)
        self.nc.gpsimd.tensor_tensor(self.ul[:, slot], self.raw[:, slot], self.uh[:, slot].bitcast(F32), ALU.subtract)\
            .then_inc(self.split, 1)

    def multiply(self, pe, n, slot, t):
        if t == 0:
            pe.wait_ge(self.split, n + 4)
            pe.wait_ge(self.ready, n + 2)
        tok = slice(t * TN, (t + 1) * TN)
        for k in range(KD):
            for u, h in ((self.uh, self.hh), (self.uh, self.hl), (self.ul, self.hh)):
                mm = self.nc.tensor.matmul(self.ps[slot][:, t, 0:TN], u[:, slot, k], h[:, k, tok],
                                           start=k == 0 and h is self.hh and u is self.uh, stop=k == KD - 1 and u is self.ul)
        if t == NT - 1:
            mm.then_inc(self.summed, 1)

    def finish(self, act, n, slot, turn):
        act.wait_ge(self.summed, n + 4)
        act.wait_ge(self.stored[slot], turn * 16 + 17)
        self.nc.scalar.activation(self.out[:, slot], self.ps[slot][:, :, 0:TN], self.function).then_inc(self.ready, 1)

    def store(self, sp, n, slot):
        sp.wait_ge(self.ready, n + 4)
        sp.dma_start(self.saved[bass.ds(n + self.first, 1)].rearrange("o p n -> p (o n)"),
                     self.out[:, slot].rearrange("p t n -> p (t n)")).then_inc(self.stored[slot], 16)


def mixer_output(nc, io, sb, pb, sm, mod, x, mh, ml, **_):
    with ExitStack() as ph:
        mixed = Product(nc, io["w_o"], None, None, sb, pb, sm, ph, mh, ml, 0, "o")
        chain, = sm(ph, "wo_chain")
        with nc.Block() as block:
            @block.sync
            def _(sp):
                for s in range(2):
                    mixed.load(sp, s, s)
                with sp.Fori(0, KD // 2 - 1) as i:
                    for s in range(2):
                        mixed.load(sp, i * 2 + (s + 2), s)

            @block.gpsimd
            def _(pool):
                pool.sem_inc(mixed.split, 2)
                with pool.Fori(0, KD // 2) as i:
                    for s in range(2):
                        mixed.split_low(pool, i * 2 + s, s)

            @block.tensor
            def _(pe):
                pe.sem_inc(mixed.summed, 2)
                with pe.Fori(0, KD // 2) as i:
                    for s in range(2):
                        for t in range(NT):
                            mixed.multiply(pe, i * 2 + s, s, t)

            @block.scalar
            def _(act):
                with act.Fori(0, KD // 2) as i:
                    for s in range(2):
                        mixed.split_high(act, i * 2 + s, s, i)

            @block.vector
            def _(dve):
                link = Chain(dve, chain)
                V = nc.vector
                dve.sem_inc(mixed.ready, 2)
                with dve.Fori(0, KD // 2) as i:
                    link.enter(i, 4)
                    for s in range(2):
                        dve.wait_ge(mixed.summed, i * 2 + (s + 4))
                        ps, mix = mixed.ps[s], mixed.out[:, s].rearrange("p t n -> p (t n)")
                        gate = mod[:, bass.ds(i * 2 + (s + GT_M), 1), :].rearrange("p o n -> p (o n)")
                        link(V.tensor_scalar(mixed.out[:, s], ps[:, :, 0:TN], gate[:, 0:1], None, ALU.mult))
                        V.tensor_tensor(mix[:, TP:T], ps[:, NT - 1, TN - NS:TN], gate[:, 1:], ALU.mult)\
                            .then_inc(mixed.ready, 1)
                        dve.wait_ge(mixed.ready, i * 2 + (s + 4))
                        xm = x[:, bass.ds(i * 2 + s, 1), :].rearrange("p o n -> p (o n)")
                        link(V.scalar_tensor_tensor(xm, xm, ALPHA, mix, ALU.mult, ALU.add))
                    link.leave(KD // 2)


E_FIRST, E_SEL, E_LAST = 8, 4, 6
FIRST_GATES = E_FIRST + (TILES - 2) * E_SEL + E_LAST


def peer_select(nc, io, sb, pb, sm, consts, hh, hl, slots, **_):
    with ExitStack() as ph:
        NJ = 2 * NH
        HJ = NJ // 2
        hid = Product(nc, io["u"], io["hidden_saved"], ACT.Gelu, sb, pb, sm, ph, hh, hl, 0, "s")
        keys = sb(ph, "keys", [P, 2, NKEY])
        qt = sb(ph, "qt", [P, NJ, P])
        s_in = sb(ph, "scores", [P, NJ, NKEY])
        s = sb(ph, "cands", [P, NJ, NKEY])
        s2 = sb(ph, "rest", [P, NJ, NKEY])
        best = sb(ph, "best", [P, NJ, TOPK])
        best_at = sb(ph, "best_at", [P, NJ, TOPK], U32)
        best_key = sb(ph, "best_key", [P, NJ, TOPK])
        AFIRST = 4
        assert (AFIRST + 1) ** 2 > TOPK
        EARLY = AFIRST * TOPK
        NSUM = EARLY + (TOPK - AFIRST) * AFIRST
        cand, cand2 = (t[:].rearrange("p (h q) n -> p h (q n)", q=2)[:, :, 0:NSUM] for t in (s, s2))
        top = sb(ph, "top", [P, NH, TOPK])
        top_at = sb(ph, "top_at", [P, NH, TOPK], U32)
        half_at = sb(ph, "half_at", [P, 4, NH, TOPK], U32)
        half_pos = sb(ph, "half_pos", [P, 4, NH, TOPK])
        late = sb(ph, "late", [P, NH, TOPK])
        pick = [s, s2]
        slot = sb(ph, "slot", [P, 3, NH, TOPK])
        total = sb(ph, "total", [P, 2, NH])
        s_ps = pb(ph, "score_ps", [P, HJ, NKEY])
        t_ps = s_ps[:].rearrange("p j n -> p (j n)")[:, 0:3 * P].rearrange("p (q n) -> p q n", q=3)
        (keys_loaded, q_loaded, scored, copied, read, chain, gate_ready, slots_ready, turned, slots_taken,
         exp_in, carried) = sm(ph, "keys_loaded", "query_loaded", "scored_keys", "scores_copied", "scores_read",
                               "select_chain", "gate_exp", "slots_ready", "slots_turned", "slots_taken", "exp_in",
                               "select_carried")
        LAST = TILES - 1

        def shape(t):
            return t[:].rearrange("p (h q) n -> p h (q n)", q=2).rearrange("p h (k a) -> p h k a", k=TOPK)

        def tiles(eng, body):
            body(0, P)
            with eng.Fori(1, LAST) as i:
                body(i, P)
            body(LAST, T - LAST * P)

        def is_(i, n):
            return isinstance(i, int) and i == n

        def chunks(i):
            if is_(i, 0):
                return [(j, j % 2, j // 2) for j in range(E_FIRST)]
            more = E_FIRST - E_SEL
            return [(i * E_SEL + (j + more), j % 2, i * (E_SEL // 2) + (j + more) // 2)
                    for j in range(E_LAST if is_(i, LAST) else E_SEL)]

        with nc.Block() as block:
            @block.sync
            def _(sp):
                def query(i, n):
                    sp.dma_start(qt[:, :, 0:n], io["query_saved"].rearrange("j p n -> p j n")[:, :, bass.ds(i * P, n)]).then_inc(q_loaded, 16)

                def body(i, n):
                    for j, (m, s_, turn) in enumerate(chunks(i)):
                        if not (is_(i, LAST) and j >= E_LAST - 2):
                            hid.load(sp, m + 2, s_)
                        if j == 1 and n:
                            sp.wait_ge(scored, i * 2 + 3)
                            query(i + 1, n)
                        hid.store(sp, m, s_)

                sp.dma_start(keys[:], io["keys"]).then_inc(keys_loaded, 16)
                query(0, P)
                for s_ in range(2):
                    sp.sem_inc(hid.stored[s_], 16)
                    hid.load(sp, s_, s_)
                body(0, P)
                with sp.Fori(1, LAST - 1) as i:
                    body(i, P)
                body(LAST - 1, T - LAST * P)
                body(LAST, 0)
                for q in range(2):
                    sp.wait_ge(hid.stored[q], FIRST_GATES // 2 * 16 + 17)

            @block.gpsimd
            def _(pool):
                pool.sem_inc(hid.split, 2)

                def body(i, n):
                    for m, s_, turn in chunks(i):
                        hid.split_low(pool, m, s_)
                tiles(pool, body)

            @block.tensor
            def _(pe):
                pe.sem_inc(hid.summed, 2)
                pe.wait_ge(keys_loaded, 17)

                def score(i, n, half):
                    if half == 0:
                        pe.wait_ge(q_loaded, i * 16 + 17)
                        pe.wait_ge(slots_taken, i + 1)
                    else:
                        pe.wait_ge(copied, i * 2 + 2)
                    for j in range(HJ):
                        mm = nc.tensor.matmul(s_ps[0:n, j], qt[:, half * HJ + j, 0:n], keys[:, j % 2], start=True, stop=True)
                    mm.then_inc(scored, 1)

                def turn(i, n):
                    pe.wait_ge(slots_ready, i + 2)
                    for q in range(3):
                        mm = nc.tensor.transpose(t_ps[:, q, 0:n], slot[0:n, q].rearrange("p h k -> p (h k)"),
                                                 col(consts, "ident")[0:n, 0:n])
                    mm.then_inc(turned, 1)

                def body(i, n):
                    for j, (m, s_, _) in enumerate(chunks(i)):
                        if j < 2:
                            score(i, n, j)
                        if j == 3 and not is_(i, 0):
                            pe.wait_ge(copied, i * 2 + 3)
                            turn(i - 1, P)
                        for t in range(NT):
                            hid.multiply(pe, m, s_, t)
                tiles(pe, body)
                turn(LAST, T - LAST * P)

            @block.scalar
            def _(act):
                S = nc.scalar
                act.sem_inc(hid.ready, 2)
                act.sem_inc(slots_taken, 1)
                hid.split_high(act, 0, 0, 0)

                def copy(i, n, half):
                    act.wait_ge(scored, i * 2 + (half + 2))
                    act.wait_ge(read, i + 1)
                    S.activation(s_in[0:n, half * HJ:(half + 1) * HJ], s_ps[0:n], ACT.Copy).then_inc(copied, 1)

                def exp(i, n):
                    act.wait_ge(exp_in, i + 2)
                    S.activation(slot[0:n, 2], slot[0:n, 2], ACT.Exp).then_inc(gate_ready, 1)

                def take(i, n):
                    act.wait_ge(turned, i + 2)
                    S.activation(slots[:, :, bass.ds(i * P, n)], t_ps[:, :, 0:n], ACT.Copy).then_inc(slots_taken, 1)

                def body(i, n):
                    for j, (m, s_, turn) in enumerate(chunks(i)):
                        if not (is_(i, LAST) and j == E_LAST - 1):
                            hid.split_high(act, m + 1, 1 - s_, turn + s_)
                        if j < 2:
                            copy(i, n, j)
                        if j == 1 and not is_(i, 0):
                            exp(i - 1, P)
                        hid.finish(act, m, s_, turn)
                        if j == 3 and not is_(i, 0):
                            take(i - 1, P)
                tiles(act, body)
                exp(LAST, T - LAST * P)
                take(LAST, T - LAST * P)

            @block.vector
            def _(dve):
                link = Chain(dve, chain)
                V = nc.vector

                def top16(n, values, rest, out, out_at, count):
                    carry(dve, carried)
                    for j in range(count):
                        ins = V.max(out=out[0:n, j, 0:8], in_=values[0:n, j])
                    link(ins)
                    carry(dve, carried)
                    for j in range(count):
                        V.max_index(out=out_at[0:n, j, 0:8], in_max=out[0:n, j, 0:8], in_values=values[0:n, j])
                        ins = V.match_replace(out=rest[0:n, j], in_to_replace=out[0:n, j, 0:8],
                                              in_values=values[0:n, j], imm_value=-3e38)
                    link(ins)
                    carry(dve, carried)
                    for j in range(count):
                        ins = V.max(out=out[0:n, j, 8:16], in_=rest[0:n, j])
                    link(ins)
                    carry(dve, carried)
                    for j in range(count):
                        ins = V.max_index(out=out_at[0:n, j, 8:16], in_max=out[0:n, j, 8:16], in_values=rest[0:n, j])
                    link(ins)

                def normalise(i, n):
                    dve.wait_ge(gate_ready, i + 2)
                    link(V.tensor_reduce(total[0:n, 0], slot[0:n, 2], AX_X, ALU.add))
                    link(V.reciprocal(total[0:n, 1], total[0:n, 0]))
                    V.tensor_tensor(slot[0:n, 2], slot[0:n, 2], total[0:n, 1].unsqueeze(2).to_broadcast([n, NH, TOPK]),
                                    ALU.mult).then_inc(slots_ready, 1)

                def body(i, n):
                    dve.wait_ge(copied, i * 2 + 3)
                    top16(n, s_in, s2, best, best_at, NJ)
                    dve.sem_inc(read, 1)
                    if not is_(i, 0):
                        normalise(i - 1, P)
                    link(V.tensor_copy(best_key[0:n], best_at[0:n]))
                    b4 = best[0:n].rearrange("p (h q) k -> p h q k", q=2)
                    k4 = best_key[0:n].rearrange("p (h q) k -> p h q k", q=2)
                    wide = [n, NH, TOPK, TOPK]
                    for a0, a1, nb, at in ((0, AFIRST, TOPK, 0), (AFIRST, TOPK, AFIRST, EARLY)):
                        part = [n, NH, a1 - a0, nb]
                        ins = V.tensor_tensor(
                            cand[0:n, :, at:at + (a1 - a0) * nb].rearrange("p h (a b) -> p h a b", b=nb),
                            b4[:, :, 0, a0:a1].unsqueeze(3).to_broadcast(part),
                            b4[:, :, 1, 0:nb].unsqueeze(2).to_broadcast(part), ALU.add)
                    link(ins)
                    top16(n, cand, cand2, top, top_at, NH)
                    if not is_(i, 0):
                        dve.wait_ge(turned, i + 1)
                    V.tensor_scalar(half_at[0:n, 0], top_at[0:n], 4, None, ALU.logical_shift_right)
                    V.tensor_scalar(half_at[0:n, 1], top_at[0:n], 15, None, ALU.bitwise_and)
                    V.tensor_scalar(half_at[0:n, 2], top_at[0:n], 2, None, ALU.logical_shift_right)
                    link(V.tensor_scalar(half_at[0:n, 3], top_at[0:n], 3, None, ALU.bitwise_and))
                    link(V.tensor_copy(half_pos[0:n], half_at[0:n]))
                    hp = half_pos[0:n]
                    V.tensor_scalar(late[0:n], hp[:, 0], float(AFIRST), None, ALU.is_ge)
                    link(V.tensor_tensor(hp[:, 2:4], hp[:, 2:4], hp[:, 0:2], ALU.subtract))
                    V.scalar_tensor_tensor(hp[:, 2], hp[:, 2], float(AFIRST - EARLY // 4), late[0:n], ALU.add, ALU.mult)
                    link(V.tensor_tensor(hp[:, 3], hp[:, 3], late[0:n], ALU.mult))
                    link(V.tensor_tensor(hp[:, 0:2], hp[:, 0:2], hp[:, 2:4], ALU.add))
                    link(V.tensor_tensor(slot[0:n, 2], top[0:n], top[0:n, :, 0:1].to_broadcast([n, NH, TOPK]), ALU.subtract))
                    dve.sem_inc(exp_in, 1)
                    iota = col(consts, "iota16")[0:n].unsqueeze(1).unsqueeze(1).to_broadcast(wide)
                    for q in range(2):
                        ins = V.tensor_tensor(shape(pick[q])[0:n], half_pos[0:n, q].unsqueeze(3).to_broadcast(wide), iota,
                                              ALU.is_equal)
                    link(ins)
                    for q in range(2):
                        ins = V.tensor_tensor(shape(pick[q])[0:n], shape(pick[q])[0:n],
                                              k4[:, :, q].unsqueeze(2).to_broadcast(wide), ALU.mult)
                    link(ins)
                    for q in range(2):
                        ins = V.tensor_reduce(slot[0:n, q], shape(pick[q])[0:n], AX_X, ALU.add)
                    link(ins)

                body(0, P)
                per = link.n + 2
                with dve.Fori(1, LAST) as i:
                    link.enter(i - 1, per)
                    body(i, P)
                    link.leave(LAST - 1)
                body(LAST, T - LAST * P)
                normalise(LAST, T - LAST * P)


TB = 24
NTB = T // TB


def peer_gates(nc, io, sb, pb, sm, consts, hh, hl, slots, **_):
    GR = 4
    NG = TB // GR
    FIRST = FIRST_GATES
    assert NKEY - FIRST == 2 * NTB
    with ExitStack() as ph:
        hid = Product(nc, io["u"], io["hidden_saved"], ACT.Gelu, sb, pb, sm, ph, hh, hl, FIRST, "g")
        second = sb(ph, "second", [P, 2, GR, NKEY], BF16)
        first = sb(ph, "first", [P, 2, GR, 3, NKEY], BF16)
        iota = sb(ph, "iota_bf16", [P, NKEY], BF16)
        part_bf16 = sb(ph, "part_bf16", [P, T], BF16)
        part = sb(ph, "gate_parts", [P, 3, T])
        gates = sb(ph, "gates", [P, 2, NKEY, TB])
        ps = [pb(ph, f"gates_ps{s}", [P, GR, NKEY]) for s in range(2)]
        first_ready, second_ready, summed, taken, stored0, stored1, block_done, chain = sm(
            ph, "first_ready", "second_ready", "gates_summed", "gates_taken", "gates_stored0", "gates_stored1",
            "gates_done", "parts_chain")
        stored = (stored0, stored1)

        def blocks(eng, body):
            with eng.Fori(0, NTB // 2) as i:
                for half in range(2):
                    body(i * 2 + half, half, i * 2 + half, False)
            body(NTB - 1, 0, NTB - 1, True)

        with nc.Block() as block:
            @block.vector
            def _(dve):
                V = nc.vector
                link = Chain(dve, chain)
                link(V.tensor_copy(iota[:], col(consts, "iota")))
                rest = slots[:, 2]
                for q in range(2):
                    link(V.tensor_copy(part_bf16[:], rest))
                    link(V.tensor_copy(part[:, q], part_bf16[:]))
                    link(V.tensor_tensor(part[:, 2], rest, part[:, q], ALU.subtract))
                    rest = part[:, 2]

                def body(b, half, turn, last):
                    for g in range(NG):
                        dve.wait_ge(summed, b * NG + g + 2)
                        for t in range(GR):
                            at = bass.ds(b * TB + (g * GR + t), 1)
                            for q in range(3):
                                ins = V.tensor_scalar(first[:, g % 2, t, q], iota[:], slots[:, 0, at], part[:, q, at],
                                                      ALU.is_equal, ALU.mult)
                        ins.then_inc(first_ready, 1)
                        V.tensor_tensor(second[:, g % 2], iota[:].unsqueeze(1).to_broadcast([P, GR, NKEY]),
                                        slots[:, 1, bass.ds(b * TB + g * GR, GR)].unsqueeze(2).to_broadcast([P, GR, NKEY]),
                                        ALU.is_equal).then_inc(second_ready, 1)
                blocks(dve, body)

            @block.gpsimd
            def _(pool):
                pool.sem_inc(hid.split, 2)

                def body(b, half, turn, last):
                    for e in range(2):
                        hid.split_low(pool, b * 2 + e, e)
                blocks(pool, body)

            @block.tensor
            def _(pe):
                pe.sem_inc(summed, 2)
                pe.sem_inc(hid.summed, 2)

                def body(b, half, turn, last):
                    for g in range(NG):
                        hid.multiply(pe, b * 2 + g // NT, g // NT, g % NT)
                        pe.wait_ge(first_ready, b * NG + g + 2)
                        pe.wait_ge(second_ready, b * NG + g + 2)
                        pe.wait_ge(taken, b * NG + g + 2)
                        for t in range(GR):
                            for q in range(3):
                                mm = nc.tensor.matmul(ps[g % 2][:, t], second[:, g % 2, t], first[:, g % 2, t, q],
                                                      start=q == 0, stop=q == 2)
                        mm.then_inc(summed, 1)
                blocks(pe, body)

            @block.scalar
            def _(act):
                act.sem_inc(taken, 2)
                act.sem_inc(hid.ready, 2)
                hid.split_high(act, 0, 0, 0)

                def body(b, half, turn, last):
                    act.wait_ge(stored[half], (turn - half) * 8 + 17)
                    for g in range(NG):
                        e = g // NT
                        if g % NT == 0 and not (last and e == 1):
                            hid.split_high(act, b * 2 + (e + 1), (e + 1) % 2, b + (e + 1) // 2)
                        if g % NT == NT - 1:
                            hid.finish(act, b * 2 + e, e, b)
                        act.wait_ge(summed, b * NG + g + 4)
                        nc.scalar.activation(gates[:, half, :, g * GR:(g + 1) * GR],
                                             ps[g % 2][:].rearrange("p t k -> p k t"), ACT.Copy).then_inc(taken, 1)
                    act.wait_ge(taken, b * NG + (NG + 3))
                    act.sem_inc(block_done, 1)
                blocks(act, body)

            @block.sync
            def _(sp):
                for s in (*stored, *hid.stored):
                    sp.sem_inc(s, 16)
                for e in range(2):
                    hid.load(sp, e, e)

                def body(b, half, turn, last):
                    for e in range(2):
                        if not last:
                            hid.load(sp, b * 2 + (e + 2), e)
                        hid.store(sp, b * 2 + e, e)
                    sp.wait_ge(block_done, b + 2)
                    out = io["gates"][:, bass.ds(b, 1)].rearrange("p o k t -> p (o k t)")
                    sp.dma_start(out, gates[:, half].rearrange("p k t -> p (k t)")).then_inc(stored[half], 16)
                blocks(sp, body)
                sp.wait_ge(stored0, (NTB // 2 + 1) * 16 + 17)
                sp.wait_ge(stored1, (NTB // 2) * 16 + 17)
                for q in range(2):
                    sp.wait_ge(hid.stored[q], (NKEY - FIRST) // 2 * 16 + 17)


def peer_experts(nc, io, sb, pb, sm, acc, **_):
    GR, NGRP, NG_LOAD = 2, 4, 4
    TURNS = NKEY // (GR * NGRP)
    CH = GR * NGRP
    NO = KD * NT
    NBANK = 8
    with ExitStack() as ph:
        v_raw = sb(ph, "v_raw", [P, 2, D])
        vh = sb(ph, "v_high", [P, 2, GR, D], F32R)
        vl = sb(ph, "v_low", [P, 2, GR, D], F32R)
        hid = sb(ph, "hidden_back", [P, 2, T])
        g = sb(ph, "g", [P, 2, NTB, NG_LOAD, TB])
        prod = sb(ph, "weighted_hidden", [P, 2, T])
        wh = sb(ph, "w_high", [P, 2, GR, T], F32R)
        wl = sb(ph, "w_low", [P, 2, GR, T], F32R)
        out_ps = [pb(ph, f"out_ps{s}", [P, 512]) for s in range(NBANK)]
        (v0, v1, h0, h1, g0, g1, v_high, v_split, g_free, weighted, w_high, w_split, summed, added, cleared) = sm(
            ph, "v0_loaded", "v1_loaded", "h0_loaded", "h1_loaded", "g0_loaded", "g1_loaded", "v_high_ready", "v_split",
            "g_free", "weighted", "w_high_ready", "w_split", "experts_summed", "experts_added", "acc_cleared")
        v_loaded, h_loaded, g_loaded = (v0, v1), (h0, h1), (g0, g1)

        with nc.Block() as block:
            @block.sync
            def _(sp):
                with sp.Fori(0, TURNS) as i:
                    for c in range(CH):
                        if c % NG_LOAD == 0:
                            half = c // NG_LOAD
                            sp.wait_ge(g_free, i * 2 + (half + 2))
                            sp.dma_start(g[:, half], io["gates"][:, :, bass.ds(i * CH + c, NG_LOAD), :])\
                                .then_inc(g_loaded[half], 16)
                        sp.wait_ge(w_split, i * CH + (c + 2))
                        sp.dma_start(hid[:, c % 2], io["hidden_saved"][bass.ds(i * CH + c, 1)].rearrange("o p n -> p (o n)"))\
                            .then_inc(h_loaded[c % 2], 16)
                        sp.wait_ge(v_split, i * CH + (c + 2))
                        sp.dma_start(v_raw[:, c % 2], io["v"][bass.ds(i * CH + c, 1)].rearrange("o p n -> p (o n)"))\
                            .then_inc(v_loaded[c % 2], 16)

            @block.gpsimd
            def _(pool):
                pool.sem_inc(v_split, 2)
                with pool.Fori(0, TURNS) as i:
                    for c in range(CH):
                        pool.wait_ge(v_high, i * CH + (c + 2))
                        half, j = c // GR % 2, c % GR
                        nc.gpsimd.tensor_tensor(vl[:, half, j], v_raw[:, c % 2], vh[:, half, j].bitcast(F32), ALU.subtract)\
                            .then_inc(v_split, 1)

            @block.scalar
            def _(act):
                with act.Fori(0, TURNS) as i:
                    for c in range(CH):
                        half, j = c // GR % 2, c % GR
                        if j == 0:
                            act.wait_ge(summed, i * (NGRP * NO) + ((c // GR + 1) * NO + 1))
                        act.wait_ge(v_loaded[c % 2], i * (CH * 8) + (c // 2 * 16 + 17))
                        nc.scalar.activation(vh[:, half, j], v_raw[:, c % 2], ACT.Copy).then_inc(v_high, 1)
                        act.wait_ge(weighted, i * CH + (c + 2))
                        nc.scalar.activation(wh[:, half, j], prod[:, c % 2], ACT.Copy).then_inc(w_high, 1)

            @block.tensor
            def _(pe):
                with pe.Fori(0, TURNS) as i:
                    for grp in range(NGRP):
                        half = grp % 2
                        pe.wait_ge(v_split, i * CH + (grp * GR + GR + 3))
                        pe.wait_ge(w_split, i * CH + (grp * GR + GR + 3))
                        for m in range(KD):
                            for t in range(NT):
                                o = m * NT + t
                                pe.wait_ge(added, i * (NGRP * NO) + (grp * NO + o + 2))
                                for j in range(GR):
                                    tok = slice(t * TN, (t + 1) * TN)
                                    feat = slice(m * P, (m + 1) * P)
                                    for q, (v, w) in enumerate(((vh, wh), (vh, wl), (vl, wh))):
                                        mm = nc.tensor.matmul(out_ps[o % NBANK][:, 0:TN], v[:, half, j, feat],
                                                              w[:, half, j, tok], start=j == 0 and q == 0,
                                                              stop=j == GR - 1 and q == 2)
                                mm.then_inc(summed, 1)

            @block.vector
            def _(dve):
                V = nc.vector
                dve.sem_inc(added, NBANK)
                dve.sem_inc(g_free, 2)
                dve.sem_inc(w_split, 2)
                dve.sem_inc(summed, 2 * NO)
                V.memset(acc[:], 0.0).then_inc(cleared, 1)
                dve.wait_ge(cleared, 2)

                def weigh(i, c):
                    dve.wait_ge(h_loaded[c % 2], i * (CH * 8) + (c // 2 * 16 + 17))
                    if c % NG_LOAD == 0:
                        dve.wait_ge(g_loaded[c // NG_LOAD], i * 16 + 17)
                    V.tensor_tensor(prod[:, c % 2].rearrange("p (b t) -> p b t", t=TB),
                                    hid[:, c % 2].rearrange("p (b t) -> p b t", t=TB),
                                    g[:, c // NG_LOAD, :, c % NG_LOAD], ALU.mult).then_inc(weighted, 1)

                def split(i, c):
                    dve.wait_ge(w_high, i * CH + (c + 2))
                    V.tensor_tensor(wl[:, c // GR % 2, c % GR], prod[:, c % 2], wh[:, c // GR % 2, c % GR].bitcast(F32),
                                    ALU.subtract).then_inc(w_split, 1)
                    if c % NG_LOAD == NG_LOAD - 1:
                        dve.sem_inc(g_free, 1)

                def add(i, grp, o):
                    dve.wait_ge(summed, i * (NGRP * NO) + (grp * NO + o + 2 + 2 * NO))
                    a = acc[:, o // NT, o % NT * TN:(o % NT + 1) * TN]
                    V.tensor_tensor(a, a, out_ps[o % NBANK][:, 0:TN], ALU.add).then_inc(added, 1)

                def turn(i, last):
                    for grp in range(NGRP):
                        for o in range(NO):
                            if o == 0:
                                dve.wait_ge(added, i * (NGRP * NO) + (grp * NO + 1 + NBANK))
                            add(i, grp, o)
                            nxt = (grp + 1) * GR
                            if not (last and grp == NGRP - 1):
                                at = {3: (weigh, 0), 7: (split, 0), 11: (weigh, 1), 15: (split, 1)}.get(o)
                                if at:
                                    c = nxt + at[1]
                                    at[0](i + c // CH, c % CH)

                for c in range(GR):
                    weigh(0, c)
                    split(0, c)
                with dve.Fori(0, TURNS - 1) as i:
                    turn(i, False)
                turn(TURNS - 1, True)


def peer_output(nc, sm, mod, x, acc, **_):
    with ExitStack() as ph:
        weighed, samples_weighed, added = sm(ph, "acc_weighed", "acc_samples_weighed", "acc_added")
        with nc.Block() as block:
            @block.scalar
            def _(act):
                for k in range(KD):
                    nc.scalar.activation(acc[:, k, 0:TP], acc[:, k, 0:TP], ACT.Identity, scale=mod[:, GT_F + k, 0:1])\
                        .then_inc(weighed, 1)

            @block.vector
            def _(dve):
                V = nc.vector
                V.tensor_tensor(acc[:, :, TP:T], acc[:, :, TP:T], mod[:, GT_F:GT_F + KD, 1:], ALU.mult)\
                    .then_inc(samples_weighed, 1)
                dve.wait_ge(samples_weighed, 2)
                for k in range(KD):
                    dve.wait_ge(weighed, k + 2)
                    V.scalar_tensor_tensor(x[:, k], x[:, k], ALPHA, acc[:, k], ALU.mult, ALU.add).then_inc(added, 1)


def _consts():
    import numpy as np
    t = np.zeros((P, NCONST), np.float32)

    def put(name, a):
        at, n = CONST[name]
        t[:, at:at + n] = a
    i64 = np.eye(HD)
    blocks = np.kron(np.eye(2), np.ones((HD, HD)))
    put("ident", np.eye(P))
    put("ident64", np.tile(i64, (2, 1)))
    put("headsum", blocks)
    put("mean", np.full((P, P), 1.0 / D))
    put("headmean", blocks / HD)
    r, c = np.arange(C)[:, None], np.arange(C)[None, :]
    put("upper", np.tile(c > r, (2, 1)))
    put("upper_incl", np.tile(c >= r, (2, 1)))
    put("first_u", np.tile((c == r + 1) & (r % 2 == 0), (2, 1)))
    put("first_l", np.tile((r == c + 1) & (c % 2 == 0), (2, 1)))
    for s in LEVELS:
        put(f"level{s}", np.tile((r // (2 * s) == c // (2 * s)) & (r % (2 * s) < s) & (c % (2 * s) >= s), (2, 1)))
    put("iota", np.tile(np.arange(P), (P, 1)))
    put("iota16", np.tile(np.arange(16), (P, 1)))
    put("ones", 1.0)
    put("ln_eps", LN_EPS)
    put("gn_eps", GN_EPS)
    return t


def _host_inputs(v):
    import numpy as np
    v = {k: np.asarray(a) for k, a in v.items()}

    def fm(a):
        return np.ascontiguousarray(a.T.reshape(-1, P, a.shape[0]).transpose(1, 0, 2))

    def colblocks(a, width=P):
        k, n = a.shape
        return np.ascontiguousarray(a.reshape(k // P, P, n // width, width).transpose(2, 1, 0, 3))

    def percol(a):
        return a.reshape(-1, P).T
    out = {}
    out["consts"] = _consts()
    out["x"] = fm(np.concatenate([v["x_prompt"][0], v["x_sample"][:, 0]]))
    out["c"] = fm(np.concatenate([v["c_prompt"], v["c_sample"]]))
    out["w_ada"] = colblocks(v["w_ada"][0], 512)
    vecs = np.zeros((P, NVEC), np.float32)
    for name, src in (("ln_in_g", "ln_in_g"), ("ln_in_b", "ln_in_b"), ("ln_1_g", "ln1_g"), ("ln_1_b", "ln1_b"),
                      ("ln_2_g", "ln2_g"), ("ln_2_b", "ln2_b"), ("b_ada", "b_ada"), ("mu", "mu_shift"),
                      ("w0", "rwkv_w0"), ("a0", "rwkv_a0"), ("k_k", "rwkv_k_k"), ("k_a", "rwkv_k_a"),
                      ("r_k", "rwkv_r_k"), ("gn_g", "rwkv_gn_g"), ("gn_b", "rwkv_gn_b")):
        at, n = VEC[name]
        vecs[:, at:at + n] = percol(v[src].reshape(-1))
    out["vecs"] = vecs
    blocks = colblocks(v["w_in"][0])
    order = [12, 13] + [b for p in range(NP) for b in (p, 4 + p, 8 + p)]
    out["w_in"] = np.ascontiguousarray(blocks[order])
    out["w_lora"] = np.ascontiguousarray(np.concatenate([v["rwkv_w2"][0], v["rwkv_a2"][0]]).reshape(P, NP, P).transpose(1, 0, 2))
    out["shift_before"] = fm(v["state_shift"][0])
    reset = np.ones((P, T), np.float32)
    reset[:, 0:TP:C] = 0.0
    reset[:, TP:] = 0.0
    out["reset"] = reset
    w = v["w_in"][0]
    q_at, k_at, v_at, ga_at, gb_at = 1792, 2304, 2432, 2560, 3584
    heads = [q_at + 64 * hd for c in range(NP) for hd in (c, 4 + c)]
    cols = np.concatenate([np.arange(a, a + 64) for a in heads] + [np.arange(k_at, v_at + 128)])
    gates = np.stack([colblocks(w[:, ga_at:gb_at]), colblocks(w[:, gb_at:])], 1).reshape(2 * KD, P, KD, P)
    out["w_side"] = np.ascontiguousarray(np.concatenate([colblocks(w[:, cols]), gates]))
    out["state_wkv"] = np.ascontiguousarray(
        v["state_wkv"][0].reshape(NS, NP, 2, HD, HD).transpose(2, 4, 1, 0, 3).reshape(P, NP, NS, HD))
    out["g2"] = np.ascontiguousarray(v["rwkv_g2"][0].reshape(P, NP, P))
    pa, pb_ = (colblocks(a) for a in (v["w_pa"][0], v["w_pb"][0].reshape(2, NP, HD, D).transpose(1, 0, 2, 3).reshape(-1, D)))
    out["w_merge"] = np.ascontiguousarray(np.concatenate([pa, pb_], axis=2))
    out["w_o"] = colblocks(v["w_o"][0])
    out["peer_wq"] = colblocks(v["peer_wq"][0])
    out["keys"] = np.ascontiguousarray(v["peer_sub_keys"][0].transpose(2, 0, 1))
    out["u"] = np.ascontiguousarray(v["peer_u"][0].reshape(NKEY, NKEY, KD, P).transpose(0, 3, 2, 1))
    out["v"] = v["peer_v"][0].reshape(NKEY, NKEY, D)
    slopes = 2.0 ** -np.arange(1.0, 9.0)
    rel = WIN + np.arange(WIN)[:, None] - np.arange(2 * WIN)[None, :]
    b = -slopes[None, :, None] * rel[:, None, :]
    b = np.where(((rel >= 0) & (rel <= WIN))[:, None, :], b, NEG)
    first = np.where(np.arange(2 * WIN) < WIN, NEG, b)
    out["att_bias"] = np.stack([first, b], 1).reshape(P, 2, -1).astype(np.float32)
    out["sinks"] = np.ascontiguousarray(np.broadcast_to(v["attn_sinks"][0], (P, NH)))
    out["k_cache"] = np.ascontiguousarray(v["cache_k_win"][0].reshape(NS, WIN, P).transpose(2, 0, 1))
    out["v_cache"] = np.ascontiguousarray(v["cache_v_win"][0].reshape(NS, WIN, P).transpose(1, 0, 2))
    sb_ = np.zeros((64, WIN + 2), np.float32)
    sb_[:, 0:WIN + 1] = np.tile(-slopes[:, None] * (WIN - np.arange(WIN + 1)), (NS, 1))
    sb_[:, WIN + 1] = np.tile(v["attn_sinks"][0], NS)
    out["sample_bias"] = sb_
    return out


_OUTS = {"shift_out": (P, 14, 1 + NS), "wkv_prompt_out": (P, NP, HD),
         "wkv_sample_out": (P, NP, NS, HD), "k_win_prompt_out": (P, WIN), "v_win_prompt_out": (P, WIN),
         "y_out": (P, KD, T), "k_win_sample_out": (P, NS, WIN), "v_win_sample_out": (WIN, NS, P)}


def kernel(**inputs):
    import numpy as np
    import concourse.bacc as bacc
    from concourse.bass_utils import run_bass_kernel_spmd

    nc = bacc.Bacc("TRN2", target_bir_lowering=False, num_devices=1)
    arrays = _host_inputs(inputs)
    io = {n: nc.dram_tensor("in_" + n, a.shape, mybir.dt.from_np(a.dtype), kind="ExternalInput").ap()
          for n, a in arrays.items()}
    io["x_saved"] = nc.dram_tensor("x_saved", [P, KD, T], F32, kind="Internal").ap()
    io["side_saved"] = nc.dram_tensor("side_saved", [P, SIDE, T], F32, kind="Internal").ap()
    io["gates"] = nc.dram_tensor("gates_saved", [P, NTB, NKEY, TB], F32, kind="Internal").ap()
    io["query_saved"] = nc.dram_tensor("query_saved", [2 * NH, P, T], F32, kind="Internal").ap()
    io["hidden_saved"] = nc.dram_tensor("hidden_saved", [NKEY, P, T], F32, kind="Internal").ap()
    for n, shape in _OUTS.items():
        io[n] = nc.dram_tensor("out_" + n, shape, F32, kind="ExternalOutput").ap()
    kernel_program(nc, io)
    r = run_bass_kernel_spmd(nc, [{"in_" + n: a for n, a in arrays.items()}], core_ids=[0]).results[0]

    def rows(a):
        return a.transpose(2, 1, 0).reshape(a.shape[2], -1)

    out = {n: np.asarray(r["out_" + n]) for n in _OUTS}
    y = rows(out["y_out"])
    shift = rows(out["shift_out"])
    wkv_p = out["wkv_prompt_out"].reshape(2, HD, NP, HD).transpose(2, 0, 3, 1).reshape(1, 1, 8, HD, HD)
    wkv_s = out["wkv_sample_out"].reshape(2, HD, NP, NS, HD).transpose(3, 2, 0, 4, 1).reshape(1, NS, 8, HD, HD)
    k_p, v_p = (out[f"{n}_win_prompt_out"].T.reshape(1, 1, WIN, 2, HD) for n in "kv")
    k_s = out["k_win_sample_out"].transpose(1, 2, 0).reshape(1, NS, WIN, 2, HD)
    v_s = out["v_win_sample_out"].transpose(1, 0, 2).reshape(1, NS, WIN, 2, HD)
    return (y[:TP][None], y[TP:][:, None], wkv_p, wkv_s, shift[0][None, None], shift[1:][None], k_p, k_s, v_p, v_s)
```
